# Optimizing a Trainium2 kernel written in Bass

```python
import math, functools
import jax, jax.numpy as jnp
from jax import lax
import numpy as np

D_MODEL = 1024
BATCH = 1
SEQ = 512
DEPTH = 1
DEC_BATCH = 8
DEC_SEQ = 8
PAST_LEN = 4096
PAGE_SIZE = 128

ATT_HEADS = 4
ATT_HEAD_DIM = 64
ATT_V_DIM = 2 * ATT_HEAD_DIM
ATT_WIDTH = ATT_HEADS * ATT_V_DIM
SSD_HEADS = 8
SSD_HEAD_DIM = 64
SSD_WIDTH = SSD_HEADS * SSD_HEAD_DIM
SSD_GROUPS = 2
D_STATE = 128
CONV_W = 4
CONV_DIM = SSD_WIDTH + 2 * SSD_GROUPS * D_STATE
SSD_CHUNK = 128
MIX_WIDTH = ATT_WIDTH + SSD_WIDTH
IN_WIDTH = 3 * ATT_WIDTH + SSD_WIDTH + CONV_DIM + SSD_HEADS
SPLITS = [ATT_WIDTH, 2 * ATT_WIDTH, 3 * ATT_WIDTH, 3 * ATT_WIDTH + SSD_WIDTH,
          3 * ATT_WIDTH + SSD_WIDTH + CONV_DIM]
D_FF = 4 * D_MODEL
N_BUCKETS = 32
MAX_DISTANCE = 128
MAX_EXACT = N_BUCKETS // 2
Q_BLOCK = 128
EPS = 1e-6

kernel_name = "hymba_diffattn_ssd_decoder_step"

F32 = jnp.float32

def _rmsnorm(x, g):
    xf = x.astype(F32)
    y = xf * lax.rsqrt(jnp.mean(xf * xf, axis=-1, keepdims=True) + EPS)
    return (y * g.astype(F32)).astype(x.dtype)

def _rel_bucket(dist):
    n = jnp.maximum(dist, 0)
    nf = jnp.maximum(n, 1).astype(F32)
    large = MAX_EXACT + (jnp.log(nf / MAX_EXACT) / math.log(MAX_DISTANCE / MAX_EXACT)
                         * (N_BUCKETS - MAX_EXACT)).astype(jnp.int32)
    large = jnp.minimum(large, N_BUCKETS - 1)
    return jnp.where(n < MAX_EXACT, n, large)

def _rel_bias(rel_table, q_pos, k_pos):
    b = rel_table[_rel_bucket(q_pos[:, None] - k_pos[None, :])]
    return jnp.transpose(b, (2, 0, 1)).astype(F32)

def _modulation(c, w, b):
    m = (jax.nn.silu(c) @ w + b)[:, None, :]
    return jnp.split(m, 6, axis=-1)

def _diff_lambda(lq1, lk1, lq2, lk2, lam_init):
    e1 = jnp.exp(jnp.sum(lq1.astype(F32) * lk1.astype(F32)))
    e2 = jnp.exp(jnp.sum(lq2.astype(F32) * lk2.astype(F32)))
    return e1 - e2 + lam_init

def _diff_combine(o, lam, subln_g, lam_init):
    d = o[..., 0, :] - lam * o[..., 1, :]
    d = d * lax.rsqrt(jnp.mean(d * d, axis=-1, keepdims=True) + EPS) * subln_g.astype(F32)
    d = d * (1.0 - lam_init)
    return d.reshape(o.shape[0], o.shape[1], ATT_WIDTH)

def _diff_attn_prompt(q, k, v, rel_table):
    B, S = q.shape[:2]
    nb = S // Q_BLOCK
    scale = ATT_HEAD_DIM ** -0.5
    k_pos = jnp.arange(S)
    qb = jnp.moveaxis(q.reshape(B, nb, Q_BLOCK, ATT_HEADS, 2, ATT_HEAD_DIM), 1, 0)

    def one_block(args):
        q_blk, start = args
        q_pos = start + jnp.arange(Q_BLOCK)
        s = jnp.einsum('bqhjd,bkhjd->bhjqk', q_blk, k).astype(F32) * scale
        s = s + _rel_bias(rel_table, q_pos, k_pos)[:, None]
        s = jnp.where(k_pos[None, :] <= q_pos[:, None], s, -jnp.inf)
        p = jax.nn.softmax(s, axis=-1)
        return jnp.einsum('bhjqk,bkhe->bqhje', p.astype(v.dtype), v).astype(F32)

    o = lax.map(one_block, (qb, jnp.arange(nb) * Q_BLOCK))
    return jnp.moveaxis(o, 0, 1).reshape(B, S, ATT_HEADS, 2, ATT_V_DIM)

def _online_step(carry, s, v):
    m, l, acc = carry
    m_new = jnp.maximum(m, jnp.max(s, axis=-1))
    alpha = jnp.exp(m - m_new)
    p = jnp.exp(s - m_new[..., None])
    l = l * alpha + jnp.sum(p, axis=-1)
    acc = acc * alpha[..., None] + jnp.einsum('bhjqk,bkhe->bhjqe', p, v.astype(F32))
    return (m_new, l, acc)

def _diff_attn_sample(q, k_new, v_new, cache_k, cache_v, layer, page_table, rel_table):
    Bd, T = q.shape[:2]
    n_pages = page_table.shape[1]
    past = n_pages * PAGE_SIZE
    q_pos = past + jnp.arange(T)
    scale = ATT_HEAD_DIM ** -0.5
    qf = q.astype(F32)
    init = (jnp.full((Bd, ATT_HEADS, 2, T), -jnp.inf, F32),
            jnp.zeros((Bd, ATT_HEADS, 2, T), F32),
            jnp.zeros((Bd, ATT_HEADS, 2, T, ATT_V_DIM), F32))

    def page_step(carry, xs):
        phys, p_idx = xs
        kp = cache_k[layer, phys]
        vp = cache_v[layer, phys]
        k_pos = p_idx * PAGE_SIZE + jnp.arange(PAGE_SIZE)
        s = jnp.einsum('bqhjd,bkhjd->bhjqk', qf, kp.astype(F32)) * scale
        s = s + _rel_bias(rel_table, q_pos, k_pos)[:, None]
        return _online_step(carry, s, vp), None

    carry, _ = lax.scan(page_step, init, (page_table.T, jnp.arange(n_pages)))
    s = jnp.einsum('bqhjd,bkhjd->bhjqk', qf, k_new.astype(F32)) * scale
    s = s + _rel_bias(rel_table, q_pos, q_pos)[:, None]
    s = jnp.where(q_pos[None, :] <= q_pos[:, None], s, -jnp.inf)
    m, l, acc = _online_step(carry, s, v_new)
    o = acc / l[..., None]
    return jnp.transpose(o, (0, 3, 1, 2, 4))

def _causal_conv(xbc, prefix, w, b):
    T = xbc.shape[1]
    xp = jnp.concatenate([prefix.astype(xbc.dtype), xbc], axis=1)
    y = b
    for i in range(CONV_W):
        y = y + xp[:, i:i + T] * w[i]
    return jax.nn.silu(y), xp[:, xp.shape[1] - (CONV_W - 1):]

def _segsum(a):
    T = a.shape[-1]
    xx = jnp.broadcast_to(a[..., None], a.shape + (T,))
    xx = jnp.where(jnp.tril(jnp.ones((T, T), bool), -1), xx, 0.0)
    ss = jnp.cumsum(xx, axis=-2)
    return jnp.where(jnp.tril(jnp.ones((T, T), bool)), ss, -jnp.inf)

def _ssd_scan(xdt, dA, Bm, Cm, h0, chunk):
    b, L = xdt.shape[:2]
    c = L // chunk
    X = xdt.reshape(b, c, chunk, SSD_HEADS, SSD_HEAD_DIM)
    Bc = Bm.reshape(b, c, chunk, SSD_HEADS, D_STATE)
    Cc = Cm.reshape(b, c, chunk, SSD_HEADS, D_STATE)
    A = jnp.transpose(dA.reshape(b, c, chunk, SSD_HEADS), (0, 3, 1, 2))
    A_cs = jnp.cumsum(A, axis=-1)
    Lmat = jnp.exp(_segsum(A))
    scores = jnp.einsum('bclhn,bcshn->bhcls', Cc, Bc) * Lmat
    y_diag = jnp.einsum('bhcls,bcshp->bclhp', scores, X)
    decay_states = jnp.exp(A_cs[..., -1:] - A_cs)
    states = jnp.einsum('bclhn,bhcl,bclhp->bchpn', Bc, decay_states, X)
    states = jnp.concatenate([h0[:, None], states], axis=1)
    decay_chunk = jnp.exp(_segsum(jnp.pad(A_cs[..., -1], ((0, 0), (0, 0), (1, 0)))))
    new_states = jnp.einsum('bhzc,bchpn->bzhpn', decay_chunk, states)
    states, final = new_states[:, :-1], new_states[:, -1]
    y_off = jnp.einsum('bclhn,bchpn,bhcl->bclhp', Cc, states, jnp.exp(A_cs))
    return (y_diag + y_off).reshape(b, L, SSD_HEADS, SSD_HEAD_DIM), final

def _ssd_branch(xbc_act, z, dt_raw, h0, dt_bias, a_log, d_skip, norm_g, chunk):
    b, T = xbc_act.shape[:2]
    xs, Bm, Cm = jnp.split(xbc_act, [SSD_WIDTH, SSD_WIDTH + SSD_GROUPS * D_STATE], axis=-1)
    xs = xs.reshape(b, T, SSD_HEADS, SSD_HEAD_DIM).astype(F32)
    rep = SSD_HEADS // SSD_GROUPS
    Bm = jnp.repeat(Bm.reshape(b, T, SSD_GROUPS, D_STATE).astype(F32), rep, axis=2)
    Cm = jnp.repeat(Cm.reshape(b, T, SSD_GROUPS, D_STATE).astype(F32), rep, axis=2)
    dt = jax.nn.softplus(dt_raw.astype(F32) + dt_bias.astype(F32))
    A = -jnp.exp(a_log.astype(F32))
    y, h_T = _ssd_scan(xs * dt[..., None], dt * A, Bm, Cm, h0.astype(F32), chunk)
    y = y + d_skip.astype(F32)[:, None] * xs
    y = y.reshape(b, T, SSD_WIDTH) * jax.nn.silu(z.astype(F32))
    yg = y.reshape(b, T, SSD_GROUPS, SSD_WIDTH // SSD_GROUPS)
    yg = yg * lax.rsqrt(jnp.mean(yg * yg, axis=-1, keepdims=True) + EPS)
    return yg.reshape(b, T, SSD_WIDTH) * norm_g.astype(F32), h_T

def _layer(x, mods, lw, attend, conv_prefix, h0, chunk, lam_init):
    (g_mix, g_ffn, w_in, w_out, lq1, lk1, lq2, lk2, subln_g, conv_w, conv_b,
     dt_bias, a_log, d_skip, ssd_norm_g, w_up, w_down) = lw
    sh1, sc1, ga1, sh2, sc2, ga2 = mods
    B, T, _ = x.shape
    h = _rmsnorm(x, g_mix) * (1 + sc1) + sh1
    proj = h @ w_in
    q, k, v, z, xbc, dt_raw = jnp.split(proj, SPLITS, axis=-1)
    q = q.reshape(B, T, ATT_HEADS, 2, ATT_HEAD_DIM)
    k = k.reshape(B, T, ATT_HEADS, 2, ATT_HEAD_DIM)
    v = v.reshape(B, T, ATT_HEADS, ATT_V_DIM)
    o = attend(q, k, v)
    att = _diff_combine(o, _diff_lambda(lq1, lk1, lq2, lk2, lam_init), subln_g, lam_init)
    xbc_act, conv_state = _causal_conv(xbc, conv_prefix, conv_w, conv_b)
    ssd, h_T = _ssd_branch(xbc_act, z, dt_raw, h0, dt_bias, a_log, d_skip, ssd_norm_g, chunk)
    mix = jnp.concatenate([att, ssd], axis=-1).astype(x.dtype) @ w_out
    x = x + ga1 * mix
    h2 = _rmsnorm(x, g_ffn) * (1 + sc2) + sh2
    u = jax.nn.relu(h2 @ w_up)
    x = x + ga2 * ((u * u) @ w_down)
    return x, k, v, conv_state, h_T.astype(x.dtype)

def setup_inputs(seed: int = 0) -> dict:
    key = jax.random.key(seed)
    ks = jax.random.split(key, 40)
    n_pages = PAST_LEN // PAGE_SIZE
    n_used = DEC_BATCH * n_pages
    n_pool = (n_used * 5) // 4
    nrm = lambda k, shape, s: jax.random.normal(k, shape, F32) * s
    dt0 = jnp.exp(jax.random.uniform(ks[20], (DEPTH, SSD_HEADS), F32)
                  * (math.log(0.1) - math.log(0.001)) + math.log(0.001))
    return {
        "x_prompt": nrm(ks[0], (BATCH, SEQ, D_MODEL), 1.0),
        "x_sample": nrm(ks[1], (DEC_BATCH, DEC_SEQ, D_MODEL), 1.0),
        "cache_k": nrm(ks[2], (DEPTH, n_pool, PAGE_SIZE, ATT_HEADS, 2, ATT_HEAD_DIM), 1.0),
        "cache_v": nrm(ks[3], (DEPTH, n_pool, PAGE_SIZE, ATT_HEADS, ATT_V_DIM), 1.0),
        "state_conv": nrm(ks[4], (DEPTH, DEC_BATCH, CONV_W - 1, CONV_DIM), 1.0),
        "state_ssm": nrm(ks[5], (DEPTH, DEC_BATCH, SSD_HEADS, SSD_HEAD_DIM, D_STATE), 0.5),
        "page_table": jax.random.permutation(ks[6], n_pool)[:n_used].reshape(DEC_BATCH, n_pages).astype(jnp.int32),
        "c_prompt": nrm(ks[7], (BATCH, D_MODEL), 1.0),
        "c_sample": nrm(ks[8], (DEC_BATCH, D_MODEL), 1.0),
        "rel_bias": nrm(ks[9], (N_BUCKETS, ATT_HEADS), 0.5),
        "w_ada": nrm(ks[10], (DEPTH, D_MODEL, 6 * D_MODEL), 0.5 * D_MODEL ** -0.5),
        "b_ada": nrm(ks[11], (DEPTH, 6 * D_MODEL), 0.01),
        "g_mix": 1.0 + nrm(ks[12], (DEPTH, D_MODEL), 0.05),
        "g_ffn": 1.0 + nrm(ks[13], (DEPTH, D_MODEL), 0.05),
        "w_in": nrm(ks[14], (DEPTH, D_MODEL, IN_WIDTH), D_MODEL ** -0.5),
        "w_out": nrm(ks[15], (DEPTH, MIX_WIDTH, D_MODEL), MIX_WIDTH ** -0.5),
        "lam_q1": nrm(ks[16], (DEPTH, ATT_HEAD_DIM), 0.1),
        "lam_k1": nrm(ks[17], (DEPTH, ATT_HEAD_DIM), 0.1),
        "lam_q2": nrm(ks[18], (DEPTH, ATT_HEAD_DIM), 0.1),
        "lam_k2": nrm(ks[19], (DEPTH, ATT_HEAD_DIM), 0.1),
        "subln_g": 1.0 + nrm(ks[21], (DEPTH, ATT_V_DIM), 0.05),
        "conv_w": nrm(ks[22], (DEPTH, CONV_W, CONV_DIM), CONV_W ** -0.5),
        "conv_b": nrm(ks[23], (DEPTH, CONV_DIM), 0.01),
        "dt_bias": dt0 + jnp.log(-jnp.expm1(-dt0)),
        "a_log": jnp.log(jax.random.uniform(ks[24], (DEPTH, SSD_HEADS), F32, 1.0, 16.0)),
        "d_skip": 1.0 + nrm(ks[25], (DEPTH, SSD_HEADS), 0.1),
        "ssd_norm_g": 1.0 + nrm(ks[26], (DEPTH, SSD_WIDTH), 0.05),
        "w_up": nrm(ks[27], (DEPTH, D_MODEL, D_FF), D_MODEL ** -0.5),
        "w_down": nrm(ks[28], (DEPTH, D_FF, D_MODEL), D_FF ** -0.5),
        "g_final": 1.0 + nrm(ks[29], (D_MODEL,), 0.05),
    }

def reference(x_prompt, x_sample, cache_k, cache_v, state_conv, state_ssm, page_table,
              c_prompt, c_sample, rel_bias, w_ada, b_ada, g_mix, g_ffn, w_in, w_out,
              lam_q1, lam_k1, lam_q2, lam_k2, subln_g, conv_w, conv_b, dt_bias, a_log,
              d_skip, ssd_norm_g, w_up, w_down, g_final):
    yp, ys = x_prompt, x_sample
    kp_l, vp_l, cp_l, hp_l = [], [], [], []
    ks_l, vs_l, cs_l, hs_l = [], [], [], []
    for l in range(DEPTH):
        lw = (g_mix[l], g_ffn[l], w_in[l], w_out[l], lam_q1[l], lam_k1[l], lam_q2[l],
              lam_k2[l], subln_g[l], conv_w[l], conv_b[l], dt_bias[l], a_log[l],
              d_skip[l], ssd_norm_g[l], w_up[l], w_down[l])
        lam_init = 0.8 - 0.6 * math.exp(-0.3 * l)
        attend_p = functools.partial(_diff_attn_prompt, rel_table=rel_bias)
        prefix_p = jnp.zeros((yp.shape[0], CONV_W - 1, CONV_DIM), yp.dtype)
        h0_p = jnp.zeros((yp.shape[0], SSD_HEADS, SSD_HEAD_DIM, D_STATE), F32)
        yp, kp, vp, cp, hp = _layer(yp, _modulation(c_prompt, w_ada[l], b_ada[l]), lw,
                                    attend_p, prefix_p, h0_p, SSD_CHUNK, lam_init)
        attend_s = functools.partial(_diff_attn_sample, cache_k=cache_k, cache_v=cache_v,
                                     layer=l, page_table=page_table, rel_table=rel_bias)
        ys, k_s, v_s, c_s, h_s = _layer(ys, _modulation(c_sample, w_ada[l], b_ada[l]), lw,
                                        attend_s, state_conv[l], state_ssm[l], ys.shape[1], lam_init)
        kp_l.append(kp); vp_l.append(vp); cp_l.append(cp); hp_l.append(hp)
        ks_l.append(k_s); vs_l.append(v_s); cs_l.append(c_s); hs_l.append(h_s)
    y_prompt = _rmsnorm(yp, g_final)
    y_sample = _rmsnorm(ys, g_final)
    return (y_prompt, y_sample,
            jnp.stack(kp_l), jnp.stack(vp_l), jnp.stack(cp_l), jnp.stack(hp_l),
            jnp.stack(ks_l), jnp.stack(vs_l), jnp.stack(cs_l), jnp.stack(hs_l))


_drawn_inputs = setup_inputs


def setup_inputs(seed=0):
    import zlib

    import numpy as np

    out = dict(_drawn_inputs(seed))
    spreads = {}
    factors = {'subln_g': 6.887, 'conv_b': 4.152, 'd_skip': 4.788, 'ssd_norm_g': 5.629, 'g_ffn': 4.606}
    for name, (base, spread) in spreads.items():
        noise = np.random.default_rng([zlib.crc32(name.encode()), seed]).standard_normal(out[name].shape)
        drawn = base * np.exp(spread * noise) if base else spread * noise
        out[name] = __import__('jax').numpy.asarray(drawn.astype(out[name].dtype))
    for name, factor in factors.items():
        out[name] = (out[name] * factor).astype(out[name].dtype)
    return out
```

```python
from contextlib import ExitStack

import concourse.bass as bass
from concourse import mybir

F32 = mybir.dt.float32
I32 = mybir.dt.int32
ALU = mybir.AluOpType
ACT = mybir.ActivationFunctionType
AX = mybir.AxisListType.X
P = 128

D = 1024
KT = D // P
TP, NB, DT = 512, 8, 8
TS = NB * DT
T = TP + TS
MT = TP // P
PAGES, PAGE = 32, 128
H, HD, VD = 4, 64, 128
SH, SP_, NS, GR = 8, 64, 128, 2
CONV = SH * SP_ + 2 * GR * NS
XT_, BT_ = 4, 4
NF = 4 * D // P
TAB = 384
OFF = 127
BIG = -1.0e30
EPS = 1e-6
IT = 256
IP = 4
SLOTS = 4
SLOT = KT * IT
XPW = 3 + TP + NB * (DT + 3)

C_BADA, C_GMIX, C_GFFN, C_GFIN, C_CB, C_CW, C_SSD, C_SUB = 0, 48, 56, 64, 72, 80, 112, 116
NROW = 117
K_ID, K_ONE, K_NM, K_NMS, K_BLK = 0, P, 2 * P, 3 * P, 3 * P + TS
K_N = K_BLK + NB


class Tally:

    def __init__(self, sem):
        self.sem, self.n = sem, 0

    def up(self, ins):
        ins.then_inc(self.sem, 1)
        self.n = self.n + 1


def link(eng, ins, tally):
    tally.up(ins)
    eng.wait_ge(tally.sem, tally.n)


def program(nc, a, o, scratch):
    ctx = ExitStack()
    with ctx:
        def sb(name, shape):
            return ctx.enter_context(nc.sbuf_tensor(name, shape, F32))

        sems = {}

        def S(name):
            if name not in sems:
                sems[name] = ctx.enter_context(nc.semaphore(name))
            return sems[name]

        ring = sb("ring", [P, SLOTS * SLOT])
        xT = sb("xT", [P, KT, T])
        hT = sb("hT", [P, KT, T])
        mix = sb("mix", [P, KT, T])
        cst = sb("cst", [P, K_N])
        cols = sb("cols", [P, NROW])
        mod = sb("mod", [P, 48, 9])
        g1 = sb("g1", [P, KT, 9])
        g2 = sb("g2", [P, KT, 9])
        rs = sb("rs", [P, T])
        cT = sb("cT", [P, KT, 9])
        small = sb("small", [P, 64])
        rows = sb("rows", [SH, 3, T])
        tok = sb("tok", [P, 5, 3, SH])
        dec = sb("dec", [P, SH, MT + NB])
        arena = sb("arena", [P, 27230])

        def at(off, *shape, parts=P):
            n = 1
            for s in shape:
                n *= s
            v = arena[0:parts, off:off + n]
            if len(shape) == 2:
                v = v.rearrange("p (a b) -> p a b", b=shape[1])
            if len(shape) == 3:
                v = v.rearrange("p (a b c) -> p a b c", b=shape[1], c=shape[2])
            if len(shape) == 4:
                v = v.rearrange("p (a b c d) -> p a b c d", b=shape[1], c=shape[2], d=shape[3])
            return v

        kT = at(0, H, T)
        vtk = at(2304, 5, H * VD)
        zT = at(4864, 4, T)
        qbd = at(7168, NB, H, 2, DT)
        newb = at(7680, NB, H * 2 * DT)
        xp = at(8448, 8, XPW)
        qT = at(13272, H, TP)
        TMP = 15320
        xtok = at(TMP, 5, D)
        crow = at(TMP + 5120, D)
        ctmp = at(TMP + 6144, D)
        scr = at(TMP + 7168, D)
        brow = at(TMP + 8192, 2, TAB)
        hot = at(TMP + 8960, 2, TAB)
        vrow = at(TMP + 9728, P)
        wdt = at(TMP + 9856, KT, SH)
        xtok2 = at(8192, 5, D)
        wrev = at(TMP, H, 2 * P)
        wb = at(TMP + 1024, H, 2 * P)
        pj = at(TMP + 2048, 2, 2, TP)
        pts = at(TMP + 4096, 2, TP)
        kout = at(TMP + 5120, 2, TP)
        p31r = at(TMP + 6144, H, DT)
        newr = at(TMP + 6176, H, DT)
        cv = at(TMP, 2, T)
        ce = at(TMP + 1152, 2, T)
        gc = at(TMP + 2304, 8, 27)
        sout = at(TMP + 7168, D)
        xdt = at(TMP, 5, SH * SP_)
        xw = at(TMP + 2560, 5, SH * SP_)
        prev = at(TMP + 5120, 4, SH * SP_)
        btk = at(TMP + 7168, 5, GR * NS)
        cbT = at(TMP + 8448, GR, T)
        lg = at(TMP + 9600, 2, T)
        ceb = at(TMP + 10752, 2, T)
        h0 = xT[:, :, :].rearrange("p a b -> p (a b)")[:, 0:4096].rearrange("p (b t q) -> p b t q", b=NB, t=4)
        h0T = hT[:, :, :].rearrange("p a b -> p (a b)")[:, 0:4096].rearrange("p (b t q) -> p b t q", b=NB, t=4)
        bblk = at(TMP + 9600, GR, NB, NS)
        xws = xw[0:TS, MT, :]
        hdec = sb("hdec", [P, 4, NB])
        NBLK = PAGES + 1
        kts = at(TMP, 2, 512)
        sc = at(TMP + 1024, NBLK, 64)
        pr = at(TMP + 3136, NBLK, 64)
        mxp = at(TMP + 5570, P)
        mrow = at(TMP + 5312, 1)
        mdg = at(TMP + 5314, 64)
        lsum = at(TMP + 5378, 64)
        rl = at(TMP + 5442, 64)
        on = at(TMP + 5506, 64)
        p31x = sb("p31x", [P, 64])
        u = at(0, NF, T)
        ytok = at(0, 2, D)

        ident = cst[:, K_ID:K_ID + P]
        ones = cst[:, K_ONE:K_ONE + P]
        bk = [ctx.enter_context(nc.psum_tensor(f"bank{i}", [P, 512], F32)) for i in range(8)]

        n_in = 12
        N_ADA1, N_ADA2 = 8, 16
        I_IN = N_ADA1
        I_ADA2 = I_IN + n_in
        I_DEC = I_ADA2 + N_ADA2
        BODY = ["K0", "K1", "V0", "K2", "V1", "K3", "V2", "K4", "V3", "K5", "V4", "K6", "V5", "K7", "V6", "V7"]
        I_LOOP = I_DEC + 8
        I_LAST = I_LOOP + 16 * (NB - 1)
        I_OUT = I_LAST + 8
        I_UP = I_OUT + 4
        I_DOWN = I_UP + 16
        ring_sem = [S(f"ring_loaded{k}") for k in range(SLOTS)]

        def landed(n):
            def upto(lo, hi, inc):
                hi = min(hi, n + 1)
                return sum(inc for m in range(lo, hi) if m % SLOTS == n % SLOTS) if hi > lo else 0
            return upto(0, I_DEC, 16) + upto(I_DEC, I_OUT, 16 * IP) + upto(I_OUT, I_DOWN + 16, 16)

        def slot(n):
            return ring[:, (n % SLOTS) * SLOT:(n % SLOTS + 1) * SLOT]

        def arrived(eng, n, i=0, step=0):
            per = landed(n + step) - landed(n) if step else 0
            eng.wait_ge(ring_sem[n % SLOTS], i * per + landed(n) if step else landed(n))

        def rows4(dram, r0, nk, c0, nc_):
            return dram[r0:r0 + nk * P, c0:c0 + nc_].rearrange("(k p) c -> p k c", p=P)

        def seg(v, s):
            return v[:, s:s + TP], v[:, 3 + TP:XPW].rearrange("p (b w) -> p b w", w=DT + 3)[:, :, s:s + DT]

        sfin = rs[:, 0:512].rearrange("p (t n) -> p t n", t=4)
        block = ctx.enter_context(nc.Block())

        @block.sync
        def _(sp):
            npar = [0]

            def par(dst, src):
                sp.dma_start(dst, src).then_inc(S("params_loaded"), 16)
                npar[0] += 1

            par(crow[0:1, :], a["c_prompt"])
            par(crow[1:9, :], a["c_sample"])
            par(cst[:, :], a["shape_consts"])
            for c0, n, src in ((C_BADA, 48, a["b_ada"][0]), (C_GMIX, 8, a["g_mix"][0]), (C_GFFN, 8, a["g_ffn"][0]),
                               (C_GFIN, 8, a["g_final"]), (C_CB, 8, a["conv_b"][0]), (C_SSD, 4, a["ssd_norm_g"][0]),
                               (C_SUB, 1, a["subln_g"][0])):
                par(vrow[c0:c0 + n, :], src.rearrange("(r c) -> r c", c=P))
            par(vrow[C_CW:C_CW + 32, :], a["conv_w"][0].rearrange("i (r c) -> (i r) c", c=P))
            for j, name in enumerate(("lam_q1", "lam_q2", "lam_k1", "lam_k2")):
                par(small[0:HD, j:j + 1], a[name].rearrange("a b -> b a"))
            for j, name in enumerate(("dt_bias", "a_log", "d_skip")):
                par(small[0:SH, 4 + j:5 + j], a[name].rearrange("a b -> b a"))
            par(small[0:32, 8:12], a["rel_bias"])
            par(scr[0:24, :], a["state_conv"][0].rearrange("b w c -> (b w) c"))
            par(hot[0:33, :, :], a["shape_hot"])
            par(rows[0:SH, 2, :], a["shape_starts"])
            assert npar[0] == N_PAR, npar
            for m in range(MT):
                sp.dma_start(xtok[:, m, :], a["x_prompt"][0, m * P:(m + 1) * P, :]).then_inc(S("x_loaded"), 16)
            sp.dma_start(xtok[0:TS, MT, :], a["x_sample"].rearrange("b t d -> (b t) d")).then_inc(S("x_loaded"), 16)

            def free(n, i=None, step=0):
                if i is not None:
                    sp.wait_ge(S("ring_used"), i * step + (n - SLOTS + 1))
                elif n >= SLOTS:
                    sp.wait_ge(S("ring_used"), n - SLOTS + 1)

            def load(n, src, nk=KT, i=None, step=0):
                free(n, i, step)
                sp.dma_start(slot(n).rearrange("p (k c) -> p k c", k=nk), src).then_inc(ring_sem[n % SLOTS], 16)

            w_ada, w_in = a["w_ada"][0], a["w_in"][0]
            for n in range(N_ADA1):
                load(n, rows4(w_ada, 0, KT, n * IT, IT))
            sp.dma_start(wdt[:, :, :], rows4(w_in, 0, KT, 3072, SH)).then_inc(S("wdt_loaded"), 16)
            for n in range(n_in):
                load(I_IN + n, rows4(w_in, 0, KT, n * IT, IT))
            sp.wait_ge(S("tables_ready"), 1)
            sp.dma_start(scratch.rearrange("r h t -> h r t"), brow[0:H, :, :]).then_inc(S("tables_stored"), 16)
            sp.wait_ge(S("tables_stored"), 16)
            sp.wait_ge(S("x_free"), 1)
            f0 = bass.AP(scratch.tensor, scratch.offset, [[1, P], [TAB, H], [1, 2 * P]])
            sp.dma_start(wrev, f0).then_inc(S("bias_loaded"), 16)
            rev = scratch.offset + H * TAB
            sp.dma_start(p31r, bass.AP(scratch.tensor, rev + 120, [[1, P], [TAB, H], [1, DT]]))\
                .then_inc(S("bias_loaded"), 16)
            for b in range(NB):
                sp.dma_start(newr[b * DT:(b + 1) * DT, :, :],
                             bass.AP(scratch.tensor, rev + 248, [[1, DT], [TAB, H], [1, DT]]))\
                    .then_inc(S("bias_loaded"), 16)
            with sp.Fori(0, N_ADA2 // SLOTS) as i:
                for k in range(SLOTS):
                    load(I_ADA2 + k, w_ada[:, bass.ds((i * SLOTS + (N_ADA1 + k)) * IT, IT)]
                         .rearrange("(k p) c -> p k c", p=P), i=i, step=SLOTS)

            for m in range(5):
                sp.wait_ge(S("kout_ready"), m + 1)
                n = P if m < MT else TS
                dst = o["k_p"][m * P:(m + 1) * P, :] if m < MT else o["k_s"]
                sp.dma_start(dst, kout[0:n, m % 2, :]).then_inc(S(f"kout_stored{m % 2}"), 16)
            for m in range(5):
                n = P if m < MT else TS
                dst = o["v_p"][m * P:(m + 1) * P, :] if m < MT else o["v_s"]
                sp.dma_start(dst, vtk[0:n, m, :]).then_inc(S("out_stored"), 16)
            sp.wait_ge(S("conv_rows"), 1)
            sp.dma_start(o["conv_p"], sout[0:3, :]).then_inc(S("out_stored"), 16)
            sp.dma_start(o["conv_s"], sout[3:27, :]).then_inc(S("out_stored"), 16)
            sp.wait_ge(S("out_stored"), 16 * 7)
            sp.wait_ge(S("xn"), KT)
            for b in range(NB):
                sp.dma_start(h0[:, b, :, :], a["state_ssm"][0, b].rearrange("(t h) p n -> (h p) t n", t=4))\
                    .then_inc(S("h0_loaded"), 16)
            sp.wait_ge(S("final_ready"), 1)
            sp.dma_start(o["ssm_p"].rearrange("(t p) n -> p t n", p=P), sfin).then_inc(S("out_stored"), 16)
            sp.wait_ge(S("ssm_ready"), 1)
            for b in range(NB):
                sp.dma_start(o["ssm_s"][b * 512:(b + 1) * 512, :].rearrange("(t p) n -> p t n", p=P), h0[:, b, :, :])\
                    .then_inc(S("ssm_stored"), 16)
            sp.wait_ge(S("ssm_stored"), 16 * NB)
            for m in range(MT):
                sp.dma_start(xtok2[:, m, :], a["x_prompt"][0, m * P:(m + 1) * P, :]).then_inc(S("x_loaded"), 16)
            sp.dma_start(xtok2[0:TS, MT, :], a["x_sample"].rearrange("b t d -> (b t) d")).then_inc(S("x_loaded"), 16)

            kc, vc = a["cache_k"], a["cache_v"]
            pt = a["page_table"]

            def pages(n, what, b, i=None, step=0):
                g = int(what[1:])
                _, phys = nc.values_load_multi_w_load_instructions(
                    pt[bass.ds(b, 1), g * IP:(g + 1) * IP], engines=[mybir.EngineType.SP],
                    min_val=0, max_val=N_POOL - 1)
                free(n, i, step)
                src = kc if what[0] == "K" else vc
                for p in range(IP):
                    sp.dma_start(slot(n)[:, p * 512:(p + 1) * 512],
                                 src[bass.ds(phys[p], 1), :, :].rearrange("a p f -> (a p) f"))\
                        .then_inc(ring_sem[n % SLOTS], 16)

            for g in range(8):
                pages(I_DEC + g, f"K{g}", 0)
            with sp.Fori(0, NB - 1) as i:
                for k, what in enumerate(BODY):
                    pages(I_LOOP + k, what, i + 1 if what[0] == "K" else i, i=i, step=16)
            for g in range(8):
                pages(I_LAST + g, f"V{g}", NB - 1)

            for k in range(4):
                load(I_OUT + k, rows4(a["w_out"][0], 0, KT, k * IT, IT))
            with sp.Fori(0, 4) as i:
                for k in range(4):
                    load(I_UP + k, a["w_up"][0][:, bass.ds((i * 4 + k) * IT, IT)]
                         .rearrange("(k p) c -> p k c", p=P), i=i, step=4)
            with sp.Fori(0, 4) as i:
                for k in range(4):
                    load(I_DOWN + k, a["w_down"][0][k * D:(k + 1) * D, bass.ds(i * IT, IT)]
                         .rearrange("(k p) c -> p k c", p=P), i=i, step=4)
            for m in range(5):
                sp.wait_ge(S("yt_a"), m + 1)
                sp.wait_ge(S("yt_v"), m + 1)
                n = P if m < MT else TS
                dst = o["y_p"][m * P:(m + 1) * P, :] if m < MT else o["y_s"]
                sp.dma_start(dst, ytok[0:n, m % 2, :]).then_inc(S(f"y_stored{m % 2}"), 16)
            for k, stores in enumerate((3, 2)):
                sp.wait_ge(S(f"y_stored{k}"), 16 * stores)
                sp.wait_ge(S(f"kout_stored{k}"), 16 * stores)
            sp.wait_ge(S("out_stored"), 16 * 8)


        tiles = [("q", h) for h in range(4)] + [("k", h) for h in range(4)]
        tiles += [("v", 5 * half + m) for half in range(2) for m in range(5)] + [("d", 0)]
        tiles += [("z", t) for t in range(4)] + [("x", c) for c in range(8)]
        by_dve = [sum(1 for kind, _ in tiles[:n] if kind not in "v") for n in range(len(tiles) + 1)]
        first = {"q": 0, "k": 2, "v": 4, "z": 6, "x": 8}
        tile_sign, plain = [], 0
        for kind, t in tiles:
            if (kind == "v" and t % 5 == 4) or (kind in "qkzx" and t % 2 == 1):
                tile_sign.append(("ring_used", I_IN + first[kind] + (t // 5 if kind == "v" else t // 2) + 1))
            else:
                plain += 1
                tile_sign.append(("ip_ps", plain))

        @block.gpsimd
        def _(pool):
            pool.memset(small[32:33, 8:12], 1.0).then_inc(S("ones_row"), 1)
            pool.wait_ge(S("ones_row"), 1)
            pool.memset(qbd, 0.0).then_inc(S("qbd_zero"), 1)
            pool.wait_ge(S("qbd_zero"), 1)
            pool.memset(xp[:, :, 0:3], 0.0).then_inc(S("xp_zero"), 1)

        @block.tensor
        def _(pe):
            mm, tr = pe.matmul, pe.transpose

            def turn_x(k, src):
                pe.wait_ge(S("x_loaded"), 16 * 5 * (k + 1))
                for m in range(5):
                    n = P if m < MT else TS
                    for half in range(2):
                        w = 2 * m + half
                        if w >= 4:
                            pe.wait_ge(S("xt_a" if half == 0 else "xt_v"), 5 * k + (w - 4) // 2 + 1)
                        for f in range(4):
                            ins = tr(bk[w % 4][:, f * P:f * P + n],
                                     src[0:n, m, (4 * half + f) * P:(4 * half + f + 1) * P], ident[0:n, 0:n])
                        ins.then_inc(S("xt_ps"), 1)

            pe.wait_ge(S("params_loaded"), 16 * N_PAR)
            tr(bk[4][:, 0:NROW], vrow[0:NROW, :], ident[0:NROW, 0:NROW]).then_inc(S("cols_ps"), 1)
            turn_x(0, xtok)
            pe.wait_ge(S("silu_rows"), 1)
            for k in range(KT):
                ins = tr(bk[5][:, k * 9:(k + 1) * 9], ctmp[0:9, k * P:(k + 1) * P], ident[0:9, 0:9])
            ins.then_inc(S("ct_ps"), 1)
            pe.wait_ge(S("lam_prod"), 1)
            mm(bk[6][:, 0:2], ones[0:HD, :], small[0:HD, 12:14], start=True, stop=True)
            for t in range(4):
                for r in range(2):
                    ins = mm(bk[6][64 * r:64 * r + 64, 4 + t:5 + t],
                             ident[0:SH, 2 * t + r:2 * t + r + 1].to_broadcast([SH, SP_]), small[0:SH, 6:7],
                             start=True, stop=True)
            ins.then_inc(S("lam_ps"), 1)
            pe.wait_ge(S("ones_row"), 1)
            pe.wait_ge(S("lam_ready"), 1)
            for r in range(2):
                ins = mm(bk[6 + r][0:H, 0:TAB], small[0:33, 8:12], hot[0:33, r, :], start=True, stop=True)
            ins.then_inc(S("tables_ps"), 1)
            pe.wait_ge(S("tables_ready"), 1)
            for c in range(8):
                ins = tr(bk[6][:, c * 24:(c + 1) * 24], scr[0:24, c * P:(c + 1) * P], ident[0:24, 0:24])
            ins.then_inc(S("cs_ps"), 1)
            pe.wait_ge(S("prefix_ready"), 1)

            def norm_sum(k):
                for f in range(KT):
                    pe.wait_ge(S("squares"), KT * k + f + 1)
                    mm(bk[6][:, :], ones, hT[:, f, 0:TP], start=(f == 0), stop=(f == KT - 1))
                    ins = mm(bk[7][:, 0:TS], ones, hT[:, f, TP:T], start=(f == 0), stop=(f == KT - 1))
                ins.then_inc(S("ssum"), 1)

            def ada(bank, n0, i, j):
                arrived(pe, n0 + j, i, SLOTS)
                w = slot(n0 + j).rearrange("p (k c) -> p k c", k=KT)
                for t in range(2):
                    col = i * (2 * SLOTS * 9) + (2 * j + t) * 9
                    for f in range(KT):
                        ins = mm(bank[:, bass.ds(col, 9)], w[:, f, t * P:(t + 1) * P], cT[:, f, :],
                                 start=(f == 0), stop=(f == KT - 1))
                ins.then_inc(S("ring_used"), 1)

            pe.wait_ge(S("ct_ready"), 1)
            with pe.Fori(0, N_ADA1 // SLOTS) as i:
                for j in range(SLOTS):
                    ada(bk[4], 0, i, j)
            norm_sum(0)

            pe.wait_ge(S("h_prompt"), KT)
            pe.wait_ge(S("h_sample"), 1)

            def dense(bp, bs, w, c0, m, ks, src, start, stop):
                for j, f in enumerate(ks):
                    s, e = start and j == 0, stop and j == len(ks) - 1
                    mm(bp[0:m, :], w[:, j, c0:c0 + m], src[:, f, 0:TP], start=s, stop=e)
                    ins = mm(bs[0:m, 0:TS], w[:, j, c0:c0 + m], src[:, f, TP:T], start=s, stop=e)
                return ins

            for n, (kind, t) in enumerate(tiles):
                bp, bs = bk[2 * (n % 2)], bk[2 * (n % 2) + 1]
                if n >= 2:
                    pe.wait_ge(S("ip_act"), n - 1)
                    if by_dve[n - 1] > 0:
                        pe.wait_ge(S("ip_dve"), by_dve[n - 1])
                sign = tile_sign[n][0]
                if kind == "v":
                    half, m = t // 5, t % 5
                    k = I_IN + first["v"] + half
                    r = P if m < MT else TS
                    if m == 0:
                        arrived(pe, k)
                    w = slot(k).rearrange("p (k c) -> p k c", k=KT)
                    for f in range(KT):
                        ins = mm(bp[0:r, 0:IT], hT[:, f, m * P:m * P + r], w[:, f, :],
                                 start=(f == 0), stop=(f == KT - 1))
                elif kind == "d":
                    pe.wait_ge(S("wdt_loaded"), 16)
                    ins = dense(bp, bs, wdt, 0, SH, range(KT), hT, True, True)
                else:
                    k = I_IN + first[kind] + t // 2
                    if t % 2 == 0:
                        arrived(pe, k)
                    w = slot(k).rearrange("p (k c) -> p k c", k=KT)
                    ins = dense(bp, bs, w, (t % 2) * P, P, range(KT), hT, True, True)
                ins.then_inc(S(sign), 1)

            with pe.Fori(0, N_ADA2 // SLOTS) as i:
                for j in range(SLOTS):
                    ada(bk[5], I_ADA2, i, j)

            for m in range(5):
                n = P if m < MT else TS
                if m == 0:
                    pe.wait_ge(S("ip_act"), len(tiles))
                    pe.wait_ge(S("ip_dve"), by_dve[-1])
                if m >= 2:
                    pe.wait_ge(S("kout_ready"), m - 1)
                for h in range(H):
                    ins = tr(bk[m % 2][0:n, h * P:(h + 1) * P], kT[:, h, m * P:m * P + n], ident)
                ins.then_inc(S("kout_ps"), 1)

            units = [(h, qb) for h in range(H) for qb in range(MT)]

            def att_scores(x):
                h, qb = units[x]
                nk = (qb + 1) * P
                if x >= 2:
                    pe.wait_ge(S("att_exp"), 2 * (x - 1))
                for j in range(2):
                    ins = mm(bk[2 + 2 * (x % 2) + j][:, 0:nk], qT[64 * j:64 * j + 64, h, qb * P:(qb + 1) * P],
                             kT[64 * j:64 * j + 64, h, 0:nk], start=True, stop=True)
                ins.then_inc(S("att_s"), 1)

            def att_transpose(x):
                h, qb = units[x]
                pe.wait_ge(S("att_p"), x + 1)
                if x >= 2:
                    pe.wait_ge(S("att_pt"), x - 1)
                for kb in range(qb + 1):
                    ins = tr(bk[6 + x % 2][:, kb * P:(kb + 1) * P], pj[:, x % 2, 0, kb * P:(kb + 1) * P], ident)
                ins.then_inc(S("att_t"), 1)

            def att_values(x):
                h, qb = units[x]
                pe.wait_ge(S("att_pt"), x + 1)
                if qb == 0 and h >= 2:
                    pe.wait_ge(S("att_o"), h - 1)
                for kb in range(qb + 1):
                    ins = mm(bk[h % 2][:, qb * P:(qb + 1) * P], vtk[:, kb, h * VD:(h + 1) * VD],
                             pts[:, x % 2, kb * P:(kb + 1) * P], start=(kb == 0), stop=(kb == qb))
                ins.then_inc(S("att_v"), 1)

            pe.wait_ge(S("kout_ready"), 5)
            NU = len(units)
            for x in range(NU + 2):
                if x < NU:
                    att_scores(x)
                if 1 <= x <= NU:
                    att_transpose(x - 1)
                if x >= 2:
                    att_values(x - 2)
            def head_norm(bank, k, n):
                pe.wait_ge(S("att_sq"), k + 1)
                mm(bank[:, 0:n], ones, hT[:, k % H, 0:n], start=True, stop=True).then_inc(S("att_ss"), 1)

            for h in range(H):
                head_norm(bk[2 + h], h, TP)

            pe.wait_ge(S("ends_ready"), 1)
            pe.wait_ge(S("att_n"), H)
            for c in range(8):
                ins = tr(bk[c // 4][0:27, (c % 4) * P:(c % 4 + 1) * P], gc[:, c, :], ident)
            ins.then_inc(S("conv_ps"), 1)

            pe.wait_ge(S("rows_ready"), 1)
            for m in range(5):
                n = P if m < MT else TS
                for r in range(3):
                    ins = tr(bk[6][0:n, (3 * m + r) * SH:(3 * m + r + 1) * SH], rows[0:SH, r, m * P:m * P + n],
                             ident[0:SH, 0:SH])
            ins.then_inc(S("tok_ps"), 1)
            for h in range(SH):
                ins = mm(bk[7][:, h * 12:(h + 1) * 12], ident[0:SH, h:h + 1].to_broadcast([SH, P]),
                         small[0:SH, 24:36], start=True, stop=True)
            ins.then_inc(S("dec_ps"), 1)
            pe.wait_ge(S("xa_ready"), 8)
            pe.wait_ge(S("conv_rows"), 1)
            for m in range(5):
                n = P if m < MT else TS
                if m >= 2:
                    pe.wait_ge(S("xtk_v"), m - 1)
                for t in range(4):
                    ins = tr(bk[m % 2][0:n, t * P:(t + 1) * P], xp[:, t, m * P:m * P + n], ident)
                ins.then_inc(S("xtk_ps"), 1)
                if m >= 2:
                    pe.wait_ge(S("btk_a"), m - 1)
                for g in range(GR):
                    ins = tr(bk[2 + m % 2][0:n, g * P:(g + 1) * P], xp[:, 4 + g, m * P:m * P + n], ident)
                ins.then_inc(S("btk_ps"), 1)
            for g in range(GR):
                if g == 0:
                    pe.wait_ge(S("dec_sb"), 1)
                for c in range(MT):
                    ins = mm(bk[4 + g][:, c * P:(c + 1) * P], xp[:, 4 + g, c * P:(c + 1) * P],
                             xp[:, 6 + g, c * P:(c + 1) * P], start=True, stop=True)
                ins.then_inc(S("cb_ps"), 1)
            for g in range(GR):
                ins = mm(bk[6][0:TS, g * TS:(g + 1) * TS], xp[:, 4 + g, TP:T], xp[:, 6 + g, TP:T],
                         start=True, stop=True)
            ins.then_inc(S("cb_ps"), 1)
            pe.wait_ge(S("xtk_v"), 5)
            pe.wait_ge(S("btk_a"), 5)
            for c in range(MT):
                for g in range(GR):
                    ins = mm(bk[c][:, g * 256:(g + 1) * 256], btk[:, c, g * NS:(g + 1) * NS],
                             xw[:, c, g * 256:(g + 1) * 256], start=True, stop=True)
                ins.then_inc(S("st_ps"), 1)

            def bcast(h):
                if h >= 2:
                    pe.wait_ge(S("cexp"), h - 1)
                sel = ident[0:SH, h:h + 1].to_broadcast([SH, P])
                mm(bk[h % 2][:, :], sel, rows[0:SH, 1, 0:TP], start=True, stop=True)
                mm(bk[2 + h % 2][:, 0:TS], sel, rows[0:SH, 1, TP:T], start=True, stop=True).then_inc(S("cs_bc"), 1)

            def ssd_y(h):
                t, r = h // 2, h % 2
                pe.wait_ge(S("g_ready"), h + 1)
                if r == 0 and t >= 2:
                    pe.wait_ge(S("y_sb"), t - 1)
                y, ys = bk[4 + t % 2][64 * r:64 * r + 64, :], bk[6 + t % 2][64 * r:64 * r + 64, :]
                hs = slice(h * SP_, (h + 1) * SP_)
                for c in range(MT):
                    mm(y[:, c * P:(c + 1) * P], xdt[:, c, hs], lg[:, h % 2, c * P:(c + 1) * P],
                       start=True, stop=(c == 0))
                    if c:
                        mm(y[:, c * P:(c + 1) * P], prev[:, c - 1, hs], ceb[:, h % 2, c * P:(c + 1) * P],
                           start=False, stop=True)
                mm(ys[:, 0:TS], xdt[0:TS, MT, hs], lg[0:TS, h % 2, TP:T], start=True, stop=False)
                for b in range(NB):
                    ins = mm(ys[:, b * DT:(b + 1) * DT], h0T[:, b, t, 64 * r:64 * r + 64],
                             ceb[:, h % 2, TP + b * DT:TP + (b + 1) * DT], start=False, stop=(b == NB - 1))
                ins.then_inc(S("y_ps"), 1)

            pe.wait_ge(S("prev_done"), 1)
            for t in range(4):
                ins = tr(bk[3][:, t * P:(t + 1) * P], prev[:, MT - 1, t * P:(t + 1) * P], ident)
            ins.then_inc(S("final_ps"), 1)
            pe.wait_ge(S("h0_loaded"), 16 * NB)
            for b in range(NB):
                if b >= 2:
                    pe.wait_ge(S("h0t_sb"), b - 1)
                for t in range(4):
                    ins = tr(bk[b % 2][:, t * P:(t + 1) * P], h0[:, b, t, :], ident)
                ins.then_inc(S("h0t_ps"), 1)
            pe.wait_ge(S("h0t_sb"), NB)
            pe.wait_ge(S("cb_sb"), 3)
            pe.wait_ge(S("final_ready"), 1)
            bcast(0)
            bcast(1)
            for h in range(SH):
                ssd_y(h)
                if h + 2 < SH:
                    bcast(h + 2)
            for g in range(GR):
                for t in (2 * g, 2 * g + 1):
                    pe.wait_ge(S("ssd_sq"), t + 1)
                    mm(bk[2 * g][:, :], ones, hT[:, t, 0:TP], start=(t % 2 == 0), stop=(t % 2 == 1))
                    ins = mm(bk[2 * g + 1][:, 0:TS], ones, hT[:, t, TP:T], start=(t % 2 == 0), stop=(t % 2 == 1))
                ins.then_inc(S("ssd_ss"), 1)
            pe.wait_ge(S("bblk_ready"), 1)
            for t in range(4):
                for q in range(2):
                    x = 2 * t + q
                    if x >= 2:
                        pe.wait_ge(S("ssm_sb"), x - 1)
                    mm(bk[4 + q][:, :], xws[:, t * P:(t + 1) * P],
                       bblk[0:TS, t // 2, 4 * q:4 * q + 4, :].rearrange("p b n -> p (b n)"),
                       start=True, stop=True).then_inc(S("ssm_ps"), 1)

            pe.wait_ge(S("dec_start"), 1)
            pe.wait_ge(S("dec_start_a"), 1)

            def k_item(n, b, g, i=None, step=0):
                if i is None:
                    arrived(pe, n)
                else:
                    arrived(pe, n, i, step)
                it = 0 if i is None else (i + 1) * PAGES
                src = slot(n).rearrange("p (q c) -> p q c", q=IP)

                def turn(p):
                    page = IP * g + p
                    for h in range(H):
                        ins = tr(bk[page % 2][:, h * P:(h + 1) * P], src[:, p, h * P:(h + 1) * P], ident)
                    ins.then_inc(S("kt_ps" if p < IP - 1 else "ring_used"), 1)

                def score(p):
                    page = IP * g + p
                    sbk = bk[2 + (g // 2) % 2]
                    pe.wait_ge(S("kt_sb"), it + (page + 1))
                    if page % 8 == 0 and (i is not None or g // 2 >= 2):
                        pe.wait_ge(S("s_sb"), (0 if i is None else (i + 1) * 4) + (g // 2 - 1))
                    for h in range(H):
                        col = (page % 8) * 64 + h * 16
                        rhs = qbd[:, bass.ds(b, 1), h, :, :].rearrange("p a j t -> p (a j t)")
                        ins = mm(sbk[:, col:col + 16], kts[:, page % 2, h * P:(h + 1) * P], rhs,
                                 start=True, stop=True)
                    if page % 8 == 7:
                        ins.then_inc(S("s_ps"), 1)

                turn(0)
                for p in range(IP):
                    if p + 1 < IP:
                        turn(p + 1)
                    score(p)

            def new_scores(b, i=None):
                for h in range(H):
                    rhs = qbd[:, bass.ds(b, 1), h, :, :].rearrange("p a j t -> p (a j t)")
                    ins = mm(bk[4][0:TS, h * 16:h * 16 + 16], kT[:, h, TP:T], rhs, start=True, stop=True)
                ins.then_inc(S("new_ps"), 1)

            def max_rows(i):
                pe.wait_ge(S("mx_ready"), i + 1)
                tr(bk[4][:, 0:P], mxp, ident).then_inc(S("mxt_ps"), 1)

            def max_bcast(i):
                pe.wait_ge(S("mdg_ready"), i + 1)
                mm(bk[4][:, 0:64], ones[0:64, :], mdg[0:64, :], start=True, stop=True).then_inc(S("mbc_ps"), 1)

            def sum_bcast(i):
                pe.wait_ge(S("lsum_ready"), i + 1)
                mm(bk[4][:, 0:64], ones, lsum, start=True, stop=True).then_inc(S("lbc_ps"), 1)

            def v_item(n, g, it, i=None, step=0):
                if i is None:
                    arrived(pe, n)
                else:
                    arrived(pe, n, i, step)
                src = slot(n).rearrange("p (q c) -> p q c", q=IP)
                if g == 0:
                    pe.wait_ge(S("exp_done"), it + 1)
                    pe.wait_ge(S("o_free"), it + 1)
                for p in range(IP):
                    page = IP * g + p
                    for h in range(H):
                        ins = mm(bk[5][:, h * 16:h * 16 + 16], src[:, p, h * P:(h + 1) * P],
                                 pr[:, page, h * 16:h * 16 + 16], start=(page == 0 and h == 0), stop=False,
                                 skip_group_check=True)
                ins.then_inc(S("ring_used"), 1)
                if g == 7:
                    for h in range(H):
                        ins = mm(bk[5][:, h * 16:h * 16 + 16], vtk[0:TS, MT, h * VD:(h + 1) * VD],
                                 pr[0:TS, PAGES, h * 16:h * 16 + 16], start=False, stop=True,
                                 skip_group_check=True)
                    ins.then_inc(S("o_ps"), 1)

            for g in range(8):
                k_item(I_DEC + g, 0, g)
            new_scores(0)
            with pe.Fori(0, NB - 1) as i:
                for k, what in enumerate(BODY):
                    g = int(what[1:])
                    if what[0] == "K":
                        k_item(I_LOOP + k, i + 1, g, i=i, step=16)
                    else:
                        if what == "V6":
                            pe.wait_ge(S("rl_ready"), i + 1)
                        v_item(I_LOOP + k, g, i, i=i, step=16)
                    if what == "K0":
                        max_rows(i)
                    if what == "K1":
                        max_bcast(i)
                    if what == "V1":
                        sum_bcast(i)
                    if what == "V6":
                        new_scores(i + 1, i)
            max_rows(NB - 1)
            max_bcast(NB - 1)
            for g in range(8):
                v_item(I_LAST + g, g, NB - 1)
                if g == 1:
                    sum_bcast(NB - 1)
            pe.wait_ge(S("od_sq"), 1)
            mm(bk[4][:, 0:H * TS], ones, hT[:, 0, 0:H * TS], start=True, stop=True).then_inc(S("od_ss"), 1)
            turn_x(1, xtok2)

            pe.wait_ge(S("mix_ready"), 1)
            pe.wait_ge(S("xt_a"), 10)
            pe.wait_ge(S("xt_v"), 10)

            for k in range(4):
                arrived(pe, I_OUT + k)
                w = slot(I_OUT + k).rearrange("p (k c) -> p k c", k=KT)
                for t in range(2):
                    x = 2 * k + t
                    if x >= 2:
                        pe.wait_ge(S("op_sb"), x - 1)
                    bp, bs = bk[2 * (x % 2)], bk[2 * (x % 2) + 1]
                    dense(bp, bs, w, t * P, P, range(KT), mix, True, True)\
                        .then_inc(S("op_ps" if t == 0 else "ring_used"), 1)
            norm_sum(1)
            pe.wait_ge(S("h_prompt"), 2 * KT)
            pe.wait_ge(S("h_sample"), 2)
            with pe.Fori(0, 4) as i:
                for k in range(4):
                    arrived(pe, I_UP + k, i, 4)
                    w = slot(I_UP + k).rearrange("p (k c) -> p k c", k=KT)
                    for t in range(2):
                        x = 2 * k + t
                        pe.wait_ge(S("up_act"), i * 8 + (x + 1))
                        bp, bs = bk[2 * (x % 2)], bk[2 * (x % 2) + 1]
                        dense(bp, bs, w, t * P, P, range(KT), hT, True, True)\
                            .then_inc(S("up_ps" if t == 0 else "ring_used"), 1)
            pe.wait_ge(S("u_ready"), NF)
            with pe.Fori(0, 4) as i:
                for k in range(4):
                    arrived(pe, I_DOWN + k, i, 4)
                    w = slot(I_DOWN + k).rearrange("p (k c) -> p k c", k=KT)
                    for t in range(2):
                        if k == 0:
                            pe.wait_ge(S("down_sb"), i * 2 + (t + 1))
                        bp, bs = bk[2 * t], bk[2 * t + 1]
                        ins = dense(bp, bs, w, t * P, P, range(8 * k, 8 * k + 8), u, k == 0, k == 3)
                        if t == 1:
                            ins.then_inc(S("ring_used"), 1)
                        elif k == 3:
                            ins.then_inc(S("down_ps"), 1)
            norm_sum(2)
            pe.wait_ge(S("h_prompt"), 3 * KT)
            for m in range(5):
                n = P if m < MT else TS
                for half in range(2):
                    w = 2 * m + half
                    if w >= 4:
                        pe.wait_ge(S("yt_a" if half == 0 else "yt_v"), (w - 4) // 2 + 1)
                    for k in range(4):
                        ins = tr(bk[w % 4][0:n, k * P:(k + 1) * P], hT[:, 4 * half + k, m * P:m * P + n], ident)
                    ins.then_inc(S("yt_ps"), 1)

        @block.scalar
        def _(act):
            step = Tally(S("act_step"))

            def A(out, in_, f, **kw):
                return act.activation(out, in_, f, **kw)

            act.wait_ge(S("params_loaded"), 16 * N_PAR)
            A(ctmp[0:9, :], crow[0:9, :], ACT.Exp, scale=-1.0).then_inc(S("silu_exp"), 1)
            A(small[0:SH, 16:17], small[0:SH, 5:6], ACT.Exp).then_inc(S("alog_exp"), 1)

            def take_x(k):
                for m in range(5):
                    n = P if m < MT else TS
                    w = 2 * m
                    act.wait_ge(S("xt_ps"), 10 * k + w + 1)
                    A(xT[:, 0:4, m * P:m * P + n], bk[w % 4][:, :].rearrange("p (k c) -> p k c", k=4)[:, :, 0:n],
                      ACT.Copy).then_inc(S("xt_a"), 1)

            take_x(0)
            act.wait_ge(S("lam_ps"), 1)
            A(small[:, 18:20], bk[6][:, 0:2], ACT.Exp).then_inc(S("lam_exp"), 1)
            act.wait_ge(S("xt_v"), 5)
            act.wait_ge(S("xt_a"), 5)

            def norm(k):
                for f in range(KT):
                    A(hT[:, f, :], xT[:, f, :], ACT.Square).then_inc(S("squares"), 1)
                act.wait_ge(S("ssum"), k + 1)
                link(act, A(rs[:, 0:TP], bk[6][:, :], ACT.Ln, scale=1.0 / D, bias=cst_eps), step)
                link(act, A(rs[:, TP:T], bk[7][:, 0:TS], ACT.Ln, scale=1.0 / D, bias=cst_eps), step)
                A(rs[:, :], rs[:, :], ACT.Exp, scale=-0.5).then_inc(S("rstd"), 1)

            def modulate(k, g, sh):
                for f in range(KT):
                    act.wait_ge(S("xn"), KT * k + f + 1)
                    A(hT[:, f, 0:TP], hT[:, f, 0:TP], ACT.Identity, scale=g[:, f, 0:1], bias=mod[:, sh + f, 0:1])\
                        .then_inc(S("h_prompt"), 1)

            cst_eps = small[:, 63:64]
            act.wait_ge(S("eps_ready"), 1)
            norm(0)
            act.wait_ge(S("mod1"), 1)
            modulate(0, g1, 0)

            for n, (kind, t) in enumerate(tiles):
                bp = bk[2 * (n % 2)]
                sign, count = tile_sign[n]
                act.wait_ge(S(sign), count)
                if kind == "q":
                    ins = A(qT[:, t, :], bp[:, :], ACT.Copy, scale=HD ** -0.5)
                elif kind == "k":
                    ins = A(kT[:, t, 0:TP], bp[:, :], ACT.Copy)
                elif kind == "v":
                    half, m = t // 5, t % 5
                    r = P if m < MT else TS
                    ins = A(vtk[0:r, m, half * IT:(half + 1) * IT], bp[0:r, 0:IT], ACT.Copy)
                elif kind == "d":
                    ins = A(rs[0:SH, 0:TP], bp[0:SH, :], ACT.Identity, bias=small[0:SH, 4:5])
                elif kind == "z":
                    ins = A(zT[:, t, 0:TP], bp[:, :], ACT.Copy)
                else:
                    ins = A(xp[:, t, 3:3 + TP], bp[:, :], ACT.Copy)
                ins.then_inc(S("ip_act"), 1)
            NU = 16
            for x in range(NU + 1):
                if x < NU:
                    h, qb = x // MT, x % MT
                    nk = (qb + 1) * P
                    for j in range(2):
                        act.wait_ge(S("att_m"), 2 * x + j + 1)
                        if x >= 2 and j == 0:
                            act.wait_ge(S("att_t"), x - 1)
                        A(pj[:, x % 2, j, 0:nk], bk[2 + 2 * (x % 2) + j][:, 0:nk], ACT.Exp,
                          bias=small[:, 36 + 2 * (x % 2) + j:37 + 2 * (x % 2) + j],
                          accum_out=small[:, 40 + 2 * (x % 2) + j:41 + 2 * (x % 2) + j]).then_inc(S("att_exp"), 1)
                if x >= 1:
                    y = x - 1
                    act.wait_ge(S("att_t"), y + 1)
                    if y >= 2:
                        act.wait_ge(S("att_v"), y - 1)
                    nk = (y % MT + 1) * P
                    A(pts[:, y % 2, 0:nk], bk[6 + y % 2][:, 0:nk], ACT.Copy).then_inc(S("att_pt"), 1)
            for h in range(H):
                act.wait_ge(S("att_o"), h + 1)
                A(hT[:, h, 0:TP], mix[:, h, 0:TP], ACT.Square).then_inc(S("att_sq"), 1)
            for h in range(H):
                act.wait_ge(S("att_ss"), h + 1)
                link(act, A(hT[:, 4 + h, 0:TP], bk[2 + h][:, :], ACT.Ln, scale=1.0 / VD, bias=cst_eps), step)
                A(hT[:, 4 + h, 0:TP], hT[:, 4 + h, 0:TP], ACT.Exp, scale=-0.5).then_inc(S("att_r"), 1)

            act.wait_ge(S("ends_ready"), 1)
            for c in range(9):
                if c < 8:
                    if c >= 2:
                        act.wait_ge(S("xa_ready"), c - 1)
                    pp, ss = seg(xp[:, c, :], 0)
                    w0, b0 = cols[:, C_CW + c:C_CW + c + 1], cols[:, C_CB + c:C_CB + c + 1]
                    A(cv[:, c % 2, 0:TP], pp, ACT.Identity, scale=w0, bias=b0).then_inc(S("tap0"), 1)
                    A(cv[:, c % 2, TP:T].rearrange("p (b t) -> p b t", b=NB), ss, ACT.Identity, scale=w0, bias=b0)\
                        .then_inc(S("tap0"), 1)
                if c >= 1:
                    act.wait_ge(S("taps"), c)
                    A(ce[:, (c - 1) % 2, :], cv[:, (c - 1) % 2, :], ACT.Exp, scale=-1.0).then_inc(S("conv_exp"), 1)
            act.wait_ge(S("dt_abs"), 1)
            link(act, A(rows[0:SH, 0, :], rows[0:SH, 0, :], ACT.Exp, scale=-1.0), step)
            A(rows[0:SH, 0, :], rows[0:SH, 0, :], ACT.Ln, bias=1.0).then_inc(S("dt_ln"), 1)
            act.wait_ge(S("dt_gap"), 1)
            A(rows[0:SH, 2, :], rows[0:SH, 2, :], ACT.Exp).then_inc(S("dt_w"), 1)
            A(small[0:SH, 24:36], small[0:SH, 24:36], ACT.Exp).then_inc(S("dt_w"), 1)
            for t in range(4):
                A(mix[:, 4 + t, :], zT[:, t, :], ACT.Exp, scale=-1.0).then_inc(S("z_exp"), 1)
            for m in range(5):
                n = P if m < MT else TS
                act.wait_ge(S("btk_ps"), m + 1)
                if m == 0:
                    act.wait_ge(S("out_stored"), 16 * 7)
                A(btk[0:n, m, :], bk[2 + m % 2][0:n, 0:256], ACT.Copy).then_inc(S("btk_a"), 1)
            for g in range(GR):
                act.wait_ge(S("cb_ps"), g + 1)
                A(cbT[:, g, 0:TP], bk[4 + g][:, :], ACT.Copy).then_inc(S("cb_sb"), 1)
            act.wait_ge(S("cb_ps"), 3)
            A(cbT[0:TS, :, TP:T], bk[6][0:TS, 0:2 * TS].rearrange("p (g t) -> p g t", g=2), ACT.Copy)\
                .then_inc(S("cb_sb"), 1)
            act.wait_ge(S("att_n"), H)
            for b in range(NB):
                act.wait_ge(S("h0t_ps"), b + 1)
                A(h0T[:, b, :, :].rearrange("p t q -> p (t q)"), bk[b % 2][:, :], ACT.Copy).then_inc(S("h0t_sb"), 1)
            for h in range(SH):
                act.wait_ge(S("seg"), 5 * (h + 1))
                if h >= 2:
                    act.wait_ge(S("y_ps"), h - 1)
                step.up(A(ceb[:, h % 2, 0:TP], bk[h % 2][:, :], ACT.Exp))
                A(ceb[:, h % 2, TP:T], bk[2 + h % 2][:, 0:TS], ACT.Exp).then_inc(S("cexp"), 1)
                step.up(A(lg[:, h % 2, 0:TP], lg[:, h % 2, 0:TP], ACT.Exp))
                A(lg[0:TS, h % 2, TP:T], lg[0:TS, h % 2, TP:T], ACT.Exp).then_inc(S("lexp"), 1)
            for t in range(4):
                act.wait_ge(S("y_gated"), t + 1)
                act.wait_ge(S("y_ps"), SH)
                A(hT[:, t, :], mix[:, 4 + t, :], ACT.Square).then_inc(S("ssd_sq"), 1)
            for g in range(GR):
                act.wait_ge(S("ssd_ss"), g + 1)
                r = hT[:, 4 + g, :]
                link(act, A(r[:, 0:TP], bk[2 * g][:, :], ACT.Ln, scale=1.0 / 256, bias=cst_eps), step)
                link(act, A(r[:, TP:T], bk[2 * g + 1][:, 0:TS], ACT.Ln, scale=1.0 / 256, bias=cst_eps), step)
                A(r, r, ACT.Exp, scale=-0.5).then_inc(S("ssd_r"), 1)
            act.wait_ge(S("dec_start"), 1)
            act.wait_ge(S("ssd_r"), 2)
            A(small[:, 50:51], cst_eps, ACT.Copy).then_inc(S("dec_start_a"), 1)

            def copy_page(it, page, i=None):
                if page % IP < IP - 1:
                    act.wait_ge(S("kt_ps"), it * (IP - 1) + (page // IP * (IP - 1) + page % IP + 1))
                elif i is None:
                    act.wait_ge(S("ring_used"), I_DEC + page // IP + 1)
                else:
                    act.wait_ge(S("ring_used"), i * 16 + (I_LOOP + BODY.index(f"K{page // IP}") + 1))
                A(kts[:, page % 2, :], bk[page % 2][:, :], ACT.Copy).then_inc(S("kt_sb"), 1)

            def softmax_exp(i):
                act.wait_ge(S("sub_done"), i + 1)
                A(pr, sc, ACT.Exp).then_inc(S("exp_done"), 1)

            for page in range(PAGES):
                copy_page(0, page)
            with act.Fori(0, NB - 1) as i:
                for page in range(PAGES):
                    copy_page((i + 1) * 8, page, i)
                    if page == 7:
                        softmax_exp(i)
            softmax_exp(NB - 1)
            act.wait_ge(S("od_ready"), 1)
            A(hT[:, 0, 0:H * TS].rearrange("p (h t) -> p h t", h=H), mix[:, 0:H, TP:T], ACT.Square).then_inc(S("od_sq"), 1)
            act.wait_ge(S("od_ss"), 1)
            link(act, A(hT[:, 1, 0:H * TS], bk[4][:, 0:H * TS], ACT.Ln, scale=1.0 / VD, bias=cst_eps), step)
            A(hT[:, 1, 0:H * TS], hT[:, 1, 0:H * TS], ACT.Exp, scale=-0.5).then_inc(S("od_r"), 1)

            take_x(1)
            act.wait_ge(S("x1_ready"), 1)
            norm(1)
            modulate(1, g2, 24)
            act.wait_ge(S("h_sample"), 2)
            A(small[:, 50:51], cst_eps, ACT.Copy).then_inc(S("up_act"), 1)
            A(small[:, 51:52], cst_eps, ACT.Copy).then_inc(S("up_act"), 1)
            with act.Fori(0, 4) as i:
                for x in range(8):
                    if x % 2 == 0:
                        act.wait_ge(S("up_ps"), i * 4 + (x // 2 + 1))
                    else:
                        act.wait_ge(S("ring_used"), i * 4 + (I_UP + x // 2 + 1))
                    tile = u[:, bass.ds(i * 8 + x, 1), :].rearrange("p a t -> p (a t)")
                    step.up(A(tile[:, 0:TP], bk[2 * (x % 2)][:, :], ACT.Relu))
                    A(tile[:, TP:T], bk[2 * (x % 2) + 1][:, 0:TS], ACT.Relu).then_inc(S("up_act"), 1)
            step.n += 3 * 8
            act.wait_ge(S("x2_ready"), 1)
            norm(2)
            for f in range(KT):
                act.wait_ge(S("xn"), KT * 2 + f + 1)
                A(hT[:, f, :], hT[:, f, :], ACT.Copy, scale=cols[:, C_GFIN + f:C_GFIN + f + 1])\
                    .then_inc(S("h_prompt"), 1)
            for m in range(5):
                n = P if m < MT else TS
                act.wait_ge(S("yt_ps"), 2 * m + 1)
                if m >= 2:
                    act.wait_ge(S(f"y_stored{m % 2}"), 16 * (m // 2))
                A(ytok[0:n, m % 2, 0:TP], bk[(2 * m) % 4][0:n, :], ACT.Copy).then_inc(S("yt_a"), 1)

        @block.vector
        def _(v):
            step = Tally(S("dve_step"))

            def L(ins):
                link(v, ins, step)

            def bc(ap, shape):
                return ap.to_broadcast(shape)

            L(v.memset(small[:, 63:64], EPS))
            v.memset(small[:, 62:63], 0.0).then_inc(S("eps_ready"), 1)
            v.wait_ge(S("params_loaded"), 16 * N_PAR)
            v.wait_ge(S("cols_ps"), 1)
            v.tensor_copy(cols[:, :], bk[4][:, 0:NROW]).then_inc(S("cols_ready"), 1)
            v.wait_ge(S("cols_ready"), 1)
            v.wait_ge(S("silu_exp"), 1)
            L(v.tensor_scalar(ctmp[0:9, :], ctmp[0:9, :], 1.0, None, ALU.add))
            L(v.reciprocal(ctmp[0:9, :], ctmp[0:9, :]))
            v.tensor_tensor(ctmp[0:9, :], ctmp[0:9, :], crow[0:9, :], ALU.mult).then_inc(S("silu_rows"), 1)
            v.wait_ge(S("alog_exp"), 1)
            L(v.tensor_scalar(small[0:SH, 16:17], small[0:SH, 16:17], -1.0, None, ALU.mult))
            v.tensor_tensor(small[0:HD, 12:14], small[0:HD, 0:2], small[0:HD, 2:4], ALU.mult)\
                .then_inc(S("lam_prod"), 1)

            def take_x(k):
                for m in range(5):
                    n = P if m < MT else TS
                    w = 2 * m + 1
                    v.wait_ge(S("xt_ps"), 10 * k + w + 1)
                    v.tensor_copy(xT[:, 4:8, m * P:m * P + n],
                                  bk[w % 4][:, :].rearrange("p (k c) -> p k c", k=4)[:, :, 0:n]).then_inc(S("xt_v"), 1)

            take_x(0)
            v.wait_ge(S("ct_ps"), 1)
            v.tensor_copy(cT[:, :, :], bk[5][:, 0:72].rearrange("p (k c) -> p k c", k=KT)).then_inc(S("ct_ready"), 1)
            v.wait_ge(S("lam_exp"), 1)
            L(v.tensor_copy(small[:, 20:24], bk[6][:, 4:8]))
            L(v.tensor_tensor(small[:, 17:18], small[:, 19:20], small[:, 18:19], ALU.subtract))
            v.tensor_scalar(small[:, 17:18], small[:, 17:18], -0.2, None, ALU.add).then_inc(S("lam_ready"), 1)
            v.wait_ge(S("lam_ready"), 1)
            v.wait_ge(S("tables_ps"), 1)
            L(v.tensor_copy(brow[0:H, 0, :], bk[6][0:H, 0:TAB]))
            v.tensor_copy(brow[0:H, 1, :], bk[7][0:H, 0:TAB]).then_inc(S("tables_ready"), 1)
            v.wait_ge(S("cs_ps"), 1)
            v.wait_ge(S("xp_zero"), 1)
            pre = xp[:, :, 3 + TP:XPW].rearrange("p c (b w) -> p c b w", w=DT + 3)[:, :, :, 0:3]
            for c in range(8):
                ins = v.tensor_copy(pre[:, c], bk[6][:, c * 24:(c + 1) * 24].rearrange("p (b w) -> p b w", b=NB))
                if c < 7:
                    L(ins)
            ins.then_inc(S("prefix_ready"), 1)
            v.wait_ge(S("prefix_ready"), 1)

            v.wait_ge(S("xt_a"), 5)
            v.memset(small[:, 61:62], 0.0).then_inc(S("x_free"), 1)

            def norm(k):
                v.wait_ge(S("rstd"), k + 1)
                for f in range(KT):
                    v.tensor_tensor(hT[:, f, :], xT[:, f, :], rs[:, :], ALU.mult).then_inc(S("xn"), 1)

            def modulate(k, g, sh):
                v.wait_ge(S("xn"), KT * (k + 1))
                for f in range(KT):
                    hs = hT[:, f, TP:T].rearrange("p (b t) -> p b t", b=NB)
                    step.up(v.tensor_tensor(hs, hs, bc(g[:, f, 1:9].unsqueeze(2), [P, NB, DT]), ALU.mult))
                v.wait_ge(step.sem, step.n)
                for f in range(KT):
                    hs = hT[:, f, TP:T].rearrange("p (b t) -> p b t", b=NB)
                    ins = v.tensor_tensor(hs, hs, bc(mod[:, sh + f, 1:9].unsqueeze(2), [P, NB, DT]), ALU.add)
                    if f < KT - 1:
                        step.up(ins)
                ins.then_inc(S("h_sample"), 1)

            def take_mod(bank, t0, nt):
                L(v.tensor_tensor(mod[:, t0:t0 + nt, :], bank[:, 0:nt * 9].rearrange("p (t c) -> p t c", c=9),
                                  bc(cols[:, C_BADA + t0:C_BADA + t0 + nt].unsqueeze(2), [P, nt, 9]), ALU.add))

            def gain(g, t0, c0):
                L(v.tensor_scalar(g[:, :, :], mod[:, t0:t0 + KT, :], 1.0, None, ALU.add))
                return v.tensor_tensor(g[:, :, :], g[:, :, :], bc(cols[:, c0:c0 + KT].unsqueeze(2), [P, KT, 9]),
                                       ALU.mult)

            v.wait_ge(S("ring_used"), N_ADA1)
            take_mod(bk[4], 0, 16)
            gain(g1, 8, C_GMIX).then_inc(S("mod1"), 1)
            v.wait_ge(S("mod1"), 1)
            norm(0)
            modulate(0, g1, 0)

            v.wait_ge(S("qbd_zero"), 1)
            for n, (kind, t) in enumerate(tiles):
                if kind == "v":
                    continue
                bs = bk[2 * (n % 2) + 1]
                sign, count = tile_sign[n]
                v.wait_ge(S(sign), count)
                sv = bs[:, 0:TS].rearrange("p (b t) -> p b t", b=NB)
                if kind == "q":
                    L(v.tensor_scalar(qbd[0:64, :, t, 0, :], sv[0:64], HD ** -0.5, None, ALU.mult))
                    ins = v.tensor_scalar(qbd[64:128, :, t, 1, :], sv[64:128], HD ** -0.5, None, ALU.mult)
                elif kind == "k":
                    ins = v.tensor_copy(kT[:, t, TP:T], bs[:, 0:TS])
                elif kind == "d":
                    ins = v.tensor_scalar(rs[0:SH, TP:T], bs[0:SH, 0:TS], small[0:SH, 4:5], None, ALU.add)
                elif kind == "z":
                    ins = v.tensor_copy(zT[:, t, TP:T], bs[:, 0:TS])
                else:
                    ins = v.tensor_copy(seg(xp[:, t, :], 3)[1], sv)
                ins.then_inc(S("ip_dve"), 1)
            v.wait_ge(S("ip_dve"), by_dve[-1])
            v.wait_ge(S("ip_act"), len(tiles))

            v.wait_ge(S("ring_used"), I_DEC)
            take_mod(bk[5], 16, 32)
            L(gain(g2, 32, C_GFFN))

            for m in range(5):
                n = P if m < MT else TS
                v.wait_ge(S("kout_ps"), m + 1)
                if m >= 2:
                    v.wait_ge(S(f"kout_stored{m % 2}"), 16 * (m // 2))
                v.tensor_copy(kout[0:n, m % 2, :], bk[m % 2][0:n, :]).then_inc(S("kout_ready"), 1)

            v.wait_ge(S("bias_loaded"), 16 * (2 + NB))
            L(v.tensor_copy(wb, wrev[:, :, ::-1]))
            L(v.tensor_copy(p31x[:, :].rearrange("p (h j t) -> p h j t", h=H, j=2)[:, :, 0, :], p31r[:, :, ::-1]))
            L(v.tensor_copy(p31x[:, :].rearrange("p (h j t) -> p h j t", h=H, j=2)[:, :, 1, :], p31r[:, :, ::-1]))
            for b in range(NB):
                for j in range(2):
                    dst = newb[0:TS, b, :].rearrange("p (h j t) -> p h j t", h=H, j=2)[:, :, j, :]
                    mask = cst[0:TS, K_NMS + b * DT:K_NMS + (b + 1) * DT]
                    step.up(v.tensor_tensor(dst, newr[0:TS, :, ::-1], bc(mask.unsqueeze(1), [TS, H, DT]), ALU.add))
            v.wait_ge(step.sem, step.n)

            NU = 16

            def att_max(x):
                h, qb = x // MT, x % MT
                nk = (qb + 1) * P
                nb_ = min(2 * P, nk)
                v.wait_ge(S("att_s"), x + 1)
                for j in range(2):
                    s = bk[2 + 2 * (x % 2) + j]
                    near = s[:, nk - nb_:nk]
                    step.up(v.tensor_tensor(near, near, wb[:, h, 2 * P - nb_:2 * P], ALU.add))
                v.wait_ge(step.sem, step.n)
                for j in range(2):
                    s = bk[2 + 2 * (x % 2) + j]
                    m_ = small[:, 36 + 2 * (x % 2) + j:37 + 2 * (x % 2) + j]
                    L(v.tensor_reduce(m_, s[:, 0:nk], AX, ALU.max))
                    v.tensor_scalar(m_, m_, -1.0, None, ALU.mult).then_inc(S("att_m"), 1)

            def att_combine(x):
                nk = (x % MT + 1) * P
                v.wait_ge(S("att_exp"), 2 * x + 2)
                r = small[:, 44 + 2 * (x % 2):46 + 2 * (x % 2)]
                L(v.reciprocal(r, small[:, 40 + 2 * (x % 2):42 + 2 * (x % 2)]))
                L(v.tensor_tensor(r[:, 1:2], r[:, 1:2], small[:, 17:18], ALU.mult))
                p0, p1 = pj[:, x % 2, 0, 0:nk], pj[:, x % 2, 1, 0:nk]
                L(v.tensor_scalar(p0, p0, r[:, 0:1], None, ALU.mult))
                v.scalar_tensor_tensor(p0, p1, r[:, 1:2], p0, ALU.mult, ALU.add).then_inc(S("att_p"), 1)

            def att_out(h):
                v.wait_ge(S("att_v"), MT * (h + 1))
                v.tensor_copy(mix[:, h, 0:TP], bk[h % 2][:, :]).then_inc(S("att_o"), 1)

            for x in range(NU + 3):
                if x < NU:
                    att_max(x)
                if 1 <= x <= NU:
                    att_combine(x - 1)
                if x >= 6 and (x - 6) % 4 == 0:
                    att_out((x - 6) // 4)
            v.wait_ge(S("att_o"), 4)
            for h in range(H):
                v.wait_ge(S("att_r"), h + 1)
                L(v.tensor_tensor(mix[:, h, 0:TP], mix[:, h, 0:TP], hT[:, 4 + h, 0:TP], ALU.mult))
                v.tensor_scalar(mix[:, h, 0:TP], mix[:, h, 0:TP], cols[:, C_SUB:C_SUB + 1], 0.8, ALU.mult, ALU.mult)\
                    .then_inc(S("att_n"), 1)
            v.wait_ge(S("att_n"), H)

            last = xp[:, :, TP:3 + TP]
            L(v.tensor_copy(gc[:, :, 0:3], last))
            for c in range(8):
                ins = v.tensor_copy(gc[:, c, 3:27].rearrange("p (b w) -> p b w", b=NB),
                                    xp[:, c, 3 + TP:XPW].rearrange("p (b w) -> p b w", w=DT + 3)[:, :, DT:DT + 3])
                if c < 7:
                    step.up(ins)
            ins.then_inc(S("ends_ready"), 1)
            v.wait_ge(S("conv_ps"), 1)
            L(v.tensor_copy(sout[0:27, 0:512], bk[0][0:27, :]))
            v.tensor_copy(sout[0:27, 512:1024], bk[1][0:27, :]).then_inc(S("conv_rows"), 1)
            for c in range(8):
                v.wait_ge(S("tap0"), 2 * c + 2)
                cp, cs = cv[:, c % 2, 0:TP], cv[:, c % 2, TP:T].rearrange("p (b t) -> p b t", b=NB)
                for s in range(1, 4):
                    pp, ss = seg(xp[:, c, :], s)
                    w = cols[:, C_CW + 8 * s + c:C_CW + 8 * s + c + 1]
                    step.up(v.scalar_tensor_tensor(cp, pp, w, cp, ALU.mult, ALU.add))
                    ins = v.scalar_tensor_tensor(cs, ss, w, cs, ALU.mult, ALU.add)
                    if s < 3:
                        L(ins)
                ins.then_inc(S("taps"), 1)
                v.wait_ge(S("taps"), c + 1)
                v.wait_ge(step.sem, step.n)
                v.wait_ge(S("conv_exp"), c + 1)
                e = ce[:, c % 2, :]
                L(v.tensor_scalar(e, e, 1.0, None, ALU.add))
                L(v.reciprocal(e, e))
                v.tensor_tensor(xp[:, c, 0:T], cv[:, c % 2, :], e, ALU.mult).then_inc(S("xa_ready"), 1)
            dt, cs, dw = (rows[0:SH, r, :] for r in range(3))
            raw = dA = rs[0:SH, :]
            L(v.tensor_scalar(dt, raw, -1.0, None, ALU.mult))
            v.tensor_tensor(dt, dt, raw, ALU.max).then_inc(S("dt_abs"), 1)
            v.wait_ge(S("dt_ln"), 1)
            L(v.scalar_tensor_tensor(dt, raw, 0.0, dt, ALU.max, ALU.add))
            L(v.tensor_scalar(dA, dt, small[0:SH, 16:17], None, ALU.mult))
            L(v.tensor_tensor_scan(cs, dw, dA, 0.0, ALU.mult, ALU.add))
            csp, css = cs[:, 0:TP].rearrange("p (c t) -> p c t", c=MT), cs[:, TP:T].rearrange("p (c t) -> p c t", c=NB)
            dwp, dws = dw[:, 0:TP].rearrange("p (c t) -> p c t", c=MT), dw[:, TP:T].rearrange("p (c t) -> p c t", c=NB)
            L(v.tensor_tensor(dwp, bc(csp[:, :, P - 1:P], [SH, MT, P]), csp, ALU.subtract))
            L(v.tensor_tensor(dws, bc(css[:, :, DT - 1:DT], [SH, NB, DT]), css, ALU.subtract))
            L(v.tensor_copy(small[0:SH, 24:28].unsqueeze(2), csp[:, :, P - 1:P]))
            v.tensor_copy(small[0:SH, 28:36].unsqueeze(2), css[:, :, DT - 1:DT]).then_inc(S("dt_gap"), 1)
            v.wait_ge(S("dt_w"), 2)
            v.tensor_tensor(dw, dw, dt, ALU.mult).then_inc(S("rows_ready"), 1)
            v.wait_ge(S("tok_ps"), 1)
            L(v.tensor_copy(tok[:, 0:MT, :, :], bk[6][:, 0:MT * 24].rearrange("p (m r h) -> p m r h", m=MT, r=3)))
            L(v.tensor_copy(tok[0:TS, MT, :, :], bk[6][0:TS, MT * 24:5 * 24].rearrange("p (r h) -> p r h", r=3)))
            v.wait_ge(S("dec_ps"), 1)
            v.tensor_copy(dec[:, :, :], bk[7][:, 0:96].rearrange("p (h c) -> p h c", h=SH)).then_inc(S("dec_sb"), 1)
            v.wait_ge(S("dec_sb"), 1)
            for t in range(4):
                v.wait_ge(S("z_exp"), t + 1)
                e = mix[:, 4 + t, :]
                L(v.tensor_scalar(e, e, 1.0, None, ALU.add))
                L(v.reciprocal(e, e))
                L(v.tensor_tensor(zT[:, t, :], zT[:, t, :], e, ALU.mult))
            v.wait_ge(S("xa_ready"), 8)
            for m in range(5):
                n = P if m < MT else TS
                v.wait_ge(S("xtk_ps"), m + 1)
                src = bk[m % 2][0:n, :].rearrange("p (h q) -> p h q", h=SH)
                L(v.tensor_tensor(xdt[0:n, m, :].rearrange("p (h q) -> p h q", h=SH), src,
                                  bc(tok[0:n, m, 0, :].unsqueeze(2), [n, SH, SP_]), ALU.mult))
                dst = xw[0:n, m, :] if m < MT else xws[:, :]
                v.tensor_tensor(dst.rearrange("p (h q) -> p h q", h=SH), src,
                                bc(tok[0:n, m, 2, :].unsqueeze(2), [n, SH, SP_]), ALU.mult).then_inc(S("xtk_v"), 1)
            v.wait_ge(S("xtk_v"), 5)
            v.wait_ge(S("st_ps"), 1)
            L(v.tensor_copy(prev[:, 0, :], bk[0][:, :]))
            for c in range(1, MT):
                v.wait_ge(S("st_ps"), c + 1)
                L(v.tensor_tensor(prev[:, c, :].rearrange("p (h q) -> p h q", h=SH),
                                  prev[:, c - 1, :].rearrange("p (h q) -> p h q", h=SH),
                                  bc(dec[:, :, c:c + 1], [P, SH, SP_]), ALU.mult))
                ins = v.tensor_tensor(prev[:, c, :], prev[:, c, :], bk[c][:, :], ALU.add)
                if c < MT - 1:
                    L(ins)
            ins.then_inc(S("prev_done"), 1)

            v.wait_ge(S("prev_done"), 1)
            v.wait_ge(S("final_ps"), 1)
            v.tensor_copy(rs[:, 0:512], bk[3][:, :]).then_inc(S("final_ready"), 1)
            for h in range(SH + 2):
                if h < SH:
                    v.wait_ge(S("cs_bc"), h + 1)
                    if h >= 2:
                        v.wait_ge(S("y_ps"), h - 1)
                    for c in range(MT):
                        v.scalar_tensor_tensor(lg[:, h % 2, c * P:(c + 1) * P], bk[h % 2][:, c * P:(c + 1) * P],
                                               tok[:, c, 1, h:h + 1], cst[:, K_NM:K_NM + P], ALU.subtract, ALU.add)\
                            .then_inc(S("seg"), 1)
                    v.scalar_tensor_tensor(lg[0:TS, h % 2, TP:T], bk[2 + h % 2][0:TS, 0:TS], tok[0:TS, MT, 1, h:h + 1],
                                           cst[0:TS, K_NMS:K_NMS + TS], ALU.subtract, ALU.add).then_inc(S("seg"), 1)
                if 1 <= h <= SH:
                    k, g = h - 1, (h - 1) // 4
                    v.wait_ge(S("cb_sb"), 3)
                    v.wait_ge(S("lexp"), k + 1)
                    step.up(v.tensor_tensor(lg[:, k % 2, 0:TP], lg[:, k % 2, 0:TP], cbT[:, g, 0:TP], ALU.mult))
                    step.up(v.tensor_tensor(lg[0:TS, k % 2, TP:T], lg[0:TS, k % 2, TP:T], cbT[0:TS, g, TP:T], ALU.mult))
                    v.tensor_tensor(ceb[:, k % 2, :], ceb[:, k % 2, :], xp[:, 6 + g, 0:T], ALU.mult)\
                        .then_inc(S("g_ready"), 1)
                if h >= 2 and h % 2 == 1:
                    t = (h - 2) // 2
                    v.wait_ge(S("y_ps"), 2 * t + 2)
                    skip = small[:, 20 + t:21 + t]
                    L(v.scalar_tensor_tensor(mix[:, 4 + t, 0:TP], xp[:, t, 0:TP], skip, bk[4 + t % 2][:, :],
                                             ALU.mult, ALU.add))
                    v.scalar_tensor_tensor(mix[:, 4 + t, TP:T], xp[:, t, TP:T], skip, bk[6 + t % 2][:, 0:TS],
                                           ALU.mult, ALU.add).then_inc(S("y_sb"), 1)
                    v.wait_ge(S("y_sb"), t + 1)
                    v.tensor_tensor(mix[:, 4 + t, :], mix[:, 4 + t, :], zT[:, t, :], ALU.mult)\
                        .then_inc(S("y_gated"), 1)
            v.wait_ge(S("y_gated"), 4)
            v.wait_ge(step.sem, step.n)
            for g in range(GR):
                ins = v.tensor_tensor(bblk[0:TS, g, :, :], bc(btk[0:TS, MT, g * NS:(g + 1) * NS].unsqueeze(1), [TS, NB, NS]),
                                      bc(cst[0:TS, K_BLK:K_BLK + NB].unsqueeze(2), [TS, NB, NS]), ALU.mult)
                if g == 0:
                    L(ins)
            ins.then_inc(S("bblk_ready"), 1)
            for r in range(2):
                half = slice(64 * r, 64 * r + 64)
                L(v.tensor_copy(hdec[half, :, :], dec[half, r:SH:2, MT:MT + NB]))
            for t in range(4):
                for q in range(2):
                    v.wait_ge(S("ssm_ps"), 2 * t + q + 1)
                    for j in range(4):
                        b = 4 * q + j
                        ins = v.scalar_tensor_tensor(h0[:, b, t, :], h0[:, b, t, :], hdec[:, t, b:b + 1],
                                                     bk[4 + q][:, j * NS:(j + 1) * NS], ALU.mult, ALU.add)
                        if j < 3:
                            step.up(ins)
                    ins.then_inc(S("ssm_sb"), 1)
            v.wait_ge(step.sem, step.n)
            v.wait_ge(S("ssm_sb"), 8)
            v.memset(small[:, 61:62], 0.0).then_inc(S("ssm_ready"), 1)
            for g in range(GR):
                v.wait_ge(S("ssd_r"), g + 1)
                for t in (2 * g, 2 * g + 1):
                    L(v.scalar_tensor_tensor(mix[:, 4 + t, :], mix[:, 4 + t, :], cols[:, C_SSD + t:C_SSD + t + 1],
                                             hT[:, 4 + g, :], ALU.mult, ALU.mult))

            L(v.memset(sc[:, PAGES, :], BIG))
            L(v.memset(mxp, 0.0))
            v.memset(small[:, 61:62], 0.0).then_inc(S("o_free"), 1)
            v.wait_ge(S("o_free"), 1)
            v.memset(small[:, 61:62], 0.0).then_inc(S("dec_start"), 1)
            chain = Tally(S("dec_step"))

            def take_scores(u, n):
                v.wait_ge(S("s_ps"), n + (u + 1))
                bank = bk[2 + u % 2]
                if u < 3:
                    v.tensor_copy(sc[:, 8 * u:8 * u + 8, :].rearrange("p n c -> p (n c)"), bank[:, :])\
                        .then_inc(S("s_sb"), 1)
                else:
                    link(v, v.tensor_tensor(sc[:, PAGES - 1, :], bank[:, 448:512], p31x[:, :], ALU.add), chain)
                    v.tensor_copy(sc[:, 24:31, :].rearrange("p n c -> p (n c)"), bank[:, 0:448]).then_inc(S("s_sb"), 1)

            def take_new(b, n):
                v.wait_ge(S("new_ps"), n + 1)
                v.tensor_tensor(sc[0:TS, PAGES, :], bk[4][0:TS, 0:64],
                                newb[0:TS, bass.ds(b, 1), :].rearrange("p a c -> p (a c)"), ALU.add)\
                    .then_inc(S("new_sb"), 1)

            def softmax(i):
                v.wait_ge(S("new_sb"), i + 1)
                v.wait_ge(S("s_sb"), i * 4 + 4)
                v.tensor_reduce(mxp[:, 0:64], sc.rearrange("p n c -> p c n"), AX, ALU.max).then_inc(S("mx_ready"), 1)
                v.wait_ge(S("mxt_ps"), i + 1)
                link(v, v.tensor_reduce(mrow[0:64, :], bk[4][0:64, 0:P], AX, ALU.max), chain)
                v.tensor_scalar(mdg[0:64, :], ident[0:64, 0:64], mrow[0:64, 0:1], None, ALU.mult)\
                    .then_inc(S("mdg_ready"), 1)
                v.wait_ge(S("mbc_ps"), i + 1)
                v.tensor_tensor(sc, sc, bc(bk[4][:, 0:64].unsqueeze(1), [P, NBLK, 64]), ALU.subtract)\
                    .then_inc(S("sub_done"), 1)
                v.wait_ge(S("exp_done"), i + 1)
                v.tensor_reduce(lsum, pr.rearrange("p n c -> p c n"), AX, ALU.add).then_inc(S("lsum_ready"), 1)

            def inverse(i):
                v.wait_ge(S("lbc_ps"), i + 1)
                v.reciprocal(rl, bk[4][:, 0:64]).then_inc(S("rl_ready"), 1)

            def finish(i, b):
                v.wait_ge(S("o_ps"), i + 1)
                v.wait_ge(S("rl_ready"), i + 1)
                v.tensor_tensor(on, bk[5][:, 0:64], rl, ALU.mult).then_inc(S("o_free"), 1)
                v.wait_ge(S("o_free"), i + 2)
                w = on.rearrange("p (h j t) -> p h j t", h=H, j=2)
                link(v, v.scalar_tensor_tensor(mix[:, 0:H, bass.ds(TP + b * DT, DT)], w[:, :, 1, :], small[:, 17:18],
                                               w[:, :, 0, :], ALU.mult, ALU.add), chain)

            for u_ in range(4):
                take_scores(u_, 0)
            take_new(0, 0)
            base = chain.n
            with v.Fori(0, NB - 1) as i:
                chain.n = i * 3 + base
                softmax(i)
                take_scores(0, i * 4 + 4)
                inverse(i)
                for u_ in range(1, 4):
                    take_scores(u_, i * 4 + 4)
                take_new(i + 1, i + 1)
                finish(i, i)
            chain.n = base + 3 * (NB - 1)
            softmax(NB - 1)
            inverse(NB - 1)
            finish(NB - 1, NB - 1)
            v.memset(small[:, 61:62], 0.0).then_inc(S("od_ready"), 1)
            v.wait_ge(S("ssm_stored"), 16 * NB)
            v.wait_ge(S("od_r"), 1)
            r4 = hT[:, 1, 0:H * TS].rearrange("p (h t) -> p h t", h=H)
            L(v.tensor_tensor(mix[:, 0:H, TP:T], mix[:, 0:H, TP:T], r4, ALU.mult))
            v.tensor_scalar(mix[:, 0:H, TP:T], mix[:, 0:H, TP:T], cols[:, C_SUB:C_SUB + 1], 0.8, ALU.mult, ALU.mult)\
                .then_inc(S("mix_ready"), 1)
            take_x(1)
            v.wait_ge(S("xt_a"), 10)
            v.wait_ge(S("xt_v"), 10)

            for x in range(KT):
                if x % 2 == 0:
                    v.wait_ge(S("op_ps"), x // 2 + 1)
                else:
                    v.wait_ge(S("ring_used"), I_OUT + x // 2 + 1)
                bp, bs = bk[2 * (x % 2)], bk[2 * (x % 2) + 1]
                ga = mod[:, 16 + x, :]
                xs = xT[:, x, TP:T].rearrange("p (b t) -> p b t", b=NB)
                step.up(v.scalar_tensor_tensor(xT[:, x, 0:TP], bp[:, :], ga[:, 0:1], xT[:, x, 0:TP], ALU.mult, ALU.add))
                g8 = rs[:, 0:TS].rearrange("p (b t) -> p b t", b=NB)
                L(v.tensor_tensor(g8, bs[:, 0:TS].rearrange("p (b t) -> p b t", b=NB),
                                  bc(ga[:, 1:9].unsqueeze(2), [P, NB, DT]), ALU.mult))
                v.tensor_tensor(xs, xs, g8, ALU.add).then_inc(S("op_sb"), 1)
                v.wait_ge(S("op_sb"), x + 1)
            v.memset(small[:, 61:62], 0.0).then_inc(S("x1_ready"), 1)
            norm(1)
            modulate(1, g2, 24)
            v.wait_ge(S("up_act"), 2)
            with v.Fori(0, 4) as i:
                for x in range(8):
                    v.wait_ge(S("up_act"), i * 8 + (x + 3))
                    tile = u[:, bass.ds(i * 8 + x, 1), :].rearrange("p a t -> p (a t)")
                    v.tensor_tensor(tile, tile, tile, ALU.mult).then_inc(S("u_ready"), 1)
            v.wait_ge(S("u_ready"), NF)
            L(v.memset(small[:, 61:62], 0.0))
            v.memset(small[:, 61:62], 0.0).then_inc(S("down_sb"), 1)
            v.wait_ge(S("down_sb"), 1)
            v.memset(small[:, 61:62], 0.0).then_inc(S("down_sb"), 1)
            down = Tally(S("down_step"))
            with v.Fori(0, 4) as i:
                down.n = i * 4
                for t in range(2):
                    if t == 0:
                        v.wait_ge(S("down_ps"), i + 1)
                    else:
                        v.wait_ge(S("ring_used"), i * 4 + (I_DOWN + 4))
                    bp, bs = bk[2 * t], bk[2 * t + 1]
                    tile = xT[:, bass.ds(i * 2 + t, 1), :].rearrange("p a t -> p (a t)")
                    ga = mod[:, bass.ds(i * 2 + (40 + t), 1), :].rearrange("p a c -> p (a c)")
                    down.up(v.scalar_tensor_tensor(tile[:, 0:TP], bp[:, :], ga[:, 0:1], tile[:, 0:TP], ALU.mult, ALU.add))
                    g8 = rs[:, t * TS:(t + 1) * TS].rearrange("p (b t) -> p b t", b=NB)
                    link(v, v.tensor_tensor(g8, bs[:, 0:TS].rearrange("p (b t) -> p b t", b=NB),
                                            bc(ga[:, 1:9].unsqueeze(2), [P, NB, DT]), ALU.mult), down)
                    xs = tile[:, TP:T].rearrange("p (b t) -> p b t", b=NB)
                    v.tensor_tensor(xs, xs, g8, ALU.add).then_inc(S("down_sb"), 1)
            v.wait_ge(S("down_sb"), 10)
            v.memset(small[:, 61:62], 0.0).then_inc(S("x2_ready"), 1)
            norm(2)
            for m in range(5):
                n = P if m < MT else TS
                v.wait_ge(S("yt_ps"), 2 * m + 2)
                if m >= 2:
                    v.wait_ge(S(f"y_stored{m % 2}"), 16 * (m // 2))
                v.tensor_copy(ytok[0:n, m % 2, TP:D], bk[(2 * m + 1) % 4][0:n, :]).then_inc(S("yt_v"), 1)


N_PAR = 22
N_POOL = 320


def shape_constants():
    import numpy as np

    c = np.zeros((P, K_N), np.float32)
    c[:, K_ID:K_ID + P] = np.eye(P)
    c[:, K_ONE:K_ONE + P] = 1
    s, l = np.meshgrid(np.arange(P), np.arange(P), indexing="ij")
    c[:, K_NM:K_NM + P] = np.where(s <= l, 0, BIG)
    s, l = s[:TS, :TS], l[:TS, :TS]
    c[:TS, K_NMS:K_NMS + TS] = np.where((s <= l) & (s // DT == l // DT), 0, BIG)
    c[:TS, K_BLK:K_BLK + NB] = np.arange(TS)[:, None] // DT == np.arange(NB)
    d = np.arange(TAB) - OFF
    n = np.maximum(d, 0)
    lt = np.log(np.maximum(n, 1).astype(np.float32) / np.float32(16)) / np.float32(np.log(8.0)) * np.float32(16)
    bucket = np.where(n < 16, n, np.minimum(16 + lt.astype(np.int32), 31))
    hot = np.zeros((33, 2, TAB), np.float32)
    hot[:32, 0] = (np.arange(32)[:, None] == bucket).astype(np.float32)
    hot[31, 0] -= 1
    hot[:, 0, d < 0] = 0
    hot[32, 0, d < 0] = BIG
    far = 2 * P - 1 + OFF
    hot[:, 1, 0:far + 1] = hot[:, 0, far::-1]
    starts = np.ones((SH, T), np.float32)
    starts[:, 0:TP:P] = 0
    starts[:, TP:T:DT] = 0
    return c, hot, starts


_OUTS = [("y_p", (TP, D)), ("y_s", (TS, D)), ("k_p", (TP, 512)), ("v_p", (TP, 512)), ("conv_p", (3, CONV)),
         ("ssm_p", (512, NS)), ("k_s", (TS, 512)), ("v_s", (TS, 512)), ("conv_s", (NB * 3, CONV)),
         ("ssm_s", (NB * 512, NS))]
_SHAPES = [(1, TP, D), (NB, DT, D), (1, 1, TP, H, 2, HD), (1, 1, TP, H, VD), (1, 1, 3, CONV), (1, 1, SH, SP_, NS),
           (1, NB, DT, H, 2, HD), (1, NB, DT, H, VD), (1, NB, 3, CONV), (1, NB, SH, SP_, NS)]


def kernel(**inputs):
    import concourse.bacc as _bacc
    import numpy as _np
    from concourse.bass_utils import run_bass_kernel_spmd as _run

    nc = _bacc.Bacc("TRN2", target_bir_lowering=False, num_devices=1)
    arrays = {k: _np.ascontiguousarray(v) for k, v in inputs.items()}
    arrays["cache_k"] = arrays["cache_k"].reshape(N_POOL, PAGE, 512)
    arrays["cache_v"] = arrays["cache_v"].reshape(N_POOL, PAGE, 512)
    arrays["shape_consts"], arrays["shape_hot"], arrays["shape_starts"] = shape_constants()
    arrays = {f"in_{k}": v for k, v in arrays.items()}
    a = {k[3:]: nc.dram_tensor(k, v.shape, mybir.dt.from_np(v.dtype), kind="ExternalInput").ap()
         for k, v in arrays.items()}
    o = {k: nc.dram_tensor(f"out_{k}", s, F32, kind="ExternalOutput").ap() for k, s in _OUTS}
    scratch = nc.dram_tensor("bias_tables", (2, H, TAB), F32, kind="Internal").ap()
    program(nc, a, o, scratch)
    r = _run(nc, [arrays], core_ids=[0])
    return tuple(r.results[0][f"out_{k}"].reshape(s) for (k, _), s in zip(_OUTS, _SHAPES))
```

```python
from contextlib import ExitStack

import concourse.bass as bass
from concourse import mybir

F32 = mybir.dt.float32
I32 = mybir.dt.int32
ALU = mybir.AluOpType
ACT = mybir.ActivationFunctionType
AX = mybir.AxisListType.X
P = 128

D = 1024
KT = D // P
TP, NB, DT = 512, 8, 8
TS = NB * DT
T = TP + TS
HF = T // 2
MT = TP // P
PAGES, PAGE = 32, 128
H, HD, VD = 4, 64, 128
SH, SP_, NS, GR = 8, 64, 128, 2
CONV = SH * SP_ + 2 * GR * NS
XT_, BT_ = 4, 4
NF = 4 * D // P
TAB = 384
OFF = 127
BIG = -1.0e30
EPS = 1e-6
IT = 256
IP = 4
SLOTS = 4
SLOT = KT * IT
XPW = 3 + TP + NB * (DT + 3)

C_BADA, C_GMIX, C_GFFN, C_GFIN, C_CB, C_CW, C_SSD, C_SUB = 0, 48, 56, 64, 72, 80, 112, 116
NROW = 117
K_ID, K_ONE, K_NM, K_NMS, K_BLK = 0, P, 2 * P, 3 * P, 3 * P + TS
K_SUM = K_BLK + NB
K_N = K_SUM + 9
NBIAS = DT + PAGE


class Tally:

    def __init__(self, sem):
        self.sem, self.n = sem, 0

    def up(self, ins):
        ins.then_inc(self.sem, 1)
        self.n = self.n + 1


def link(eng, ins, tally):
    tally.up(ins)
    eng.wait_ge(tally.sem, tally.n)


def program(nc, a, o, scratch):
    ctx = ExitStack()
    with ctx:
        def sb(name, shape):
            return ctx.enter_context(nc.sbuf_tensor(name, shape, F32))

        sems = {}

        def S(name):
            if name not in sems:
                sems[name] = ctx.enter_context(nc.semaphore(name))
            return sems[name]

        ring = sb("ring", [P, SLOTS * SLOT])
        xT = sb("xT", [P, KT, T])
        hT = sb("hT", [P, KT, T])
        mix = sb("mix", [P, KT, T])
        cst = sb("cst", [P, K_N])
        cols = sb("cols", [P, NROW])
        mod = sb("mod", [P, 48, 9])
        g1 = sb("g1", [P, KT, 9])
        g2 = sb("g2", [P, KT, 9])
        rs = sb("rs", [P, T])
        cT = sb("cT", [P, KT, 9])
        small = sb("small", [P, 64])
        rows = sb("rows", [SH, 3, T])
        tok = sb("tok", [P, 5, 3, SH])
        dec = sb("dec", [P, SH, MT + NB])
        arena = sb("arena", [P, 27230])

        def at(off, *shape, parts=P):
            n = 1
            for s in shape:
                n *= s
            v = arena[0:parts, off:off + n]
            if len(shape) == 2:
                v = v.rearrange("p (a b) -> p a b", b=shape[1])
            if len(shape) == 3:
                v = v.rearrange("p (a b c) -> p a b c", b=shape[1], c=shape[2])
            if len(shape) == 4:
                v = v.rearrange("p (a b c d) -> p a b c d", b=shape[1], c=shape[2], d=shape[3])
            return v

        kT = at(0, H, T)
        vtk = at(2304, 5, H * VD)
        zT = at(4864, 4, T)
        qbd = at(7168, NB, H, 2, DT)
        newb = at(7680, NB, TS)
        xp = at(8448, 8, XPW)
        qT = at(13272, H, TP)
        TMP = 15320
        xtok = at(TMP, 5, D)
        crow = at(TMP + 5120, D)
        ctmp = at(TMP + 6144, D)
        scr = at(TMP + 7168, D)
        brow = at(TMP + 8192, 2, TAB)
        hot = at(TMP + 8960, 2, TAB)
        vrow = at(TMP + 9728, P)
        wdt = at(TMP + 9856, KT, SH)
        picks = at(TMP + 10944, 2, NB * H)
        adas = at(TMP + 9920, 2, 2 * IT)
        wrev = at(TMP, H, 2 * P)
        wb = at(TMP + 1024, H, 2 * P)
        pj = at(TMP + 2048, 2, 2, TP)
        pts = at(TMP + 4096, 2, TP)
        kout = at(TMP + 5120, 2, TP)
        adas2 = at(TMP + 6144, 8, 2 * IT)
        nearr = at(TMP + 11300, NBIAS)
        cv = at(TMP + 5120, 2, T)
        ce = at(TMP + 6272, 2, T)
        gc = at(TMP + 7424, 8, 27)
        sout = at(TMP + 10240, D)
        xdt = at(TMP, 5, SH * SP_)
        xw = at(TMP + 2560, 5, SH * SP_)
        prev = at(TMP + 5120, 4, SH * SP_)
        btk = at(TMP + 7168, 5, GR * NS)
        cbT = at(TMP + 8448, GR, T)
        lg = at(TMP + 9600, 2, T)
        ceb = at(TMP + 10752, 2, T)
        h0 = xT[:, :, :].rearrange("p a b -> p (a b)")[:, 0:4096].rearrange("p (b t q) -> p b t q", b=NB, t=4)
        h0T = hT[:, :, :].rearrange("p a b -> p (a b)")[:, 0:4096].rearrange("p (b t q) -> p b t q", b=NB, t=4)
        bblk = at(TMP + 9600, GR, NB, NS)
        xws = xw[0:TS, MT, :]
        hdec = sb("hdec", [P, 4, NB])
        NK = PAGES * PAGE
        DEC = 8448
        kts = at(DEC, 2, H, IP * PAGE)
        sc = at(DEC + 4096, NK + TS)
        pr = at(DEC + 8256, NK + TS)
        pT = at(DEC + 12416, 2, IP * P)
        qcur = at(DEC + 13440, H, 32)
        on = at(DEC + 13568, P)
        nearb = mod[:, 0:16, :].rearrange("p a b -> p (a b)")[:, 0:NBIAS]
        sel = g1[:, :, :].rearrange("p a b -> p (a b)")[:, 0:NB * H]
        xtok2 = at(8192, 5, D)
        u = at(0, NF, T)
        ytok = at(0, 2, D)

        ident = cst[:, K_ID:K_ID + P]
        ones = cst[:, K_ONE:K_ONE + P]
        bk = [ctx.enter_context(nc.psum_tensor(f"bank{i}", [P, 512], F32)) for i in range(8)]

        n_in = 12
        N_ADA1, N_ADA2 = 8, 16
        I_IN = N_ADA1
        I_ADA2 = I_IN + n_in
        I_DEC = I_ADA2 + N_ADA2
        BODY = ["K0", "K1", "V0", "K2", "V1", "K3", "V2", "K4", "V3", "K5", "V4", "K6", "V5", "V6", "V7", "K7"]
        I_LOOP = I_DEC + 8
        I_LAST = I_LOOP + 16 * (NB - 1)
        I_OUT = I_LAST + 8
        I_UP = I_OUT + 4
        I_DOWN = I_UP + 16
        ring_sem = [S(f"ring_loaded{k}") for k in range(SLOTS)]

        def landed(n):
            def upto(lo, hi, inc):
                hi = min(hi, n + 1)
                return sum(inc for m in range(lo, hi) if m % SLOTS == n % SLOTS) if hi > lo else 0
            return upto(0, I_DEC, 16) + upto(I_DEC, I_OUT, 16 * IP) + upto(I_OUT, I_DOWN + 16, 16)

        def slot(n):
            return ring[:, (n % SLOTS) * SLOT:(n % SLOTS + 1) * SLOT]

        def arrived(eng, n, i=0, step=0):
            per = landed(n + step) - landed(n) if step else 0
            eng.wait_ge(ring_sem[n % SLOTS], i * per + landed(n) if step else landed(n))

        def rows4(dram, r0, nk, c0, nc_):
            return dram[r0:r0 + nk * P, c0:c0 + nc_].rearrange("(k p) c -> p k c", p=P)

        def seg(v, s):
            return v[:, s:s + TP], v[:, 3 + TP:XPW].rearrange("p (b w) -> p b w", w=DT + 3)[:, :, s:s + DT]

        sfin = rs[:, 0:512].rearrange("p (t n) -> p t n", t=4)
        block = ctx.enter_context(nc.Block())

        @block.sync
        def _(sp):
            npar = [0]

            def par(dst, src):
                sp.dma_start(dst, src).then_inc(S("params_loaded"), 16)
                npar[0] += 1

            par(crow[0:1, :], a["c_prompt"])
            par(crow[1:9, :], a["c_sample"])
            par(cst[:, :], a["shape_consts"])
            par(newb[:, :, :].rearrange("p b k -> p (b k)"), a["shape_new"])
            par(picks, a["shape_picks"])
            for c0, n, src in ((C_BADA, 48, a["b_ada"][0]), (C_GMIX, 8, a["g_mix"][0]), (C_GFFN, 8, a["g_ffn"][0]),
                               (C_GFIN, 8, a["g_final"]), (C_CB, 8, a["conv_b"][0]), (C_SSD, 4, a["ssd_norm_g"][0]),
                               (C_SUB, 1, a["subln_g"][0])):
                par(vrow[c0:c0 + n, :], src.rearrange("(r c) -> r c", c=P))
            par(vrow[C_CW:C_CW + 32, :], a["conv_w"][0].rearrange("i (r c) -> (i r) c", c=P))
            for j, name in enumerate(("lam_q1", "lam_q2", "lam_k1", "lam_k2")):
                par(small[0:HD, j:j + 1], a[name].rearrange("a b -> b a"))
            for j, name in enumerate(("dt_bias", "a_log", "d_skip")):
                par(small[0:SH, 4 + j:5 + j], a[name].rearrange("a b -> b a"))
            par(small[0:32, 8:12], a["rel_bias"])
            par(scr[0:24, :], a["state_conv"][0].rearrange("b w c -> (b w) c"))
            par(hot[0:33, :, :], a["shape_hot"])
            par(rows[0:SH, 2, :], a["shape_starts"])
            assert npar[0] == N_PAR, npar
            for m in range(MT):
                sp.dma_start(xtok[:, m, :], a["x_prompt"][0, m * P:(m + 1) * P, :]).then_inc(S("x_loaded"), 16)
            sp.dma_start(xtok[0:TS, MT, :], a["x_sample"].rearrange("b t d -> (b t) d")).then_inc(S("x_loaded"), 16)

            def free(n, i=None, step=0):
                if i is not None:
                    sp.wait_ge(S("ring_used"), i * step + (n - SLOTS + 1))
                elif n >= SLOTS:
                    sp.wait_ge(S("ring_used"), n - SLOTS + 1)

            def load(n, src, nk=KT, i=None, step=0):
                free(n, i, step)
                sp.dma_start(slot(n).rearrange("p (k c) -> p k c", k=nk), src).then_inc(ring_sem[n % SLOTS], 16)

            w_ada, w_in = a["w_ada"][0], a["w_in"][0]
            for n in range(N_ADA1):
                load(n, rows4(w_ada, 0, KT, n * IT, IT))
            sp.dma_start(wdt[:, :, :], rows4(w_in, 0, KT, 3072, SH)).then_inc(S("wdt_loaded"), 16)
            for n, c in enumerate((8, 9, 10, 11, 6, 7, 0, 1, 2, 3, 4, 5)):
                load(I_IN + n, rows4(w_in, 0, KT, c * IT, IT))
            sp.wait_ge(S("tables_ready"), 1)
            sp.dma_start(scratch.rearrange("r h t -> h r t"), brow[0:H, :, :]).then_inc(S("tables_stored"), 16)
            sp.wait_ge(S("tables_stored"), 16)
            sp.wait_ge(S("x_free"), 1)
            f0 = bass.AP(scratch.tensor, scratch.offset, [[1, P], [TAB, H], [1, 2 * P]])
            sp.dma_start(wrev, f0).then_inc(S("bias_loaded"), 16)
            sp.wait_ge(S("near_zero"), 1)
            for h in range(H):
                for j in range(2):
                    row = 32 * h + DT * j
                    sp.dma_start(nearr[row:row + DT, :],
                                 bass.AP(scratch.tensor, scratch.offset + h * TAB + OFF - (DT - 1),
                                         [[1, DT], [1, NBIAS]])).then_inc(S("bias_loaded"), 16)
            with sp.Fori(0, N_ADA2 // SLOTS) as i:
                for k in range(SLOTS):
                    load(I_ADA2 + k, w_ada[:, bass.ds((i * SLOTS + (N_ADA1 + k)) * IT, IT)]
                         .rearrange("(k p) c -> p k c", p=P), i=i, step=SLOTS)

            kc, vc = a["cache_k"], a["cache_v"]
            pt = a["page_table"]

            numbers = {}

            def pages(n, what, b, i=None, step=0):
                g = int(what[1:])
                if g % 4 == 0:
                    _, numbers[what[0]] = nc.values_load_multi_w_load_instructions(
                        pt[bass.ds(b, 1), g * IP:(g + 4) * IP], engines=[mybir.EngineType.SP],
                        min_val=0, max_val=N_POOL - 1)
                phys = numbers[what[0]][g % 4 * IP:(g % 4 + 1) * IP]
                free(n, i, step)
                src = kc if what[0] == "K" else vc
                for p in range(IP):
                    sp.dma_start(slot(n)[:, p * 512:(p + 1) * 512],
                                 src[bass.ds(phys[p], 1), :, :].rearrange("a p f -> (a p) f"))\
                        .then_inc(ring_sem[n % SLOTS], 16)

            for g in range(8):
                pages(I_DEC + g, f"K{g}", 0)
            with sp.Fori(0, NB - 1) as i:
                for k, what in enumerate(BODY):
                    pages(I_LOOP + k, what, i + 1 if what[0] == "K" else i, i=i, step=16)
            for g in range(8):
                pages(I_LAST + g, f"V{g}", NB - 1)

            for k in range(4):
                load(I_OUT + k, rows4(a["w_out"][0], 0, KT, k * IT, IT))
            with sp.Fori(0, 4) as i:
                for k in range(4):
                    load(I_UP + k, a["w_up"][0][:, bass.ds((i * 4 + k) * IT, IT)]
                         .rearrange("(k p) c -> p k c", p=P), i=i, step=4)
            with sp.Fori(0, 4) as i:
                for k in range(4):
                    load(I_DOWN + k, a["w_down"][0][k * D:(k + 1) * D, bass.ds(i * IT, IT)]
                         .rearrange("(k p) c -> p k c", p=P), i=i, step=4)
            for m in range(5):
                sp.wait_ge(S("yt_a"), m + 1)
                sp.wait_ge(S("yt_v"), m + 1)
                n = P if m < MT else TS
                dst = o["y_p"][m * P:(m + 1) * P, :] if m < MT else o["y_s"]
                sp.dma_start(dst, ytok[0:n, m % 2, :]).then_inc(S(f"y_stored{m % 2}"), 16)
            for k, stores in enumerate((3, 2)):
                sp.wait_ge(S(f"y_stored{k}"), 16 * stores)
                sp.wait_ge(S(f"kout_stored{k}"), 16 * stores)
            sp.wait_ge(S("out_stored"), 16 * 8)


        tiles = [("x", c) for c in range(8)] + [("d", 0)] + [("z", t) for t in range(4)]
        tiles += [("q", h) for h in range(4)] + [("k", h) for h in range(4)]
        tiles += [("v", 5 * half + m) for half in range(2) for m in range(5)]
        by_dve = [sum(1 for kind, _ in tiles[:n] if kind not in "v") for n in range(len(tiles) + 1)]
        first = {"x": 0, "z": 4, "q": 6, "k": 8, "v": 10}
        tile_sign, plain = [], 0
        for kind, t in tiles:
            if (kind == "v" and t % 5 == 4) or (kind in "qkzx" and t % 2 == 1):
                tile_sign.append(("ring_used", I_IN + first[kind] + (t // 5 if kind == "v" else t // 2) + 1))
            else:
                plain += 1
                tile_sign.append(("ip_ps", plain))

        @block.gpsimd
        def _(pool):
            pool.memset(small[32:33, 8:12], 1.0).then_inc(S("ones_row"), 1)
            pool.wait_ge(S("ones_row"), 1)
            pool.memset(qbd, 0.0).then_inc(S("qbd_zero"), 1)
            pool.wait_ge(S("qbd_zero"), 1)
            pool.memset(xp[:, :, 0:3], 0.0).then_inc(S("xp_zero"), 1)
            pool.wait_ge(S("x_free"), 1)
            pool.memset(nearr, 0.0).then_inc(S("near_zero"), 1)

            for m in range(5):
                pool.wait_ge(S("kout_ready"), m + 1)
                n = P if m < MT else TS
                dst = o["k_p"][m * P:(m + 1) * P, :] if m < MT else o["k_s"]
                pool.dma_start(dst, kout[0:n, m % 2, :]).then_inc(S(f"kout_stored{m % 2}"), 16)
            for m in range(5):
                n = P if m < MT else TS
                dst = o["v_p"][m * P:(m + 1) * P, :] if m < MT else o["v_s"]
                pool.dma_start(dst, vtk[0:n, m, :]).then_inc(S("out_stored"), 16)
            pool.wait_ge(S("conv_rows"), 1)
            pool.dma_start(o["conv_p"], sout[0:3, :]).then_inc(S("out_stored"), 16)
            pool.dma_start(o["conv_s"], sout[3:27, :]).then_inc(S("out_stored"), 16)
            pool.wait_ge(S("out_stored"), 16 * 7)
            pool.wait_ge(S("xn"), KT)
            for b in range(NB):
                pool.dma_start(h0[:, b, :, :], a["state_ssm"][0, b].rearrange("(t h) p n -> (h p) t n", t=4))\
                    .then_inc(S("h0_loaded"), 16)
            pool.wait_ge(S("final_ready"), 1)
            pool.dma_start(o["ssm_p"].rearrange("(t p) n -> p t n", p=P), sfin).then_inc(S("out_stored"), 16)
            pool.wait_ge(S("ssm_ready"), 1)
            for b in range(NB):
                pool.dma_start(o["ssm_s"][b * 512:(b + 1) * 512, :].rearrange("(t p) n -> p t n", p=P), h0[:, b, :, :])\
                    .then_inc(S("ssm_stored"), 16)
            pool.wait_ge(S("dec_start"), 1)
            pool.tensor_copy(qcur[:, :, 0:2 * DT], qbd[:, 0, :, :, :].rearrange("p h j t -> p h (j t)"))\
                .then_inc(S("q_ready"), 1)
            with pool.Fori(0, NB - 1) as i:
                pool.wait_ge(S("s_ps"), i * 8 + 8)
                pool.wait_ge(S("q_ready"), i + 1)
                pool.tensor_copy(qcur[:, :, 0:2 * DT],
                                 qbd[:, bass.ds(i + 1, 1), :, :, :].rearrange("p a h j t -> p (a h) (j t)"))\
                    .then_inc(S("q_ready"), 1)
            pool.wait_ge(S("od_ready"), 1)
            pool.wait_ge(S("ssm_stored"), 16 * NB)
            for m in range(MT):
                pool.dma_start(xtok2[:, m, :], a["x_prompt"][0, m * P:(m + 1) * P, :]).then_inc(S("x_reloaded"), 16)
            pool.dma_start(xtok2[0:TS, MT, :], a["x_sample"].rearrange("b t d -> (b t) d")).then_inc(S("x_reloaded"), 16)


        @block.tensor
        def _(pe):
            mm, tr = pe.matmul, pe.transpose

            def turn_x(k, src):
                pe.wait_ge(S("x_reloaded" if k else "x_loaded"), 16 * 5)
                for m in range(5):
                    n = P if m < MT else TS
                    for half in range(2):
                        w = 2 * m + half
                        if w >= 4:
                            pe.wait_ge(S("xt_a" if half == 0 else "xt_v"), 5 * k + (w - 4) // 2 + 1)
                        for f in range(4):
                            ins = tr(bk[w % 4][:, f * P:f * P + n],
                                     src[0:n, m, (4 * half + f) * P:(4 * half + f + 1) * P], ident[0:n, 0:n])
                        ins.then_inc(S("xt_ps"), 1)

            pe.wait_ge(S("params_loaded"), 16 * N_PAR)
            pe.wait_ge(S("ada_sb"), 2)
            tr(bk[4][:, 0:NROW], vrow[0:NROW, :], ident[0:NROW, 0:NROW]).then_inc(S("cols_ps"), 1)
            turn_x(0, xtok)
            pe.wait_ge(S("silu_rows"), 1)
            for k in range(KT):
                ins = tr(bk[5][:, k * 9:(k + 1) * 9], ctmp[0:9, k * P:(k + 1) * P], ident[0:9, 0:9])
            ins.then_inc(S("ct_ps"), 1)
            pe.wait_ge(S("lam_prod"), 1)
            mm(bk[6][:, 0:2], ones[0:HD, :], small[0:HD, 12:14], start=True, stop=True)
            for t in range(4):
                for r in range(2):
                    ins = mm(bk[6][64 * r:64 * r + 64, 4 + t:5 + t],
                             ident[0:SH, 2 * t + r:2 * t + r + 1].to_broadcast([SH, SP_]), small[0:SH, 6:7],
                             start=True, stop=True)
            ins.then_inc(S("lam_ps"), 1)
            pe.wait_ge(S("ones_row"), 1)
            pe.wait_ge(S("lam_ready"), 1)
            for r in range(2):
                ins = mm(bk[6 + r][0:H, 0:TAB], small[0:33, 8:12], hot[0:33, r, :], start=True, stop=True)
            ins.then_inc(S("tables_ps"), 1)
            pe.wait_ge(S("tables_ready"), 1)
            for c in range(8):
                ins = tr(bk[6][:, c * 24:(c + 1) * 24], scr[0:24, c * P:(c + 1) * P], ident[0:24, 0:24])
            ins.then_inc(S("cs_ps"), 1)
            pe.wait_ge(S("prefix_ready"), 1)

            def norm_sum(k):
                for f in range(KT):
                    pe.wait_ge(S("squares"), KT * k + f + 1)
                    mm(bk[6][:, 0:HF], ones, hT[:, f, 0:HF], start=(f == 0), stop=(f == KT - 1))
                    ins = mm(bk[7][:, 0:HF], ones, hT[:, f, HF:T], start=(f == 0), stop=(f == KT - 1))
                ins.then_inc(S("ssum"), 1)

            def ada_parts(bank, j, w):
                w = w.rearrange("p (k c) -> p k c", k=KT)
                for f in range(KT):
                    r = 32 * (f % 4)
                    ins = mm(bank[r:r + 9, (j % 2) * IT:(j % 2 + 1) * IT], cT[:, f, :], w[:, f, :],
                             start=(f < 4), stop=(f >= 4))
                ins.then_inc(S("ring_used"), 1)

            def ada(n0, i):
                for q in range(2):
                    pe.wait_ge(S("ada_sb"), i * 2 + (q + 1))
                    for j in (2 * q, 2 * q + 1):
                        arrived(pe, n0 + j, i, SLOTS)
                        ada_parts(bk[4 + q], j, slot(n0 + j))
                for q in range(2):
                    pe.wait_ge(S("ada_sb"), i * 2 + (q + 3))
                    for t in range(4):
                        ins = mm(bk[3][:, bass.ds(i * (8 * 9) + (4 * q + t) * 9, 9)], adas[:, q, t * P:(t + 1) * P],
                                 cst[:, K_SUM:K_SUM + 9], start=True, stop=True)
                ins.then_inc(S("mod_ps"), 1)

            pe.wait_ge(S("ct_ready"), 1)
            with pe.Fori(0, N_ADA1 // SLOTS) as i:
                ada(0, i)
            norm_sum(0)

            pe.wait_ge(S("h_prompt"), KT)
            pe.wait_ge(S("h_sample"), 1)

            def dense(bp, bs, w, c0, m, ks, src, start, stop):
                for j, f in enumerate(ks):
                    s, e = start and j == 0, stop and j == len(ks) - 1
                    mm(bp[0:m, 0:HF], w[:, j, c0:c0 + m], src[:, f, 0:HF], start=s, stop=e)
                    ins = mm(bs[0:m, 0:HF], w[:, j, c0:c0 + m], src[:, f, HF:T], start=s, stop=e)
                return ins

            def tok_rows():
                pe.wait_ge(S("rows_ready"), 1)
                for m in range(5):
                    n = P if m < MT else TS
                    for r in range(3):
                        ins = tr(bk[6][0:n, (3 * m + r) * SH:(3 * m + r + 1) * SH], rows[0:SH, r, m * P:m * P + n],
                                 ident[0:SH, 0:SH])
                ins.then_inc(S("tok_ps"), 1)
                for h in range(SH):
                    ins = mm(bk[7][:, h * 12:(h + 1) * 12], ident[0:SH, h:h + 1].to_broadcast([SH, P]),
                             small[0:SH, 24:36], start=True, stop=True)
                ins.then_inc(S("dec_ps"), 1)

            def conv_ends():
                pe.wait_ge(S("ends_ready"), 8)
                for c in range(8):
                    ins = tr(bk[c // 4][0:27, (c % 4) * P:(c % 4 + 1) * P], gc[:, c, :], ident)
                ins.then_inc(S("conv_ps"), 1)
                pe.wait_ge(S("conv_rows"), 1)

            for n, (kind, t) in enumerate(tiles):
                bp, bs = bk[2 * (n % 2)], bk[2 * (n % 2) + 1]
                if n >= 2:
                    pe.wait_ge(S("ip_act"), n - 1)
                    if by_dve[n - 1] > 0:
                        pe.wait_ge(S("ip_dve"), by_dve[n - 1])
                sign = tile_sign[n][0]
                if kind == "v":
                    half, m = t // 5, t % 5
                    k = I_IN + first["v"] + half
                    r = P if m < MT else TS
                    if m == 0:
                        arrived(pe, k)
                    w = slot(k).rearrange("p (k c) -> p k c", k=KT)
                    for f in range(KT):
                        ins = mm(bp[0:r, 0:IT], hT[:, f, m * P:m * P + r], w[:, f, :],
                                 start=(f == 0), stop=(f == KT - 1))
                elif kind == "d":
                    pe.wait_ge(S("wdt_loaded"), 16)
                    ins = dense(bp, bs, wdt, 0, SH, range(KT), hT, True, True)
                else:
                    k = I_IN + first[kind] + t // 2
                    if t % 2 == 0:
                        arrived(pe, k)
                    w = slot(k).rearrange("p (k c) -> p k c", k=KT)
                    ins = dense(bp, bs, w, (t % 2) * P, P, range(KT), hT, True, True)
                ins.then_inc(S(sign), 1)

            pe.wait_ge(S("ip_act"), len(tiles))
            pe.wait_ge(S("ip_dve"), by_dve[-1])
            tok_rows()
            conv_ends()
            for m in range(5):
                n = P if m < MT else TS
                if m >= 2:
                    pe.wait_ge(S("kout_ready"), m - 1)
                for h in range(H):
                    ins = tr(bk[m % 2][0:n, h * P:(h + 1) * P], kT[:, h, m * P:m * P + n], ident)
                ins.then_inc(S("kout_ps"), 1)

            units = [(h, qb) for h in range(H) for qb in range(MT)]

            def ada_item(x):
                if x >= 2 and x % 2 == 0:
                    pe.wait_ge(S("ada_sb"), 2 + N_ADA1 // 2 + x // 2)
                arrived(pe, I_ADA2 + x)
                ada_parts(bk[1], x, slot(I_ADA2 + x))

            def att_scores(x):
                h, qb = units[x]
                nk = (qb + 1) * P
                if x >= 2:
                    pe.wait_ge(S("att_exp"), 2 * (x - 1))
                for j in range(2):
                    ins = mm(bk[2 + 2 * (x % 2) + j][:, 0:nk], qT[64 * j:64 * j + 64, h, qb * P:(qb + 1) * P],
                             kT[64 * j:64 * j + 64, h, 0:nk], start=True, stop=True)
                ins.then_inc(S("att_s"), 1)

            def att_transpose(x):
                h, qb = units[x]
                pe.wait_ge(S("att_p"), x + 1)
                if x >= 2:
                    pe.wait_ge(S("att_pt"), x - 1)
                for kb in range(qb + 1):
                    ins = tr(bk[6 + x % 2][:, kb * P:(kb + 1) * P], pj[:, x % 2, 0, kb * P:(kb + 1) * P], ident)
                ins.then_inc(S("att_t"), 1)

            def att_values(x):
                h, qb = units[x]
                pe.wait_ge(S("att_pt"), x + 1)
                if qb == 0 and h >= 1:
                    pe.wait_ge(S("att_o"), h)
                for kb in range(qb + 1):
                    ins = mm(bk[0][:, qb * P:(qb + 1) * P], vtk[:, kb, h * VD:(h + 1) * VD],
                             pts[:, x % 2, kb * P:(kb + 1) * P], start=(kb == 0), stop=(kb == qb))
                ins.then_inc(S("att_v"), 1)

            pe.wait_ge(S("kout_ready"), 5)
            pe.wait_ge(S("dec_sb"), 1)
            NU = len(units)
            att_scores(0)
            for x in range(NU + 2):
                if x + 1 < NU:
                    att_scores(x + 1)
                if x < NU:
                    ada_item(x)
                if 1 <= x <= NU:
                    att_transpose(x - 1)
                if x >= 2:
                    att_values(x - 2)
            def head_norm(bank, k, n):
                pe.wait_ge(S("att_sq"), k + 1)
                mm(bank[:, 0:n], ones, hT[:, k % H, 0:n], start=True, stop=True).then_inc(S("att_ss"), 1)

            for h in range(H):
                head_norm(bk[2 + h], h, TP)

            pe.wait_ge(S("ada_sb"), 2 + (N_ADA1 + N_ADA2) // 2)
            for k in range(N_ADA2 // 2):
                for t in range(4):
                    ins = mm(bk[1][:, (4 * k + t) * 9:(4 * k + t + 1) * 9], adas2[:, k, t * P:(t + 1) * P],
                             cst[:, K_SUM:K_SUM + 9], start=True, stop=True)
            ins.then_inc(S("mod_ps"), 1)
            pe.wait_ge(S("att_n"), H)
            pe.wait_ge(S("mod2"), 1)
            for m in range(5):
                n = P if m < MT else TS
                if m >= 2:
                    pe.wait_ge(S("xtk_v"), m - 1)
                for t in range(4):
                    ins = tr(bk[m % 2][0:n, t * P:(t + 1) * P], xp[:, t, m * P:m * P + n], ident)
                ins.then_inc(S("xtk_ps"), 1)
                if m >= 2:
                    pe.wait_ge(S("btk_a"), m - 1)
                for g in range(GR):
                    ins = tr(bk[2 + m % 2][0:n, g * P:(g + 1) * P], xp[:, 4 + g, m * P:m * P + n], ident)
                ins.then_inc(S("btk_ps"), 1)
            for g in range(GR):
                for c in range(MT):
                    ins = mm(bk[4 + g][:, c * P:(c + 1) * P], xp[:, 4 + g, c * P:(c + 1) * P],
                             xp[:, 6 + g, c * P:(c + 1) * P], start=True, stop=True)
                ins.then_inc(S("cb_ps"), 1)
            for g in range(GR):
                ins = mm(bk[6][0:TS, g * TS:(g + 1) * TS], xp[:, 4 + g, TP:T], xp[:, 6 + g, TP:T],
                         start=True, stop=True)
            ins.then_inc(S("cb_ps"), 1)
            pe.wait_ge(S("xtk_v"), 5)
            pe.wait_ge(S("btk_a"), 5)
            for c in range(MT):
                for g in range(GR):
                    ins = mm(bk[c][:, g * 256:(g + 1) * 256], btk[:, c, g * NS:(g + 1) * NS],
                             xw[:, c, g * 256:(g + 1) * 256], start=True, stop=True)
                ins.then_inc(S("st_ps"), 1)

            def bcast(h):
                if h >= 2:
                    pe.wait_ge(S("cexp"), h - 1)
                sel = ident[0:SH, h:h + 1].to_broadcast([SH, P])
                mm(bk[h % 2][:, :], sel, rows[0:SH, 1, 0:TP], start=True, stop=True)
                mm(bk[2 + h % 2][:, 0:TS], sel, rows[0:SH, 1, TP:T], start=True, stop=True).then_inc(S("cs_bc"), 1)

            def ssd_y(h):
                t, r = h // 2, h % 2
                pe.wait_ge(S("g_ready"), h + 1)
                if r == 0 and t >= 2:
                    pe.wait_ge(S("y_sb"), t - 1)
                y, ys = bk[4 + t % 2][64 * r:64 * r + 64, :], bk[6 + t % 2][64 * r:64 * r + 64, :]
                hs = slice(h * SP_, (h + 1) * SP_)
                for c in range(MT):
                    mm(y[:, c * P:(c + 1) * P], xdt[:, c, hs], lg[:, h % 2, c * P:(c + 1) * P],
                       start=True, stop=(c == 0))
                    if c:
                        mm(y[:, c * P:(c + 1) * P], prev[:, c - 1, hs], ceb[:, h % 2, c * P:(c + 1) * P],
                           start=False, stop=True)
                mm(ys[:, 0:TS], xdt[0:TS, MT, hs], lg[0:TS, h % 2, TP:T], start=True, stop=False)
                for b in range(NB):
                    ins = mm(ys[:, b * DT:(b + 1) * DT], h0T[:, b, t, 64 * r:64 * r + 64],
                             ceb[:, h % 2, TP + b * DT:TP + (b + 1) * DT], start=False, stop=(b == NB - 1))
                ins.then_inc(S("y_ps"), 1)

            pe.wait_ge(S("prev_done"), 1)
            for t in range(4):
                ins = tr(bk[3][:, t * P:(t + 1) * P], prev[:, MT - 1, t * P:(t + 1) * P], ident)
            ins.then_inc(S("final_ps"), 1)
            pe.wait_ge(S("h0_loaded"), 16 * NB)
            for b in range(NB):
                if b >= 2:
                    pe.wait_ge(S("h0t_sb"), b - 1)
                for t in range(4):
                    ins = tr(bk[b % 2][:, t * P:(t + 1) * P], h0[:, b, t, :], ident)
                ins.then_inc(S("h0t_ps"), 1)
            pe.wait_ge(S("h0t_sb"), NB)
            pe.wait_ge(S("cb_sb"), 3)
            pe.wait_ge(S("final_ready"), 1)
            bcast(0)
            bcast(1)
            for h in range(SH):
                ssd_y(h)
                if h + 2 < SH:
                    bcast(h + 2)
            for g in range(GR):
                for t in (2 * g, 2 * g + 1):
                    pe.wait_ge(S("ssd_sq"), t + 1)
                    mm(bk[2 * g][:, 0:HF], ones, hT[:, t, 0:HF], start=(t % 2 == 0), stop=(t % 2 == 1))
                    ins = mm(bk[2 * g + 1][:, 0:HF], ones, hT[:, t, HF:T], start=(t % 2 == 0), stop=(t % 2 == 1))
                ins.then_inc(S("ssd_ss"), 1)
            pe.wait_ge(S("bblk_ready"), 1)
            for t in range(4):
                for q in range(2):
                    x = 2 * t + q
                    if x >= 2:
                        pe.wait_ge(S("ssm_sb"), x - 1)
                    mm(bk[4 + q][:, :], xws[:, t * P:(t + 1) * P],
                       bblk[0:TS, t // 2, 4 * q:4 * q + 4, :].rearrange("p b n -> p (b n)"),
                       start=True, stop=True).then_inc(S("ssm_ps"), 1)

            pe.wait_ge(S("dec_start"), 1)
            pe.wait_ge(S("dec_start_a"), 1)

            def k_item(n, b, g, i=None, step=0):
                arrived(pe, n, i, step) if step else arrived(pe, n)
                src = slot(n).rearrange("p (q c) -> p q c", q=IP)
                items = g if i is None else i * 8 + (8 + g)
                for p in range(IP):
                    if i is not None or g or p >= 2:
                        pe.wait_ge(S("kt_sb"), items * IP + (p - 1))
                    for h in range(H):
                        ins = tr(bk[p % 2][:, h * P:(h + 1) * P], src[:, p, h * P:(h + 1) * P], ident)
                    ins.then_inc(S("kt_ps" if p < IP - 1 else "ring_used"), 1)
                if g == 0:
                    pe.wait_ge(S("q_ready"), 1 if i is None else i + 2)
                if i is not None or g >= 2:
                    pe.wait_ge(S("s_sb"), items - 1)
                pe.wait_ge(S("kt_sb"), items * IP + IP)
                for h in range(H):
                    ins = mm(bk[2 + g % 2][32 * h:32 * h + 32, :], qcur[:, h, :], kts[:, g % 2, h, :],
                             start=True, stop=True)
                ins.then_inc(S("s_ps"), 1)

            def new_scores():
                for h in range(H):
                    ins = mm(bk[7][32 * h:32 * h + 32, 0:TS], qcur[:, h, :], kT[:, h, TP:T], start=True, stop=True)
                ins.then_inc(S("new_ps"), 1)

            def v_item(n, g, it, i=None, step=0):
                groups = (9 * it if i is None else i * 9) + g
                exps = 4 * it if i is None else i * 4
                arrived(pe, n, i, step) if step else arrived(pe, n)
                src = slot(n).rearrange("p (q c) -> p q c", q=IP)
                pe.wait_ge(S("pt_sb"), groups + (2 if g == 7 else 1))
                for p in range(IP):
                    for h in range(H):
                        ins = mm(bk[5][32 * h:32 * h + 16, 0:P], pT[:, g % 2, p * P + 32 * h:p * P + 32 * h + 16],
                                 src[:, p, h * P:(h + 1) * P], start=(g == 0 and p == 0), stop=False)
                ins.then_inc(S("ring_used"), 1)
                if g < 7:
                    turn_p(g + 1, exps)
                if g == 6:
                    turn_p(8, exps)
                if g == 7:
                    for h in range(H):
                        ins = mm(bk[5][32 * h:32 * h + 16, 0:P], pT[0:TS, 0, 32 * h:32 * h + 16],
                                 vtk[0:TS, MT, h * VD:(h + 1) * VD], start=False, stop=True)
                    ins.then_inc(S("o_ps"), 1)

            def turn_p(g, exps):
                if g % 2 == 0 and g < 8:
                    pe.wait_ge(S("exp_done"), exps + (g // 2 + 1))
                bank = bk[4 + 2 * (g % 2)]
                if g < 8:
                    for p in range(IP):
                        ins = tr(bank[:, p * P:(p + 1) * P], pr[:, (IP * g + p) * P:(IP * g + p + 1) * P], ident)
                else:
                    ins = tr(bank[0:TS, 0:P], pr[:, NK:NK + TS], ident)
                ins.then_inc(S("pt_ps"), 1)

            def combine(i, new):
                pe.wait_ge(S("on_ready"), i + 1)
                pe.wait_ge(S("new_sb"), new)
                mm(bk[7][:, P:P + NB * H], on, sel, start=True, stop=True).then_inc(S("od_ps"), 1)

            for g in range(8):
                k_item(I_DEC + g, 0, g)
                if g == 3:
                    new_scores()
            with pe.Fori(0, NB - 1) as i:
                for k, what in enumerate(BODY):
                    g = int(what[1:])
                    if what[0] == "K":
                        k_item(I_LOOP + k, i + 1, g, i=i, step=16)
                    else:
                        v_item(I_LOOP + k, g, None, i=i, step=16)
                    if what == "K1":
                        turn_p(0, i * 4)
                    if what == "K3":
                        pe.wait_ge(S("od_sb"), i + 1)
                        new_scores()
                combine(i, i + 2)
            turn_p(0, 4 * (NB - 1))
            for g in range(8):
                v_item(I_LAST + g, g, NB - 1)
            combine(NB - 1, NB)
            pe.wait_ge(S("od_sq"), 1)
            mm(bk[4][:, 0:H * TS], ones, hT[:, 0, 0:H * TS], start=True, stop=True).then_inc(S("od_ss"), 1)
            turn_x(1, xtok2)

            pe.wait_ge(S("mix_ready"), 1)
            pe.wait_ge(S("xt_a"), 10)
            pe.wait_ge(S("xt_v"), 10)

            for k in range(4):
                arrived(pe, I_OUT + k)
                w = slot(I_OUT + k).rearrange("p (k c) -> p k c", k=KT)
                for t in range(2):
                    x = 2 * k + t
                    if x >= 2:
                        pe.wait_ge(S("op_sb"), x - 1)
                    bp, bs = bk[2 * (x % 2)], bk[2 * (x % 2) + 1]
                    dense(bp, bs, w, t * P, P, range(KT), mix, True, True)\
                        .then_inc(S("op_ps" if t == 0 else "ring_used"), 1)
            norm_sum(1)
            pe.wait_ge(S("h_prompt"), 2 * KT)
            pe.wait_ge(S("h_sample"), 2)
            with pe.Fori(0, 4) as i:
                for k in range(4):
                    arrived(pe, I_UP + k, i, 4)
                    w = slot(I_UP + k).rearrange("p (k c) -> p k c", k=KT)
                    for t in range(2):
                        x = 2 * k + t
                        pe.wait_ge(S("up_sb"), i * 8 + (x + 1))
                        bp, bs = bk[2 * (x % 2)], bk[2 * (x % 2) + 1]
                        dense(bp, bs, w, t * P, P, range(KT), hT, True, True)\
                            .then_inc(S("up_ps" if t == 0 else "ring_used"), 1)
            pe.wait_ge(S("u_ready"), NF)
            with pe.Fori(0, 4) as i:
                for k in range(4):
                    arrived(pe, I_DOWN + k, i, 4)
                    w = slot(I_DOWN + k).rearrange("p (k c) -> p k c", k=KT)
                    for t in range(2):
                        if k == 0:
                            pe.wait_ge(S("down_sb"), i * 2 + (t + 1))
                        bp, bs = bk[2 * t], bk[2 * t + 1]
                        ins = dense(bp, bs, w, t * P, P, range(8 * k, 8 * k + 8), u, k == 0, k == 3)
                        if t == 1:
                            ins.then_inc(S("ring_used"), 1)
                        elif k == 3:
                            ins.then_inc(S("down_ps"), 1)
            norm_sum(2)
            pe.wait_ge(S("h_prompt"), 3 * KT)
            for m in range(5):
                n = P if m < MT else TS
                for half in range(2):
                    w = 2 * m + half
                    if w >= 4:
                        pe.wait_ge(S("yt_a" if half == 0 else "yt_v"), (w - 4) // 2 + 1)
                    for k in range(4):
                        ins = tr(bk[w % 4][0:n, k * P:(k + 1) * P], hT[:, 4 * half + k, m * P:m * P + n], ident)
                    ins.then_inc(S("yt_ps"), 1)

        @block.scalar
        def _(act):
            step = Tally(S("act_step"))

            def A(out, in_, f, **kw):
                return act.activation(out, in_, f, **kw)

            act.wait_ge(S("params_loaded"), 16 * N_PAR)
            A(ctmp[0:9, :], crow[0:9, :], ACT.Exp, scale=-1.0).then_inc(S("silu_exp"), 1)
            A(small[0:SH, 16:17], small[0:SH, 5:6], ACT.Exp).then_inc(S("alog_exp"), 1)

            def take_x(k):
                for m in range(5):
                    n = P if m < MT else TS
                    w = 2 * m
                    act.wait_ge(S("xt_ps"), 10 * k + w + 1)
                    A(xT[:, 0:4, m * P:m * P + n], bk[w % 4][:, :].rearrange("p (k c) -> p k c", k=4)[:, :, 0:n],
                      ACT.Copy).then_inc(S("xt_a"), 1)

            take_x(0)
            act.wait_ge(S("lam_ps"), 1)
            A(small[:, 18:20], bk[6][:, 0:2], ACT.Exp).then_inc(S("lam_exp"), 1)
            act.wait_ge(S("xt_v"), 5)
            act.wait_ge(S("xt_a"), 5)

            def norm(k):
                for f in range(KT):
                    A(hT[:, f, :], xT[:, f, :], ACT.Square).then_inc(S("squares"), 1)
                act.wait_ge(S("ssum"), k + 1)
                link(act, A(rs[:, 0:HF], bk[6][:, 0:HF], ACT.Ln, scale=1.0 / D, bias=cst_eps), step)
                link(act, A(rs[:, HF:T], bk[7][:, 0:HF], ACT.Ln, scale=1.0 / D, bias=cst_eps), step)
                A(rs[:, :], rs[:, :], ACT.Exp, scale=-0.5).then_inc(S("rstd"), 1)

            def modulate(k, g, sh):
                for f in range(KT):
                    act.wait_ge(S("xn"), KT * k + f + 1)
                    A(hT[:, f, 0:TP], hT[:, f, 0:TP], ACT.Identity, scale=g[:, f, 0:1], bias=mod[:, sh + f, 0:1])\
                        .then_inc(S("h_prompt"), 1)

            cst_eps = small[:, 63:64]
            act.wait_ge(S("eps_ready"), 1)
            norm(0)
            act.wait_ge(S("mod1"), 1)
            modulate(0, g1, 0)

            def sigmoid(out, x, done):
                link(act, A(out, x, ACT.Exp, scale=-1.0), step)
                link(act, A(out, out, ACT.Ln, bias=1.0), step)
                A(out, out, ACT.Exp, scale=-1.0).then_inc(S(done), 1)

            for n, (kind, t) in enumerate(tiles):
                bp = bk[2 * (n % 2)]
                sign, count = tile_sign[n]
                act.wait_ge(S(sign), count)
                if kind == "q":
                    ins = A(qT[:, t, 0:HF], bp[:, 0:HF], ACT.Copy, scale=HD ** -0.5)
                elif kind == "k":
                    ins = A(kT[:, t, 0:HF], bp[:, 0:HF], ACT.Copy)
                elif kind == "v":
                    half, m = t // 5, t % 5
                    r = P if m < MT else TS
                    ins = A(vtk[0:r, m, half * IT:(half + 1) * IT], bp[0:r, 0:IT], ACT.Copy)
                elif kind == "d":
                    ins = A(rs[0:SH, 0:HF], bp[0:SH, 0:HF], ACT.Identity, bias=small[0:SH, 4:5])
                elif kind == "z":
                    ins = A(zT[:, t, 0:HF], bp[:, 0:HF], ACT.Copy)
                else:
                    ins = A(xp[:, t, 3:3 + HF], bp[:, 0:HF], ACT.Copy)
                ins.then_inc(S("ip_act"), 1)
                if 1 <= n <= 8:
                    c = n - 1
                    act.wait_ge(S("ip_act"), c + 1)
                    act.wait_ge(S("ip_dve"), c + 1)
                    if c >= 2:
                        act.wait_ge(S("xa_ready"), c - 1)
                    pp, ss = seg(xp[:, c, :], 0)
                    w0, b0 = cols[:, C_CW + c:C_CW + c + 1], cols[:, C_CB + c:C_CB + c + 1]
                    A(cv[:, c % 2, 0:TP], pp, ACT.Identity, scale=w0, bias=b0).then_inc(S("tap0"), 1)
                    A(cv[:, c % 2, TP:T].rearrange("p (b t) -> p b t", b=NB), ss, ACT.Identity, scale=w0, bias=b0)\
                        .then_inc(S("tap0"), 1)
                if 2 <= n <= 9:
                    act.wait_ge(S("taps"), n - 1)
                    sigmoid(ce[:, n % 2, :], cv[:, n % 2, :], "conv_gate")
                if n == 10:
                    act.wait_ge(S("dt_abs"), 1)
                    link(act, A(rows[0:SH, 0, :], rows[0:SH, 0, :], ACT.Exp, scale=-1.0), step)
                    A(rows[0:SH, 0, :], rows[0:SH, 0, :], ACT.Ln, bias=1.0).then_inc(S("dt_ln"), 1)
                if n == 11:
                    act.wait_ge(S("dt_gap"), 1)
                    A(rows[0:SH, 2, :], rows[0:SH, 2, :], ACT.Exp).then_inc(S("dt_w"), 1)
                    A(small[0:SH, 24:36], small[0:SH, 24:36], ACT.Exp).then_inc(S("dt_w"), 1)
                if 12 <= n <= 15:
                    act.wait_ge(S("ip_act"), 9 + n - 11)
                    act.wait_ge(S("ip_dve"), 9 + n - 11)
                    sigmoid(mix[:, n - 8, :], zT[:, n - 12, :], "z_gate")
            NU = 16
            for x in range(NU + 1):
                if x < NU:
                    h, qb = x // MT, x % MT
                    nk = (qb + 1) * P
                    for j in range(2):
                        act.wait_ge(S("att_m"), 2 * x + j + 1)
                        if x >= 2 and j == 0:
                            act.wait_ge(S("att_t"), x - 1)
                        A(pj[:, x % 2, j, 0:nk], bk[2 + 2 * (x % 2) + j][:, 0:nk], ACT.Exp,
                          bias=small[:, 36 + 2 * (x % 2) + j:37 + 2 * (x % 2) + j],
                          accum_out=small[:, 40 + 2 * (x % 2) + j:41 + 2 * (x % 2) + j]).then_inc(S("att_exp"), 1)
                if x >= 1:
                    y = x - 1
                    act.wait_ge(S("att_t"), y + 1)
                    if y >= 2:
                        act.wait_ge(S("att_v"), y - 1)
                    nk = (y % MT + 1) * P
                    A(pts[:, y % 2, 0:nk], bk[6 + y % 2][:, 0:nk], ACT.Copy).then_inc(S("att_pt"), 1)
            for h in range(H):
                act.wait_ge(S("att_o"), h + 1)
                A(hT[:, h, 0:TP], mix[:, h, 0:TP], ACT.Square).then_inc(S("att_sq"), 1)
            for h in range(H):
                act.wait_ge(S("att_ss"), h + 1)
                link(act, A(hT[:, 4 + h, 0:TP], bk[2 + h][:, :], ACT.Ln, scale=1.0 / VD, bias=cst_eps), step)
                A(hT[:, 4 + h, 0:TP], hT[:, 4 + h, 0:TP], ACT.Exp, scale=-0.5).then_inc(S("att_r"), 1)

            for m in range(5):
                n = P if m < MT else TS
                act.wait_ge(S("btk_ps"), m + 1)
                if m == 0:
                    act.wait_ge(S("out_stored"), 16 * 7)
                A(btk[0:n, m, :], bk[2 + m % 2][0:n, 0:256], ACT.Copy).then_inc(S("btk_a"), 1)
            for g in range(GR):
                act.wait_ge(S("cb_ps"), g + 1)
                A(cbT[:, g, 0:TP], bk[4 + g][:, :], ACT.Copy).then_inc(S("cb_sb"), 1)
            act.wait_ge(S("cb_ps"), 3)
            A(cbT[0:TS, :, TP:T], bk[6][0:TS, 0:2 * TS].rearrange("p (g t) -> p g t", g=2), ACT.Copy)\
                .then_inc(S("cb_sb"), 1)
            act.wait_ge(S("att_n"), H)
            for b in range(NB):
                act.wait_ge(S("h0t_ps"), b + 1)
                A(h0T[:, b, :, :].rearrange("p t q -> p (t q)"), bk[b % 2][:, :], ACT.Copy).then_inc(S("h0t_sb"), 1)
            for h in range(SH):
                act.wait_ge(S("seg"), 5 * (h + 1))
                if h >= 2:
                    act.wait_ge(S("y_ps"), h - 1)
                step.up(A(ceb[:, h % 2, 0:TP], bk[h % 2][:, :], ACT.Exp))
                A(ceb[:, h % 2, TP:T], bk[2 + h % 2][:, 0:TS], ACT.Exp).then_inc(S("cexp"), 1)
                step.up(A(lg[:, h % 2, 0:TP], lg[:, h % 2, 0:TP], ACT.Exp))
                A(lg[0:TS, h % 2, TP:T], lg[0:TS, h % 2, TP:T], ACT.Exp).then_inc(S("lexp"), 1)
            for t in range(4):
                act.wait_ge(S("y_gated"), t + 1)
                act.wait_ge(S("y_ps"), SH)
                A(hT[:, t, :], mix[:, 4 + t, :], ACT.Square).then_inc(S("ssd_sq"), 1)
            for g in range(GR):
                act.wait_ge(S("ssd_ss"), g + 1)
                r = hT[:, 4 + g, :]
                link(act, A(r[:, 0:HF], bk[2 * g][:, 0:HF], ACT.Ln, scale=1.0 / 256, bias=cst_eps), step)
                link(act, A(r[:, HF:T], bk[2 * g + 1][:, 0:HF], ACT.Ln, scale=1.0 / 256, bias=cst_eps), step)
                A(r, r, ACT.Exp, scale=-0.5).then_inc(S("ssd_r"), 1)
            act.wait_ge(S("dec_start"), 1)
            act.wait_ge(S("ssd_r"), 2)
            A(small[:, 56:57], cst_eps, ACT.Copy).then_inc(S("dec_start_a"), 1)

            def copy_page(page, i=None):
                if page % IP < IP - 1:
                    n = page // IP * (IP - 1) + page % IP + 1
                    act.wait_ge(S("kt_ps"), n if i is None else i * (8 * (IP - 1)) + (8 * (IP - 1) + n))
                elif i is None:
                    act.wait_ge(S("ring_used"), I_DEC + page // IP + 1)
                else:
                    act.wait_ge(S("ring_used"), i * 16 + (I_LOOP + BODY.index(f"K{page // IP}") + 1))
                g, p = page // IP, page % IP
                if i is not None or g >= 2:
                    act.wait_ge(S("s_ps"), g - 1 if i is None else i * 8 + (g + 7))
                A(kts[:, g % 2, :, p * P:(p + 1) * P], bk[p % 2][:, :].rearrange("p (h c) -> p h c", h=H), ACT.Copy)\
                    .then_inc(S("kt_sb"), 1)

            def softmax_exp(i, c):
                act.wait_ge(S("max_ready"), i + 1)
                lo, hi = c * (NK // 4), (c + 1) * (NK // 4) if c < 3 else NK + TS
                A(pr[:, lo:hi], sc[:, lo:hi], ACT.Exp, bias=small[:, 46:47], accum_out=small[:, 50 + c:51 + c])\
                    .then_inc(S("exp_done"), 1)

            for page in range(PAGES):
                copy_page(page)
            with act.Fori(0, NB - 1) as i:
                for page in range(PAGES):
                    copy_page(page, i)
                    if 2 <= page < 6:
                        softmax_exp(i, page - 2)
            for c in range(4):
                softmax_exp(NB - 1, c)
            act.wait_ge(S("od_ready"), 1)
            A(hT[:, 0, 0:H * TS].rearrange("p (h t) -> p h t", h=H), mix[:, 0:H, TP:T], ACT.Square).then_inc(S("od_sq"), 1)
            act.wait_ge(S("od_ss"), 1)
            link(act, A(hT[:, 1, 0:H * TS], bk[4][:, 0:H * TS], ACT.Ln, scale=1.0 / VD, bias=cst_eps), step)
            A(hT[:, 1, 0:H * TS], hT[:, 1, 0:H * TS], ACT.Exp, scale=-0.5).then_inc(S("od_r"), 1)

            take_x(1)
            act.wait_ge(S("x1_ready"), 1)
            norm(1)
            modulate(1, g2, 24)
            act.wait_ge(S("h_sample"), 2)
            act.wait_ge(S("x2_ready"), 1)
            norm(2)
            for f in range(KT):
                act.wait_ge(S("xn"), KT * 2 + f + 1)
                A(hT[:, f, :], hT[:, f, :], ACT.Copy, scale=cols[:, C_GFIN + f:C_GFIN + f + 1])\
                    .then_inc(S("h_prompt"), 1)
            for m in range(5):
                n = P if m < MT else TS
                act.wait_ge(S("yt_ps"), 2 * m + 1)
                if m >= 2:
                    act.wait_ge(S(f"y_stored{m % 2}"), 16 * (m // 2))
                A(ytok[0:n, m % 2, 0:TP], bk[(2 * m) % 4][0:n, :], ACT.Copy).then_inc(S("yt_a"), 1)

        @block.vector
        def _(v):
            step = Tally(S("dve_step"))

            def L(ins):
                link(v, ins, step)

            def bc(ap, shape):
                return ap.to_broadcast(shape)

            L(v.memset(small[:, 63:64], EPS))
            v.memset(bk[4][:, :], 0.0).then_inc(S("ada_sb"), 1)
            v.memset(bk[5][:, :], 0.0).then_inc(S("ada_sb"), 1)
            v.memset(small[:, 62:63], 0.0).then_inc(S("eps_ready"), 1)
            v.wait_ge(S("params_loaded"), 16 * N_PAR)
            v.wait_ge(S("cols_ps"), 1)
            v.tensor_copy(cols[:, :], bk[4][:, 0:NROW]).then_inc(S("cols_ready"), 1)
            v.wait_ge(S("cols_ready"), 1)
            v.wait_ge(S("silu_exp"), 1)
            L(v.tensor_scalar(ctmp[0:9, :], ctmp[0:9, :], 1.0, None, ALU.add))
            L(v.reciprocal(ctmp[0:9, :], ctmp[0:9, :]))
            v.tensor_tensor(ctmp[0:9, :], ctmp[0:9, :], crow[0:9, :], ALU.mult).then_inc(S("silu_rows"), 1)
            v.wait_ge(S("alog_exp"), 1)
            L(v.tensor_scalar(small[0:SH, 16:17], small[0:SH, 16:17], -1.0, None, ALU.mult))
            v.tensor_tensor(small[0:HD, 12:14], small[0:HD, 0:2], small[0:HD, 2:4], ALU.mult)\
                .then_inc(S("lam_prod"), 1)

            def take_x(k):
                for m in range(5):
                    n = P if m < MT else TS
                    w = 2 * m + 1
                    v.wait_ge(S("xt_ps"), 10 * k + w + 1)
                    v.tensor_copy(xT[:, 4:8, m * P:m * P + n],
                                  bk[w % 4][:, :].rearrange("p (k c) -> p k c", k=4)[:, :, 0:n]).then_inc(S("xt_v"), 1)

            take_x(0)
            v.wait_ge(S("ct_ps"), 1)
            v.tensor_copy(cT[:, :, :], bk[5][:, 0:72].rearrange("p (k c) -> p k c", k=KT)).then_inc(S("ct_ready"), 1)
            v.wait_ge(S("lam_exp"), 1)
            L(v.tensor_copy(small[:, 20:24], bk[6][:, 4:8]))
            L(v.tensor_tensor(small[:, 17:18], small[:, 19:20], small[:, 18:19], ALU.subtract))
            v.tensor_scalar(small[:, 17:18], small[:, 17:18], -0.2, None, ALU.add).then_inc(S("lam_ready"), 1)
            v.wait_ge(S("lam_ready"), 1)
            v.wait_ge(S("tables_ps"), 1)
            L(v.tensor_copy(brow[0:H, 0, :], bk[6][0:H, 0:TAB]))
            v.tensor_copy(brow[0:H, 1, :], bk[7][0:H, 0:TAB]).then_inc(S("tables_ready"), 1)
            v.wait_ge(S("cs_ps"), 1)
            v.wait_ge(S("xp_zero"), 1)
            pre = xp[:, :, 3 + TP:XPW].rearrange("p c (b w) -> p c b w", w=DT + 3)[:, :, :, 0:3]
            for c in range(8):
                ins = v.tensor_copy(pre[:, c], bk[6][:, c * 24:(c + 1) * 24].rearrange("p (b w) -> p b w", b=NB))
                if c < 7:
                    L(ins)
            ins.then_inc(S("prefix_ready"), 1)
            v.wait_ge(S("prefix_ready"), 1)

            v.wait_ge(S("xt_a"), 5)
            v.memset(small[:, 61:62], 0.0).then_inc(S("x_free"), 1)

            def norm(k):
                v.wait_ge(S("rstd"), k + 1)
                for f in range(KT):
                    v.tensor_tensor(hT[:, f, :], xT[:, f, :], rs[:, :], ALU.mult).then_inc(S("xn"), 1)

            def modulate(k, g, sh):
                v.wait_ge(S("xn"), KT * (k + 1))
                for f in range(KT):
                    hs = hT[:, f, TP:T].rearrange("p (b t) -> p b t", b=NB)
                    step.up(v.tensor_tensor(hs, hs, bc(g[:, f, 1:9].unsqueeze(2), [P, NB, DT]), ALU.mult))
                v.wait_ge(step.sem, step.n)
                for f in range(KT):
                    hs = hT[:, f, TP:T].rearrange("p (b t) -> p b t", b=NB)
                    ins = v.tensor_tensor(hs, hs, bc(mod[:, sh + f, 1:9].unsqueeze(2), [P, NB, DT]), ALU.add)
                    if f < KT - 1:
                        step.up(ins)
                ins.then_inc(S("h_sample"), 1)

            def take_mod(bank, t0, nt):
                L(v.tensor_tensor(mod[:, t0:t0 + nt, :], bank[:, 0:nt * 9].rearrange("p (t c) -> p t c", c=9),
                                  bc(cols[:, C_BADA + t0:C_BADA + t0 + nt].unsqueeze(2), [P, nt, 9]), ALU.add))

            def gain(g, t0, c0):
                L(v.tensor_scalar(g[:, :, :], mod[:, t0:t0 + KT, :], 1.0, None, ALU.add))
                return v.tensor_tensor(g[:, :, :], g[:, :, :], bc(cols[:, c0:c0 + KT].unsqueeze(2), [P, KT, 9]),
                                       ALU.mult)

            def copy_ada(n0, iters):
                with v.Fori(0, iters) as i:
                    for q in range(2):
                        v.wait_ge(S("ring_used"), i * SLOTS + (n0 + 2 * q + 2))
                        v.tensor_copy(adas[:, q, :], bk[4 + q][:, :]).then_inc(S("ada_sb"), 1)

            copy_ada(0, N_ADA1 // SLOTS)
            v.wait_ge(S("mod_ps"), N_ADA1 // SLOTS)
            take_mod(bk[3], 0, 16)
            gain(g1, 8, C_GMIX).then_inc(S("mod1"), 1)
            v.wait_ge(S("mod1"), 1)
            norm(0)
            modulate(0, g1, 0)

            v.wait_ge(S("h_prompt"), KT)
            L(v.scalar_tensor_tensor(sel, picks[:, 1, :], small[:, 17:18], picks[:, 0, :], ALU.mult, ALU.add))

            def conv_taps(c):
                step.up(v.tensor_copy(gc[:, c, 0:3], xp[:, c, TP:3 + TP]))
                v.tensor_copy(gc[:, c, 3:27].rearrange("p (b w) -> p b w", b=NB),
                              xp[:, c, 3 + TP:XPW].rearrange("p (b w) -> p b w", w=DT + 3)[:, :, DT:DT + 3])\
                    .then_inc(S("ends_ready"), 1)
                v.wait_ge(S("tap0"), 2 * c + 2)
                cp, cs = cv[:, c % 2, 0:TP], cv[:, c % 2, TP:T].rearrange("p (b t) -> p b t", b=NB)
                for s in range(1, 4):
                    pp, ss = seg(xp[:, c, :], s)
                    w = cols[:, C_CW + 8 * s + c:C_CW + 8 * s + c + 1]
                    step.up(v.scalar_tensor_tensor(cp, pp, w, cp, ALU.mult, ALU.add))
                    ins = v.scalar_tensor_tensor(cs, ss, w, cs, ALU.mult, ALU.add)
                    if s < 3:
                        L(ins)
                ins.then_inc(S("taps"), 1)

            def conv_out(c):
                v.wait_ge(S("taps"), c + 1)
                v.wait_ge(S("ends_ready"), c + 1)
                v.wait_ge(S("conv_gate"), c + 1)
                v.tensor_tensor(xp[:, c, 0:T], cv[:, c % 2, :], ce[:, c % 2, :], ALU.mult).then_inc(S("xa_ready"), 1)

            dt, cs, dw = (rows[0:SH, r, :] for r in range(3))
            raw = dA = rs[0:SH, :]

            v.wait_ge(S("qbd_zero"), 1)
            for n, (kind, t) in enumerate(tiles):
                if 2 <= n <= 9:
                    conv_out(n - 2)
                if 1 <= n <= 8:
                    v.wait_ge(S("ip_dve"), n)
                    v.wait_ge(S("ip_act"), n)
                    conv_taps(n - 1)
                if n == 10:
                    v.wait_ge(S("ip_dve"), 9)
                    v.wait_ge(S("ip_act"), 9)
                    L(v.tensor_scalar(dt, raw, -1.0, None, ALU.mult))
                    v.tensor_tensor(dt, dt, raw, ALU.max).then_inc(S("dt_abs"), 1)
                if n == 11:
                    v.wait_ge(S("dt_ln"), 1)
                    L(v.scalar_tensor_tensor(dt, raw, 0.0, dt, ALU.max, ALU.add))
                    L(v.tensor_scalar(dA, dt, small[0:SH, 16:17], None, ALU.mult))
                    L(v.tensor_tensor_scan(cs, dw, dA, 0.0, ALU.mult, ALU.add))
                    csp, css = cs[:, 0:TP].rearrange("p (c t) -> p c t", c=MT), cs[:, TP:T].rearrange("p (c t) -> p c t", c=NB)
                    dwp, dws = dw[:, 0:TP].rearrange("p (c t) -> p c t", c=MT), dw[:, TP:T].rearrange("p (c t) -> p c t", c=NB)
                    L(v.tensor_tensor(dwp, bc(csp[:, :, P - 1:P], [SH, MT, P]), csp, ALU.subtract))
                    L(v.tensor_tensor(dws, bc(css[:, :, DT - 1:DT], [SH, NB, DT]), css, ALU.subtract))
                    L(v.tensor_copy(small[0:SH, 24:28].unsqueeze(2), csp[:, :, P - 1:P]))
                    v.tensor_copy(small[0:SH, 28:36].unsqueeze(2), css[:, :, DT - 1:DT]).then_inc(S("dt_gap"), 1)
                if n == 12:
                    v.wait_ge(S("dt_w"), 2)
                    v.tensor_tensor(dw, dw, dt, ALU.mult).then_inc(S("rows_ready"), 1)
                if 13 <= n <= 16:
                    v.wait_ge(S("z_gate"), n - 12)
                    v.tensor_tensor(zT[:, n - 13, :], zT[:, n - 13, :], mix[:, n - 9, :], ALU.mult)\
                        .then_inc(S("z_ready"), 1)
                if kind == "v":
                    continue
                bs = bk[2 * (n % 2) + 1]
                sign, count = tile_sign[n]
                v.wait_ge(S(sign), count)
                sv = bs[:, TP - HF:HF].rearrange("p (b t) -> p b t", b=NB)
                if kind == "q":
                    step.up(v.tensor_scalar(qT[:, t, HF:TP], bs[:, 0:TP - HF], HD ** -0.5, None, ALU.mult))
                    L(v.tensor_scalar(qbd[0:64, :, t, 0, :], sv[0:64], HD ** -0.5, None, ALU.mult))
                    ins = v.tensor_scalar(qbd[64:128, :, t, 1, :], sv[64:128], HD ** -0.5, None, ALU.mult)
                elif kind == "k":
                    ins = v.tensor_copy(kT[:, t, HF:T], bs[:, 0:HF])
                elif kind == "d":
                    ins = v.tensor_scalar(rs[0:SH, HF:T], bs[0:SH, 0:HF], small[0:SH, 4:5], None, ALU.add)
                elif kind == "z":
                    ins = v.tensor_copy(zT[:, t, HF:T], bs[:, 0:HF])
                else:
                    step.up(v.tensor_copy(xp[:, t, 3 + HF:3 + TP], bs[:, 0:TP - HF]))
                    ins = v.tensor_copy(seg(xp[:, t, :], 3)[1], sv)
                ins.then_inc(S("ip_dve"), 1)
            v.wait_ge(S("ip_dve"), by_dve[-1])
            v.wait_ge(S("ip_act"), len(tiles))

            v.wait_ge(S("tok_ps"), 1)
            L(v.tensor_copy(tok[:, 0:MT, :, :], bk[6][:, 0:MT * 24].rearrange("p (m r h) -> p m r h", m=MT, r=3)))
            L(v.tensor_copy(tok[0:TS, MT, :, :], bk[6][0:TS, MT * 24:5 * 24].rearrange("p (r h) -> p r h", r=3)))
            v.wait_ge(S("dec_ps"), 1)
            v.tensor_copy(dec[:, :, :], bk[7][:, 0:96].rearrange("p (h c) -> p h c", h=SH)).then_inc(S("dec_sb"), 1)
            v.wait_ge(S("dec_sb"), 1)
            v.wait_ge(S("z_ready"), 4)
            v.wait_ge(S("conv_ps"), 1)
            v.wait_ge(S("tables_stored"), 16)
            L(v.tensor_copy(sout[0:27, 0:512], bk[0][0:27, :]))
            v.tensor_copy(sout[0:27, 512:1024], bk[1][0:27, :]).then_inc(S("conv_rows"), 1)

            for m in range(5):
                n = P if m < MT else TS
                v.wait_ge(S("kout_ps"), m + 1)
                if m >= 2:
                    v.wait_ge(S(f"kout_stored{m % 2}"), 16 * (m // 2))
                v.tensor_copy(kout[0:n, m % 2, :], bk[m % 2][0:n, :]).then_inc(S("kout_ready"), 1)

            v.wait_ge(S("bias_loaded"), 16 * (1 + 2 * H))
            L(v.tensor_copy(wb, wrev[:, :, ::-1]))
            L(v.tensor_copy(nearb[:, 0:DT], nearr[:, 0:DT][:, ::-1]))
            L(v.tensor_copy(nearb[:, DT:NBIAS], nearr[:, DT:NBIAS][:, ::-1]))
            L(v.tensor_tensor(newb.rearrange("p b (c k) -> p (b c) k", c=NB), newb.rearrange("p b (c k) -> p (b c) k", c=NB),
                              bc(nearb[:, 0:DT].unsqueeze(1), [P, NB * NB, DT]), ALU.add))

            NU = 16

            def att_max(x):
                h, qb = x // MT, x % MT
                nk = (qb + 1) * P
                nb_ = min(2 * P, nk)
                v.wait_ge(S("att_s"), x + 1)
                for j in range(2):
                    s = bk[2 + 2 * (x % 2) + j]
                    near = s[:, nk - nb_:nk]
                    step.up(v.tensor_tensor(near, near, wb[:, h, 2 * P - nb_:2 * P], ALU.add))
                v.wait_ge(step.sem, step.n)
                for j in range(2):
                    s = bk[2 + 2 * (x % 2) + j]
                    m_ = small[:, 36 + 2 * (x % 2) + j:37 + 2 * (x % 2) + j]
                    L(v.tensor_reduce(m_, s[:, 0:nk], AX, ALU.max))
                    v.tensor_scalar(m_, m_, -1.0, None, ALU.mult).then_inc(S("att_m"), 1)

            def att_combine(x):
                nk = (x % MT + 1) * P
                v.wait_ge(S("att_exp"), 2 * x + 2)
                r = small[:, 44 + 2 * (x % 2):46 + 2 * (x % 2)]
                L(v.reciprocal(r, small[:, 40 + 2 * (x % 2):42 + 2 * (x % 2)]))
                L(v.tensor_tensor(r[:, 1:2], r[:, 1:2], small[:, 17:18], ALU.mult))
                p0, p1 = pj[:, x % 2, 0, 0:nk], pj[:, x % 2, 1, 0:nk]
                L(v.tensor_scalar(p0, p0, r[:, 0:1], None, ALU.mult))
                v.scalar_tensor_tensor(p0, p1, r[:, 1:2], p0, ALU.mult, ALU.add).then_inc(S("att_p"), 1)

            def att_out(h):
                v.wait_ge(S("att_v"), MT * (h + 1))
                v.tensor_copy(mix[:, h, 0:TP], bk[0][:, :]).then_inc(S("att_o"), 1)

            for x in range(NU + 3):
                if x >= 6 and (x - 6) % 4 == 0:
                    att_out((x - 6) // 4)
                if x < NU:
                    att_max(x)
                if 1 <= x <= NU:
                    att_combine(x - 1)
                if x >= 2 and x % 2 == 0 and x <= NU:
                    v.wait_ge(S("ring_used"), I_ADA2 + x)
                    v.tensor_copy(adas2[:, x // 2 - 1, :], bk[1][:, :]).then_inc(S("ada_sb"), 1)
            v.wait_ge(S("att_o"), 4)
            for h in range(H):
                v.wait_ge(S("att_r"), h + 1)
                L(v.tensor_tensor(mix[:, h, 0:TP], mix[:, h, 0:TP], hT[:, 4 + h, 0:TP], ALU.mult))
                v.tensor_scalar(mix[:, h, 0:TP], mix[:, h, 0:TP], cols[:, C_SUB:C_SUB + 1], 0.8, ALU.mult, ALU.mult)\
                    .then_inc(S("att_n"), 1)
            v.wait_ge(S("att_n"), H)
            v.wait_ge(S("mod_ps"), N_ADA1 // SLOTS + 1)
            take_mod(bk[1], 16, 32)
            gain(g2, 32, C_GFFN).then_inc(S("mod2"), 1)
            v.wait_ge(S("mod2"), 1)

            v.wait_ge(S("xa_ready"), 8)
            for m in range(5):
                n = P if m < MT else TS
                v.wait_ge(S("xtk_ps"), m + 1)
                src = bk[m % 2][0:n, :].rearrange("p (h q) -> p h q", h=SH)
                L(v.tensor_tensor(xdt[0:n, m, :].rearrange("p (h q) -> p h q", h=SH), src,
                                  bc(tok[0:n, m, 0, :].unsqueeze(2), [n, SH, SP_]), ALU.mult))
                dst = xw[0:n, m, :] if m < MT else xws[:, :]
                v.tensor_tensor(dst.rearrange("p (h q) -> p h q", h=SH), src,
                                bc(tok[0:n, m, 2, :].unsqueeze(2), [n, SH, SP_]), ALU.mult).then_inc(S("xtk_v"), 1)
            v.wait_ge(S("xtk_v"), 5)
            v.wait_ge(S("st_ps"), 1)
            L(v.tensor_copy(prev[:, 0, :], bk[0][:, :]))
            for c in range(1, MT):
                v.wait_ge(S("st_ps"), c + 1)
                L(v.tensor_tensor(prev[:, c, :].rearrange("p (h q) -> p h q", h=SH),
                                  prev[:, c - 1, :].rearrange("p (h q) -> p h q", h=SH),
                                  bc(dec[:, :, c:c + 1], [P, SH, SP_]), ALU.mult))
                ins = v.tensor_tensor(prev[:, c, :], prev[:, c, :], bk[c][:, :], ALU.add)
                if c < MT - 1:
                    L(ins)
            ins.then_inc(S("prev_done"), 1)

            v.wait_ge(S("prev_done"), 1)
            v.wait_ge(S("final_ps"), 1)
            v.tensor_copy(rs[:, 0:512], bk[3][:, :]).then_inc(S("final_ready"), 1)
            for h in range(SH + 2):
                if h < SH:
                    v.wait_ge(S("cs_bc"), h + 1)
                    if h >= 2:
                        v.wait_ge(S("y_ps"), h - 1)
                    for c in range(MT):
                        v.scalar_tensor_tensor(lg[:, h % 2, c * P:(c + 1) * P], bk[h % 2][:, c * P:(c + 1) * P],
                                               tok[:, c, 1, h:h + 1], cst[:, K_NM:K_NM + P], ALU.subtract, ALU.add)\
                            .then_inc(S("seg"), 1)
                    v.scalar_tensor_tensor(lg[0:TS, h % 2, TP:T], bk[2 + h % 2][0:TS, 0:TS], tok[0:TS, MT, 1, h:h + 1],
                                           cst[0:TS, K_NMS:K_NMS + TS], ALU.subtract, ALU.add).then_inc(S("seg"), 1)
                if 1 <= h <= SH:
                    k, g = h - 1, (h - 1) // 4
                    v.wait_ge(S("cb_sb"), 3)
                    v.wait_ge(S("lexp"), k + 1)
                    step.up(v.tensor_tensor(lg[:, k % 2, 0:TP], lg[:, k % 2, 0:TP], cbT[:, g, 0:TP], ALU.mult))
                    step.up(v.tensor_tensor(lg[0:TS, k % 2, TP:T], lg[0:TS, k % 2, TP:T], cbT[0:TS, g, TP:T], ALU.mult))
                    v.tensor_tensor(ceb[:, k % 2, :], ceb[:, k % 2, :], xp[:, 6 + g, 0:T], ALU.mult)\
                        .then_inc(S("g_ready"), 1)
                if h >= 2 and h % 2 == 1:
                    t = (h - 2) // 2
                    v.wait_ge(S("y_ps"), 2 * t + 2)
                    skip = small[:, 20 + t:21 + t]
                    L(v.scalar_tensor_tensor(mix[:, 4 + t, 0:TP], xp[:, t, 0:TP], skip, bk[4 + t % 2][:, :],
                                             ALU.mult, ALU.add))
                    v.scalar_tensor_tensor(mix[:, 4 + t, TP:T], xp[:, t, TP:T], skip, bk[6 + t % 2][:, 0:TS],
                                           ALU.mult, ALU.add).then_inc(S("y_sb"), 1)
                    v.wait_ge(S("y_sb"), t + 1)
                    v.tensor_tensor(mix[:, 4 + t, :], mix[:, 4 + t, :], zT[:, t, :], ALU.mult)\
                        .then_inc(S("y_gated"), 1)
            v.wait_ge(S("y_gated"), 4)
            v.wait_ge(step.sem, step.n)
            for g in range(GR):
                ins = v.tensor_tensor(bblk[0:TS, g, :, :], bc(btk[0:TS, MT, g * NS:(g + 1) * NS].unsqueeze(1), [TS, NB, NS]),
                                      bc(cst[0:TS, K_BLK:K_BLK + NB].unsqueeze(2), [TS, NB, NS]), ALU.mult)
                if g == 0:
                    L(ins)
            ins.then_inc(S("bblk_ready"), 1)
            for r in range(2):
                half = slice(64 * r, 64 * r + 64)
                L(v.tensor_copy(hdec[half, :, :], dec[half, r:SH:2, MT:MT + NB]))
            for t in range(4):
                for q in range(2):
                    v.wait_ge(S("ssm_ps"), 2 * t + q + 1)
                    for j in range(4):
                        b = 4 * q + j
                        ins = v.scalar_tensor_tensor(h0[:, b, t, :], h0[:, b, t, :], hdec[:, t, b:b + 1],
                                                     bk[4 + q][:, j * NS:(j + 1) * NS], ALU.mult, ALU.add)
                        if j < 3:
                            step.up(ins)
                    ins.then_inc(S("ssm_sb"), 1)
            v.wait_ge(step.sem, step.n)
            v.wait_ge(S("ssm_sb"), 8)
            v.memset(small[:, 61:62], 0.0).then_inc(S("ssm_ready"), 1)
            for g in range(GR):
                v.wait_ge(S("ssd_r"), g + 1)
                for t in (2 * g, 2 * g + 1):
                    L(v.scalar_tensor_tensor(mix[:, 4 + t, :], mix[:, 4 + t, :], cols[:, C_SSD + t:C_SSD + t + 1],
                                             hT[:, 4 + g, :], ALU.mult, ALU.mult))

            L(v.memset(qcur, 0.0))
            L(v.memset(bk[5][:, :], 0.0))
            v.memset(small[:, 61:62], 0.0).then_inc(S("dec_start"), 1)
            chain = Tally(S("dec_step"))

            def take_scores(g, n):
                v.wait_ge(S("s_ps"), n + (g + 1))
                bank, dst = bk[2 + g % 2], sc[:, g * 512:(g + 1) * 512]
                if g < 7:
                    chain.up(v.tensor_reduce(small[:, 36 + g:37 + g], bank[:, :], AX, ALU.max))
                    v.tensor_copy(dst, bank[:, :]).then_inc(S("s_sb"), 1)
                else:
                    chain.up(v.tensor_tensor(dst[:, 384:512], bank[:, 384:512], nearb[:, DT:NBIAS], ALU.add))
                    v.tensor_copy(dst[:, 0:384], bank[:, 0:384]).then_inc(S("s_sb"), 1)
                    v.wait_ge(S("s_sb"), n + 8)
                    v.wait_ge(chain.sem, chain.n)
                    link(v, v.tensor_reduce(small[:, 43:44], dst, AX, ALU.max), chain)

            def take_new(b, n):
                v.wait_ge(S("new_ps"), n + 1)
                link(v, v.tensor_tensor(sc[:, NK:NK + TS], bk[7][:, 0:TS],
                                        newb[:, bass.ds(b, 1), :].rearrange("p a c -> p (a c)"), ALU.add), chain)
                v.tensor_reduce(small[:, 44:45], sc[:, NK:NK + TS], AX, ALU.max).then_inc(S("new_sb"), 1)

            def largest(b):
                v.wait_ge(S("new_sb"), b + 1)
                link(v, v.tensor_reduce(small[:, 45:46], small[:, 36:45], AX, ALU.max), chain)
                v.tensor_scalar(small[:, 46:47], small[:, 45:46], -1.0, None, ALU.mult).then_inc(S("max_ready"), 1)

            def copy_p(groups, g):
                v.wait_ge(S("pt_ps"), groups + (g + 1))
                bank = bk[4 + 2 * (g % 2)]
                if g < 8:
                    ins = v.tensor_copy(pT[:, g % 2, :], bank[:, :])
                else:
                    ins = v.tensor_copy(pT[0:TS, 0, 0:P], bank[0:TS, 0:P])
                ins.then_inc(S("pt_sb"), 1)

            def inverse(i):
                v.wait_ge(S("exp_done"), i * 4 + 4)
                link(v, v.tensor_reduce(small[:, 54:55], small[:, 50:54], AX, ALU.add), chain)
                link(v, v.reciprocal(small[:, 55:56], small[:, 54:55]), chain)

            def finish(i):
                v.wait_ge(S("o_ps"), i + 1)
                v.tensor_scalar(on, bk[5][:, 0:P], small[:, 55:56], None, ALU.mult).then_inc(S("on_ready"), 1)

            def take_out(i):
                v.wait_ge(S("od_ps"), i + 1)
                v.tensor_copy(mix[:, 0:H, bass.ds(TP + i * DT, DT)],
                              bk[7][:, P:P + NB * H].rearrange("p (h t) -> p h t", h=H)).then_inc(S("od_sb"), 1)

            for g in range(8):
                take_scores(g, 0)
                if g == 3:
                    take_new(0, 0)
            largest(0)
            v.memset(small[:, 61:62], 0.0).then_inc(S("od_sb"), 1)
            v.wait_ge(S("od_sb"), 1)
            base = chain.n
            per = sum((2 if w == "K7" else 1) if w[0] == "K" else 0 for w in BODY) + 1 + 1 + 2
            with v.Fori(0, NB - 1) as i:
                chain.n = i * per + base
                for what in BODY:
                    g = int(what[1:])
                    if what == "K0":
                        inverse(i)
                    if what[0] == "K":
                        take_scores(g, i * 8 + 8)
                    elif g < 7:
                        copy_p(i * 9, g + 1)
                    if what == "K1":
                        copy_p(i * 9, 0)
                    if what == "V6":
                        copy_p(i * 9, 8)
                    if what == "K3":
                        take_new(i + 1, i + 1)
                    if what == "V7":
                        finish(i)
                largest(i + 1)
                take_out(i)
            chain.n = base + per * (NB - 1)
            inverse(NB - 1)
            for g in range(9):
                copy_p(9 * (NB - 1), g)
            finish(NB - 1)
            v.wait_ge(S("od_ps"), NB)
            v.tensor_copy(mix[:, 0:H, T - DT:T], bk[7][:, P:P + NB * H].rearrange("p (h t) -> p h t", h=H))\
                .then_inc(S("od_sb"), 1)
            v.wait_ge(S("od_sb"), NB + 1)
            v.memset(small[:, 61:62], 0.0).then_inc(S("od_ready"), 1)
            v.wait_ge(S("ssm_stored"), 16 * NB)
            v.wait_ge(S("od_r"), 1)
            r4 = hT[:, 1, 0:H * TS].rearrange("p (h t) -> p h t", h=H)
            L(v.tensor_tensor(mix[:, 0:H, TP:T], mix[:, 0:H, TP:T], r4, ALU.mult))
            v.tensor_scalar(mix[:, 0:H, TP:T], mix[:, 0:H, TP:T], cols[:, C_SUB:C_SUB + 1], 0.8, ALU.mult, ALU.mult)\
                .then_inc(S("mix_ready"), 1)
            take_x(1)
            v.wait_ge(S("xt_a"), 10)
            v.wait_ge(S("xt_v"), 10)

            for x in range(KT):
                if x % 2 == 0:
                    v.wait_ge(S("op_ps"), x // 2 + 1)
                else:
                    v.wait_ge(S("ring_used"), I_OUT + x // 2 + 1)
                bp, bs = bk[2 * (x % 2)], bk[2 * (x % 2) + 1]
                ga = mod[:, 16 + x, :]
                xs = xT[:, x, TP:T].rearrange("p (b t) -> p b t", b=NB)
                step.up(v.scalar_tensor_tensor(xT[:, x, 0:HF], bp[:, 0:HF], ga[:, 0:1], xT[:, x, 0:HF], ALU.mult, ALU.add))
                step.up(v.scalar_tensor_tensor(xT[:, x, HF:TP], bs[:, 0:TP - HF], ga[:, 0:1], xT[:, x, HF:TP],
                                               ALU.mult, ALU.add))
                g8 = rs[:, 0:TS].rearrange("p (b t) -> p b t", b=NB)
                L(v.tensor_tensor(g8, bs[:, TP - HF:HF].rearrange("p (b t) -> p b t", b=NB),
                                  bc(ga[:, 1:9].unsqueeze(2), [P, NB, DT]), ALU.mult))
                v.tensor_tensor(xs, xs, g8, ALU.add).then_inc(S("op_sb"), 1)
                v.wait_ge(S("op_sb"), x + 1)
            v.memset(small[:, 61:62], 0.0).then_inc(S("x1_ready"), 1)
            norm(1)
            modulate(1, g2, 24)
            for k in range(2):
                v.memset(small[:, 61:62], 0.0).then_inc(S("up_sb"), 1)
                v.wait_ge(S("up_sb"), k + 1)
            with v.Fori(0, 4) as i:
                for x in range(8):
                    if x % 2 == 0:
                        v.wait_ge(S("up_ps"), i * 4 + (x // 2 + 1))
                    else:
                        v.wait_ge(S("ring_used"), i * 4 + (I_UP + x // 2 + 1))
                    tile = u[:, bass.ds(i * 8 + x, 1), :].rearrange("p a t -> p (a t)")
                    for half in range(2):
                        src = bk[2 * (x % 2) + half][:, 0:HF]
                        ins = v.tensor_scalar(tile[:, half * HF:(half + 1) * HF], src, 0.0, None, ALU.max)
                    ins.then_inc(S("up_sb"), 1)
                    v.wait_ge(S("up_sb"), i * 8 + (x + 3))
                    v.tensor_tensor(tile, tile, tile, ALU.mult).then_inc(S("u_ready"), 1)
            v.memset(small[:, 61:62], 0.0).then_inc(S("down_sb"), 1)
            v.wait_ge(S("down_sb"), 1)
            v.memset(small[:, 61:62], 0.0).then_inc(S("down_sb"), 1)
            down = Tally(S("down_step"))
            with v.Fori(0, 4) as i:
                down.n = i * 6
                for t in range(2):
                    if t == 0:
                        v.wait_ge(S("down_ps"), i + 1)
                    else:
                        v.wait_ge(S("ring_used"), i * 4 + (I_DOWN + 4))
                    bp, bs = bk[2 * t], bk[2 * t + 1]
                    tile = xT[:, bass.ds(i * 2 + t, 1), :].rearrange("p a t -> p (a t)")
                    ga = mod[:, bass.ds(i * 2 + (40 + t), 1), :].rearrange("p a c -> p (a c)")
                    down.up(v.scalar_tensor_tensor(tile[:, 0:HF], bp[:, 0:HF], ga[:, 0:1], tile[:, 0:HF],
                                                   ALU.mult, ALU.add))
                    down.up(v.scalar_tensor_tensor(tile[:, HF:TP], bs[:, 0:TP - HF], ga[:, 0:1], tile[:, HF:TP],
                                                   ALU.mult, ALU.add))
                    g8 = rs[:, t * TS:(t + 1) * TS].rearrange("p (b t) -> p b t", b=NB)
                    link(v, v.tensor_tensor(g8, bs[:, TP - HF:HF].rearrange("p (b t) -> p b t", b=NB),
                                            bc(ga[:, 1:9].unsqueeze(2), [P, NB, DT]), ALU.mult), down)
                    xs = tile[:, TP:T].rearrange("p (b t) -> p b t", b=NB)
                    v.tensor_tensor(xs, xs, g8, ALU.add).then_inc(S("down_sb"), 1)
            v.wait_ge(S("down_sb"), 10)
            v.memset(small[:, 61:62], 0.0).then_inc(S("x2_ready"), 1)
            norm(2)
            for m in range(5):
                n = P if m < MT else TS
                v.wait_ge(S("yt_ps"), 2 * m + 2)
                if m >= 2:
                    v.wait_ge(S(f"y_stored{m % 2}"), 16 * (m // 2))
                v.tensor_copy(ytok[0:n, m % 2, TP:D], bk[(2 * m + 1) % 4][0:n, :]).then_inc(S("yt_v"), 1)


N_PAR = 24
N_POOL = 320


def shape_constants():
    import numpy as np

    c = np.zeros((P, K_N), np.float32)
    c[:, K_ID:K_ID + P] = np.eye(P)
    c[:, K_ONE:K_ONE + P] = 1
    s, l = np.meshgrid(np.arange(P), np.arange(P), indexing="ij")
    c[:, K_NM:K_NM + P] = np.where(s <= l, 0, BIG)
    s, l = s[:TS, :TS], l[:TS, :TS]
    c[:TS, K_NMS:K_NMS + TS] = np.where((s <= l) & (s // DT == l // DT), 0, BIG)
    c[:TS, K_BLK:K_BLK + NB] = np.arange(TS)[:, None] // DT == np.arange(NB)
    q = np.arange(NB * H)
    row = 32 * (q // DT) + q % DT
    for r in range(4):
        c[32 * r + np.arange(9), K_SUM + np.arange(9)] = 1
    picks = np.zeros((P, 2, NB * H), np.float32)
    picks[row, 0, q] = 1
    picks[row + DT, 1, q] = 1
    r, b, k = np.meshgrid(np.arange(P), np.arange(NB), np.arange(TS), indexing="ij")
    seen = (k // DT == b) & (k % DT <= r % DT) | (r % 32 >= 2 * DT)
    new = np.where(seen, 0, BIG).astype(np.float32).reshape(P, NB * TS)
    d = np.arange(TAB) - OFF
    n = np.maximum(d, 0)
    lt = np.log(np.maximum(n, 1).astype(np.float32) / np.float32(16)) / np.float32(np.log(8.0)) * np.float32(16)
    bucket = np.where(n < 16, n, np.minimum(16 + lt.astype(np.int32), 31))
    hot = np.zeros((33, 2, TAB), np.float32)
    hot[:32, 0] = (np.arange(32)[:, None] == bucket).astype(np.float32)
    hot[31, 0] -= 1
    hot[:, 0, d < 0] = 0
    hot[32, 0, d < 0] = BIG
    far = 2 * P - 1 + OFF
    hot[:, 1, 0:far + 1] = hot[:, 0, far::-1]
    starts = np.ones((SH, T), np.float32)
    starts[:, 0:TP:P] = 0
    starts[:, TP:T:DT] = 0
    return c, hot, starts, new, picks


_OUTS = [("y_p", (TP, D)), ("y_s", (TS, D)), ("k_p", (TP, 512)), ("v_p", (TP, 512)), ("conv_p", (3, CONV)),
         ("ssm_p", (512, NS)), ("k_s", (TS, 512)), ("v_s", (TS, 512)), ("conv_s", (NB * 3, CONV)),
         ("ssm_s", (NB * 512, NS))]
_SHAPES = [(1, TP, D), (NB, DT, D), (1, 1, TP, H, 2, HD), (1, 1, TP, H, VD), (1, 1, 3, CONV), (1, 1, SH, SP_, NS),
           (1, NB, DT, H, 2, HD), (1, NB, DT, H, VD), (1, NB, 3, CONV), (1, NB, SH, SP_, NS)]


def kernel(**inputs):
    import concourse.bacc as _bacc
    import numpy as _np
    from concourse.bass_utils import run_bass_kernel_spmd as _run

    nc = _bacc.Bacc("TRN2", target_bir_lowering=False, num_devices=1)
    arrays = {k: _np.ascontiguousarray(v) for k, v in inputs.items()}
    arrays["cache_k"] = arrays["cache_k"].reshape(N_POOL, PAGE, 512)
    arrays["cache_v"] = arrays["cache_v"].reshape(N_POOL, PAGE, 512)
    arrays["shape_consts"], arrays["shape_hot"], arrays["shape_starts"], arrays["shape_new"], arrays["shape_picks"] = shape_constants()
    arrays = {f"in_{k}": v for k, v in arrays.items()}
    a = {k[3:]: nc.dram_tensor(k, v.shape, mybir.dt.from_np(v.dtype), kind="ExternalInput").ap()
         for k, v in arrays.items()}
    o = {k: nc.dram_tensor(f"out_{k}", s, F32, kind="ExternalOutput").ap() for k, s in _OUTS}
    scratch = nc.dram_tensor("bias_tables", (2, H, TAB), F32, kind="Internal").ap()
    program(nc, a, o, scratch)
    r = _run(nc, [arrays], core_ids=[0])
    return tuple(r.results[0][f"out_{k}"].reshape(s) for (k, _), s in zip(_OUTS, _SHAPES))
```

```python
from contextlib import ExitStack

import concourse.bass as bass
from concourse import mybir

F32 = mybir.dt.float32
F32R = mybir.dt.float32r
I32 = mybir.dt.int32
ALU = mybir.AluOpType
ACT = mybir.ActivationFunctionType
AX = mybir.AxisListType.X
P = 128

D = 1024
KT = D // P
TP, NB, DT = 512, 8, 8
TS = NB * DT
T = TP + TS
HF = T // 2
MT = TP // P
PAGES, PAGE = 32, 128
H, HD, VD = 4, 64, 128
SH, SP_, NS, GR = 8, 64, 128, 2
CONV = SH * SP_ + 2 * GR * NS
XT_, BT_ = 4, 4
NF = 4 * D // P
TAB = 384
OFF = 127
BIG = -1.0e30
EPS = 1e-6
IT = 256
IP = 4
SLOTS = 4
SLOT = KT * IT
XPW = 3 + TP + NB * (DT + 3)

C_BADA, C_GMIX, C_GFFN, C_GFIN, C_CB, C_CW, C_SSD, C_SUB = 0, 48, 56, 64, 72, 80, 112, 116
NROW = 117
K_ID, K_ONE, K_NM, K_NMS, K_BLK = 0, P, 2 * P, 3 * P, 3 * P + TS
K_SUM = K_BLK + NB
K_N = K_SUM + 9
NBIAS = DT + PAGE


class Tally:

    def __init__(self, sem):
        self.sem, self.n = sem, 0

    def up(self, ins):
        ins.then_inc(self.sem, 1)
        self.n = self.n + 1


def link(eng, ins, tally):
    tally.up(ins)
    eng.wait_ge(tally.sem, tally.n)


def program(nc, a, o, scratch):
    ctx = ExitStack()
    with ctx:
        def sb(name, shape):
            return ctx.enter_context(nc.sbuf_tensor(name, shape, F32))

        sems = {}

        def S(name):
            if name not in sems:
                sems[name] = ctx.enter_context(nc.semaphore(name))
            return sems[name]

        SETUP_ACT = {"silu_exp": 1, "alog_exp": 2, "lam_exp": 3}
        SETUP_DVE = {"silu_rows": 1, "ct_ready": 2, "lam_prod": 3, "lam_ready": 4, "tables_ready": 5, "prefix_ready": 6}
        SETUP_PS = {"ct_ps": 1, "cols_ps": 2, "lam_ps": 3, "tables_ps": 4, "cs_ps": 5}
        SSD_PS = {"tok_ps": 1, "dec_ps": 2, "final_ps": 3}

        def twin(name, shape):
            with ExitStack() as place:
                rounded = place.enter_context(nc.sbuf_tensor(name + "_r", shape, F32R))
            return sb(name, shape), rounded

        ring, ring_r = twin("ring", [P, SLOTS * SLOT])
        xT, xT_r = twin("xT", [P, KT, T])
        hT, hT_r = twin("hT", [P, KT, T])
        mix, mix_r = twin("mix", [P, KT, T])
        cst = sb("cst", [P, K_N])
        cols = sb("cols", [P, NROW])
        mod = sb("mod", [P, 48, 9])
        g1 = sb("g1", [P, KT, 9])
        g2 = sb("g2", [P, KT, 9])
        rs = sb("rs", [P, T])
        cT = sb("cT", [P, KT, 9])
        small = sb("small", [P, 64])
        rows = sb("rows", [P, 3, T])
        ptab = rows[32:33, :, :].rearrange("p r t -> p (r t)")[:, 0:NB * PAGES].bitcast(I32)
        tok = sb("tok", [P, 5, 3, SH])
        dec = sb("dec", [P, SH, MT + NB])
        arena, arena_r = twin("arena", [P, 27230])

        def at(off, *shape, parts=P, of=arena):
            n = 1
            for s in shape:
                n *= s
            v = of[0:parts, off:off + n]
            if len(shape) == 2:
                v = v.rearrange("p (a b) -> p a b", b=shape[1])
            if len(shape) == 3:
                v = v.rearrange("p (a b c) -> p a b c", b=shape[1], c=shape[2])
            if len(shape) == 4:
                v = v.rearrange("p (a b c d) -> p a b c d", b=shape[1], c=shape[2], d=shape[3])
            return v

        def at_r(off, *shape):
            return at(off, *shape, of=arena_r)

        kT = at(0, H, T)
        vtk = at(2304, 5, H * VD)
        zT = at(4864, 4, T)
        qbd = at(7168, NB, H, 2, DT)
        newb = at(7680, NB, TS)
        xp = at(8448, 8, XPW)
        qT = at(13272, H, TP)
        TMP = 15320
        xtok = at(TMP, 5, D)
        crow = at(TMP + 5120, D)
        ctmp = at(TMP + 6144, D)
        scr = at(TMP + 7168, D)
        brow = at(TMP + 8192, 2, TAB)
        hot = at(TMP + 8960, 2, TAB)
        vrow = at(TMP + 9728, P)
        wdt = at(TMP + 9856, KT, SH)
        picks = at(TMP + 10944, 2, NB * H)
        adas = at(TMP + 9920, 2, 2 * IT)
        wrev = at(TMP, H, 2 * P)
        wb = at(TMP + 1024, H, 2 * P)
        pj = at(TMP + 2048, 2, 2, TP)
        pts = at(TMP + 4096, 2, TP)
        kout = at(TMP + 5120, 2, TP)
        adas2 = at(TMP + 6144, 8, 2 * IT)
        kouts = [kout[:, 0, :], kout[:, 1, :]] + [adas2[:, k, :] for k in (5, 6, 7)]
        nearr = at(TMP + 11300, NBIAS)
        cv = at(TMP + 5120, 2, T)
        ce = at(TMP + 6272, 2, T)
        gc = at(TMP + 7424, 8, 27)
        sout = at(TMP + 10240, D)
        xdt = at(TMP, 5, SH * SP_)
        xw = at(TMP + 2560, 5, SH * SP_)
        prev = at(TMP + 5120, 4, SH * SP_)
        btk = at(TMP + 7168, 5, GR * NS)
        cbT = at(TMP + 8448, GR, T)
        lg = at(13272, 3, T)
        ceb = at(TMP + 9600, 3, T)
        h0 = xT[:, :, :].rearrange("p a b -> p (a b)")[:, 0:4096].rearrange("p (b t q) -> p b t q", b=NB, t=4)
        h0T = hT[:, :, :].rearrange("p a b -> p (a b)")[:, 0:4096].rearrange("p (b t q) -> p b t q", b=NB, t=4)
        bblk = at(TMP + 9600, GR, NB, NS)
        xws = xw[0:TS, MT, :]
        hdec = sb("hdec", [P, 4, NB])
        NK = PAGES * PAGE
        DEC = 8448
        kts = at(DEC, 2, H, IP * PAGE)
        sc = at(DEC + 4096, NK + TS)
        pr = at(DEC + 8256, NK + TS)
        pT = at(DEC + 12416, 2, IP * P)
        qcur = at(DEC + 13440, H, 32)
        on = at(DEC + 13568, P)
        nearb = mod[:, 0:16, :].rearrange("p a b -> p (a b)")[:, 0:NBIAS]
        sel = g1[:, :, :].rearrange("p a b -> p (a b)")[:, 0:NB * H]
        xtok2 = [at(4864, 2, TP), at(4864 + D, 2, TP), kT[:, 0:2, 0:TP], kT[:, 2:4, 0:TP], vtk[:, 0:2, :]]
        UH = NF // 2
        u = at(0, UH, T)
        ul, uh = at_r(0, UH, T), at_r(UH * T, UH, T)
        hh_ffn = at_r(2 * UH * T, KT, T)
        sq = at(2 * UH * T, KT, T)
        wh_ffn = at_r(2 * UH * T + KT * T, 2, SLOT)
        hh_in, hl = xT_r, hT_r
        wh_in = [at_r(TMP + 2048, SLOT), at_r(TMP + 7640, SLOT)]
        wdth, wdtl = at_r(TMP + 11440, KT, SH), at_r(TMP + 9856, KT, SH)
        mh, ml = hT_r, mix_r
        odt = at(14000, 2, H * TS)
        ytok = at(0, 2, D)

        ident = cst[:, K_ID:K_ID + P]
        ones = cst[:, K_ONE:K_ONE + P]
        bk = [ctx.enter_context(nc.psum_tensor(f"bank{i}", [P, 512], F32)) for i in range(8)]

        def norm_banks(k):
            return (bk[0], bk[1]) if k == 2 else (bk[6], bk[7])

        def ffn_banks(ph, c, t):
            b = 4 * ph if c is None else 4 * ((c + 1 + ph) % 2)
            return bk[b + 2 * t], bk[b + 2 * t + 1]

        n_in = 12
        N_ADA1, N_ADA2 = 8, 16
        N_EARLY = 4
        I_IN = N_ADA1
        I_ADA2 = I_IN + n_in
        I_DEC = I_ADA2 + N_ADA2
        BODY = ["K0", "K1", "V0", "K2", "V1", "K3", "V2", "K4", "V3", "K5", "V4", "K6", "V5", "V6", "K7", "V7"]
        STEPS = ["T0", "T1", "S0", "P0", "V0", "P1", "S1", "T2", "V1", "P2", "S2", "T3", "V2", "P3", "S3", "T4", "V3",
                 "P4", "S4", "T5", "V4", "P5", "S5", "T6", "V5", "P6", "S6", "V6", "P7", "P8", "T7", "V7", "S7"]
        I_LOOP = I_DEC + 8
        I_LAST = I_LOOP + 16 * (NB - 1)
        I_OUT = I_LAST + 8
        I_UP = I_OUT + 4
        N_FFN = 32
        ring_sem = [S(f"ring_loaded{k}") for k in range(SLOTS)]

        def landed(n):
            def upto(lo, hi, inc):
                hi = min(hi, n + 1)
                return sum(inc for m in range(lo, hi) if m % SLOTS == n % SLOTS) if hi > lo else 0
            return upto(0, I_DEC, 16) + upto(I_DEC, I_OUT, 16 * IP) + upto(I_OUT, I_UP + N_FFN + SLOTS, 16)

        def slot_r(n):
            return ring_r[:, (n % SLOTS) * SLOT:(n % SLOTS + 1) * SLOT]

        def slot(n):
            return ring[:, (n % SLOTS) * SLOT:(n % SLOTS + 1) * SLOT]

        def split(n):
            return n - I_IN if n < I_OUT else n_in + n - I_OUT

        def high(n):
            return wh_in[n % 2] if n < I_OUT else wh_ffn[:, n % 2, :]

        def split_high(act, n, i=0, step=0):
            arrived(act, n, i, step)
            if n >= I_OUT + 2 or I_IN + 2 <= n < I_OUT:
                act.wait_ge(S("ring_used"), i * step + (n - 1))
            nc.scalar.activation(high(n), slot(n), ACT.Copy).then_inc(S("w_high"), 1)

        def split_low(v, n, i=0, step=0):
            v.wait_ge(S("w_high"), i * step + (split(n) + 1))
            nc.vector.tensor_tensor(slot_r(n), slot(n), high(n), ALU.subtract).then_inc(S("w_low"), 1)

        def parts(pe, n, i=0, step=0):
            pe.wait_ge(S("w_low"), i * step + (split(n) + 1))
            return [w.rearrange("p (k c) -> p k c", k=KT) for w in (high(n), slot_r(n))]

        def arrived(eng, n, i=0, step=0):
            per = landed(n + step) - landed(n) if step else 0
            eng.wait_ge(ring_sem[n % SLOTS], i * per + landed(n) if step else landed(n))

        def rows4(dram, r0, nk, c0, nc_):
            return dram[r0:r0 + nk * P, c0:c0 + nc_].rearrange("(k p) c -> p k c", p=P)

        def seg(v, s):
            return v[:, s:s + TP], v[:, 3 + TP:XPW].rearrange("p (b w) -> p b w", w=DT + 3)[:, :, s:s + DT]

        sfin = rs[:, 0:512].rearrange("p (t n) -> p t n", t=4)
        block = ctx.enter_context(nc.Block())

        @block.sync
        def _(sp):
            def free(n, i=None, step=0):
                if i is not None:
                    sp.wait_ge(S("ring_used"), i * step + (n - SLOTS + 1))
                elif n >= SLOTS:
                    sp.wait_ge(S("ring_used"), n - SLOTS + 1)

            def load(n, src, nk=KT, i=None, step=0):
                free(n, i, step)
                sp.dma_start(slot(n).rearrange("p (k c) -> p k c", k=nk), src).then_inc(ring_sem[n % SLOTS], 16)

            for dst, src in ((crow[0:1, :], a["c_prompt"]), (crow[1:9, :], a["c_sample"]), (cst[:, :], a["shape_consts"])):
                sp.dma_start(dst, src).then_inc(S("cond_loaded"), 16)
            params = [(newb[:, :, :].rearrange("p b k -> p (b k)"), a["shape_new"]), (picks, a["shape_picks"]),
                      (ptab, a["page_table"].rearrange("(a b) p -> a (b p)", a=1))]
            for c0, n, src in ((C_BADA, 48, a["b_ada"][0]), (C_GMIX, 8, a["g_mix"][0]), (C_GFFN, 8, a["g_ffn"][0]),
                               (C_GFIN, 8, a["g_final"]), (C_CB, 8, a["conv_b"][0]), (C_SSD, 4, a["ssd_norm_g"][0]),
                               (C_SUB, 1, a["subln_g"][0])):
                params.append((vrow[c0:c0 + n, :], src.rearrange("(r c) -> r c", c=P)))
            params.append((vrow[C_CW:C_CW + 32, :], a["conv_w"][0].rearrange("i (r c) -> (i r) c", c=P)))
            for j, name in enumerate(("lam_q1", "lam_q2", "lam_k1", "lam_k2")):
                params.append((small[0:HD, j:j + 1], a[name].rearrange("a b -> b a")))
            for j, name in enumerate(("dt_bias", "a_log", "d_skip")):
                params.append((small[0:SH, 4 + j:5 + j], a[name].rearrange("a b -> b a")))
            params += [(small[0:32, 8:12], a["rel_bias"]), (scr[0:24, :], a["state_conv"][0].rearrange("b w c -> (b w) c")),
                       (hot[0:33, :, :], a["shape_hot"]), (rows[0:SH, 2, :], a["shape_starts"])]
            assert len(params) == N_PAR, len(params)
            for n in range(SLOTS):
                load(n, rows4(a["w_ada"][0], 0, KT, n * IT, IT))
                for dst, src in params[6 * n:6 * n + 6]:
                    sp.dma_start(dst, src).then_inc(S("params_loaded"), 16)
            for m in range(MT):
                sp.dma_start(xtok[:, m, :], a["x_prompt"][0, m * P:(m + 1) * P, :]).then_inc(S("x_loaded"), 16)
            sp.dma_start(xtok[0:TS, MT, :], a["x_sample"].rearrange("b t d -> (b t) d")).then_inc(S("x_loaded"), 16)

            w_ada, w_in = a["w_ada"][0], a["w_in"][0]
            for n in range(SLOTS, N_ADA1):
                load(n, rows4(w_ada, 0, KT, n * IT, IT))
            sp.dma_start(wdt[:, :, :], rows4(w_in, 0, KT, 3072, SH)).then_inc(S("wdt_loaded"), 16)
            in_order = (8, 9, 10, 11, 6, 7, 0, 1, 2, 3, 4, 5)
            for n in range(SLOTS):
                load(I_IN + n, rows4(w_in, 0, KT, in_order[n] * IT, IT))
            sp.wait_ge(S("setup_dve"), SETUP_DVE["tables_ready"])
            sp.dma_start(scratch.rearrange("r h t -> h r t"), brow[0:H, :, :]).then_inc(S("tables_stored"), 16)
            sp.wait_ge(S("tables_stored"), 16)
            sp.wait_ge(S("x_free"), 1)
            f0 = bass.AP(scratch.tensor, scratch.offset, [[1, P], [TAB, H], [1, 2 * P]])
            sp.dma_start(wrev, f0).then_inc(S("bias_loaded"), 16)
            sp.wait_ge(S("near_zero"), 1)
            for h in range(H):
                for j in range(2):
                    row = 32 * h + DT * j
                    sp.dma_start(nearr[row:row + DT, :],
                                 bass.AP(scratch.tensor, scratch.offset + h * TAB + OFF - (DT - 1),
                                         [[1, DT], [1, NBIAS]])).then_inc(S("bias_loaded"), 16)
            for n in range(SLOTS, n_in):
                load(I_IN + n, rows4(w_in, 0, KT, in_order[n] * IT, IT))
            with sp.Fori(0, N_ADA2 // SLOTS) as i:
                for k in range(SLOTS):
                    load(I_ADA2 + k, w_ada[:, bass.ds((i * SLOTS + (N_ADA1 + k)) * IT, IT)]
                         .rearrange("(k p) c -> p k c", p=P), i=i, step=SLOTS)

            kc, vc = a["cache_k"], a["cache_v"]
            sp.wait_ge(S("params_loaded"), 16 * N_PAR)

            numbers = {}

            def pages(n, what, b, i=None, step=0):
                g = int(what[1:])
                if g % 4 == 0:
                    _, numbers[what[0]] = nc.values_load_multi_w_load_instructions(
                        ptab[:, bass.ds(b * PAGES + g * IP, 4 * IP)], engines=[mybir.EngineType.SP],
                        min_val=0, max_val=N_POOL - 1)
                phys = numbers[what[0]][g % 4 * IP:(g % 4 + 1) * IP]
                free(n, i, step)
                src = kc if what[0] == "K" else vc
                for p in range(IP):
                    sp.dma_start(slot(n)[:, p * 512:(p + 1) * 512],
                                 src[bass.ds(phys[p], 1), :, :].rearrange("a p f -> (a p) f"))\
                        .then_inc(ring_sem[n % SLOTS], 16)

            for g in range(8):
                pages(I_DEC + g, f"K{g}", 0)
            with sp.Fori(0, NB - 1) as i:
                for k, what in enumerate(BODY):
                    pages(I_LOOP + k, what, i + 1 if what[0] == "K" else i, i=i, step=16)
            for g in range(8):
                pages(I_LAST + g, f"V{g}", NB - 1)

            for k in range(4):
                load(I_OUT + k, rows4(a["w_out"][0], 0, KT, k * IT, IT))
            for ph in range(2):
                up, down = I_UP + 16 * ph, I_UP + 16 * ph + 8
                with sp.Fori(0, 2) as i:
                    for k in range(4):
                        load(up + k, a["w_up"][0][:, bass.ds((i * 4 + (8 * ph + k)) * IT, IT)]
                             .rearrange("(k p) c -> p k c", p=P), i=i, step=4)
                with sp.Fori(0, 2) as i:
                    for k in range(4):
                        r0 = (2 * ph + k % 2) * D
                        load(down + k, a["w_down"][0][r0:r0 + D, bass.ds((i * 2 + k // 2) * IT, IT)]
                             .rearrange("(k p) c -> p k c", p=P), i=i, step=4)
            for m in range(5):
                sp.wait_ge(S("yt_a"), m + 1)
                sp.wait_ge(S("yt_v"), m + 1)
                n = P if m < MT else TS
                dst = o["y_p"][m * P:(m + 1) * P, :] if m < MT else o["y_s"]
                sp.dma_start(dst, ytok[0:n, m % 2, :]).then_inc(S(f"y_stored{m % 2}"), 16)
            for k, stores in enumerate((3, 2)):
                sp.wait_ge(S(f"y_stored{k}"), 16 * stores)
                sp.wait_ge(S(f"kout_stored{k}"), 16 * stores)
            sp.wait_ge(S("out_stored"), 16 * 8)


        tiles = [("x", c) for c in range(8)] + [("d", 0)] + [("z", t) for t in range(4)]
        tiles += [("q", h) for h in range(4)] + [("k", h) for h in range(4)]
        tiles += [("v", 5 * half + m) for half in range(2) for m in range(5)]
        by_dve = [sum(1 for kind, _ in tiles[:n] if kind not in "v") for n in range(len(tiles) + 1)]
        first = {"x": 0, "z": 4, "q": 6, "k": 8, "v": 10}
        tile_sign, plain = [], 0
        for kind, t in tiles:
            if (kind == "v" and t % 5 == 4) or (kind in "qkzx" and t % 2 == 1):
                tile_sign.append(("ring_used", I_IN + first[kind] + (t // 5 if kind == "v" else t // 2) + 1))
            else:
                plain += 1
                tile_sign.append(("ip_ps", plain))

        @block.gpsimd
        def _(pool):
            pool.memset(small[32:33, 8:12], 1.0).then_inc(S("ones_row"), 1)
            pool.wait_ge(S("ones_row"), 1)
            pool.memset(qbd, 0.0).then_inc(S("qbd_zero"), 1)
            pool.wait_ge(S("qbd_zero"), 1)
            pool.memset(xp[:, :, 0:3], 0.0).then_inc(S("xp_zero"), 1)
            pool.wait_ge(S("x_free"), 1)
            pool.memset(nearr, 0.0).then_inc(S("near_zero"), 1)

            for m in range(5):
                pool.wait_ge(S("kout_ready"), m + 1)
                n = P if m < MT else TS
                dst = o["k_p"][m * P:(m + 1) * P, :] if m < MT else o["k_s"]
                pool.dma_start(dst, kouts[m][0:n, :]).then_inc(S(f"kout_stored{m % 2}"), 16)
            for m in range(5):
                n = P if m < MT else TS
                dst = o["v_p"][m * P:(m + 1) * P, :] if m < MT else o["v_s"]
                pool.dma_start(dst, vtk[0:n, m, :]).then_inc(S("out_stored"), 16)
            pool.wait_ge(S("conv_rows"), 1)
            pool.dma_start(o["conv_p"], sout[0:3, :]).then_inc(S("out_stored"), 16)
            pool.dma_start(o["conv_s"], sout[3:27, :]).then_inc(S("out_stored"), 16)
            pool.wait_ge(S("out_stored"), 16 * 7)
            pool.wait_ge(S("xn"), KT)
            for b in range(NB):
                pool.dma_start(h0[:, b, :, :], a["state_ssm"][0, b].rearrange("(t h) p n -> (h p) t n", t=4))\
                    .then_inc(S("h0_loaded"), 16)
            pool.wait_ge(S("final_ready"), 1)
            pool.dma_start(o["ssm_p"].rearrange("(t p) n -> p t n", p=P), sfin).then_inc(S("out_stored"), 16)
            pool.wait_ge(S("ssm_ready"), 1)
            for b in range(NB):
                pool.dma_start(o["ssm_s"][b * 512:(b + 1) * 512, :].rearrange("(t p) n -> p t n", p=P), h0[:, b, :, :])\
                    .then_inc(S("ssm_stored"), 16)
            pool.wait_ge(S("dec_start"), 1)
            pool.tensor_copy(qcur[:, :, 0:2 * DT], qbd[:, 0, :, :, :].rearrange("p h j t -> p h (j t)"))\
                .then_inc(S("q_ready"), 1)
            pool.wait_ge(S("dec_start_a"), 1)
            for m in range(MT):
                pool.dma_start(xtok2[m], a["x_prompt"][0, m * P:(m + 1) * P, :].rearrange("p (a c) -> p a c", a=2))\
                    .then_inc(S("x_reloaded"), 16)
            pool.dma_start(xtok2[MT][0:TS, :, :], a["x_sample"].rearrange("b t (a c) -> (b t) a c", a=2))\
                .then_inc(S("x_reloaded"), 16)
            with pool.Fori(0, NB - 1) as i:
                pool.wait_ge(S("s_ps"), i * 8 + 8)
                pool.wait_ge(S("q_ready"), i + 1)
                pool.tensor_copy(qcur[:, :, 0:2 * DT],
                                 qbd[:, bass.ds(i + 1, 1), :, :, :].rearrange("p a h j t -> p (a h) (j t)"))\
                    .then_inc(S("q_ready"), 1)

        @block.tensor
        def _(pe):
            mm, tr = pe.matmul, pe.transpose

            def turn_x(k, m, src, banks):
                n = P if m < MT else TS
                for half in range(2):
                    if m >= len(banks) // 2 or k:
                        pe.wait_ge(S("xt_a" if half == 0 else "xt_v"), 5 * k + m - len(banks) // 2 + 1)
                    for f in range(4):
                        ins = tr(banks[(2 * m + half) % len(banks)][:, f * P:f * P + n],
                                 src[0:n, half, f * P:(f + 1) * P], ident[0:n, 0:n])
                    ins.then_inc(S("xt_ps"), 1)

            def norm_sum(k):
                for f in range(KT):
                    pe.wait_ge(S("squares"), KT * k + f + 1)
                    x = hT if k == 0 else sq
                    b0, b1 = norm_banks(k)
                    mm(b0[:, 0:HF], ones, x[:, f, 0:HF], start=(f == 0), stop=(f == KT - 1))
                    ins = mm(b1[:, 0:HF], ones, x[:, f, HF:T], start=(f == 0), stop=(f == KT - 1))
                ins.then_inc(S("ssum"), 1)

            def ada_parts(bank, j, w):
                w = w.rearrange("p (k c) -> p k c", k=KT)
                for f in range(KT):
                    r = 32 * (f % 4)
                    ins = mm(bank[r:r + 9, (j % 2) * IT:(j % 2 + 1) * IT], cT[:, f, :], w[:, f, :],
                             start=(f < 4), stop=(f >= 4))
                ins.then_inc(S("ring_used"), 1)

            def ada(i):
                for q in range(2):
                    pe.wait_ge(S("ada_sb"), i * 2 + (q + 1))
                    for j in (2 * q, 2 * q + 1):
                        arrived(pe, i * SLOTS + j)
                        ada_parts(bk[4 + q], j, slot(i * SLOTS + j))
                for q in range(2):
                    pe.wait_ge(S("ada_sb"), i * 2 + (q + 3))
                    for t in range(4):
                        c0 = (8 * i + 4 * q + t) * 9
                        ins = mm(bk[3][:, c0:c0 + 9], adas[:, q, t * P:(t + 1) * P],
                                 cst[:, K_SUM:K_SUM + 9], start=True, stop=True)
                ins.then_inc(S("mod_ps"), 1)

            pe.wait_ge(S("cond_loaded"), 16 * 3)
            pe.wait_ge(S("ada_sb"), 2)
            pe.wait_ge(S("setup_dve"), SETUP_DVE["silu_rows"])
            for k in range(KT):
                ins = tr(bk[5][:, k * 9:(k + 1) * 9], ctmp[0:9, k * P:(k + 1) * P], ident[0:9, 0:9])
            ins.then_inc(S("setup_ps"), 1)
            pe.wait_ge(S("setup_dve"), SETUP_DVE["ct_ready"])
            ada(0)
            pe.wait_ge(S("params_loaded"), 16 * N_PAR)
            tr(bk[6][:, 0:NROW], vrow[0:NROW, :], ident[0:NROW, 0:NROW]).then_inc(S("setup_ps"), 1)
            pe.wait_ge(S("setup_dve"), SETUP_DVE["lam_prod"])
            mm(bk[6][:, 0:2], ones[0:HD, :], small[0:HD, 12:14], start=True, stop=True)
            for t in range(4):
                for r in range(2):
                    ins = mm(bk[6][64 * r:64 * r + 64, 4 + t:5 + t],
                             ident[0:SH, 2 * t + r:2 * t + r + 1].to_broadcast([SH, SP_]), small[0:SH, 6:7],
                             start=True, stop=True)
            ins.then_inc(S("setup_ps"), 1)
            pe.wait_ge(S("ones_row"), 1)
            pe.wait_ge(S("setup_dve"), SETUP_DVE["lam_ready"])
            for r in range(2):
                ins = mm(bk[6 + r][0:H, 0:TAB], small[0:33, 8:12], hot[0:33, r, :], start=True, stop=True)
            ins.then_inc(S("setup_ps"), 1)
            pe.wait_ge(S("setup_dve"), SETUP_DVE["tables_ready"])
            for c in range(8):
                ins = tr(bk[6][:, c * 24:(c + 1) * 24], scr[0:24, c * P:(c + 1) * P], ident[0:24, 0:24])
            ins.then_inc(S("setup_ps"), 1)
            pe.wait_ge(S("setup_dve"), SETUP_DVE["prefix_ready"])

            pe.wait_ge(S("x_loaded"), 16 * 5)
            for m in range(5):
                turn_x(0, m, xtok[:, m, :].rearrange("p (a c) -> p a c", a=2), (bk[0], bk[1], bk[2], bk[7]))
            ada(1)
            norm_sum(0)

            def dense(bp, bs, w, c0, m, fs, hi, lo, start=True, stop=True):
                for j, f in enumerate(fs):
                    for k, (a_, b_) in enumerate(((w[0], hi), (w[0], lo), (w[1], hi))):
                        s = start and j == 0 and k == 0
                        e = stop and j == len(fs) - 1 and k == 2
                        mm(bp[0:m, 0:HF], a_[:, j, c0:c0 + m], b_[:, f, 0:HF], start=s, stop=e)
                        ins = mm(bs[0:m, 0:HF], a_[:, j, c0:c0 + m], b_[:, f, HF:T], start=s, stop=e)
                return ins

            def dense_half(bank, half, w, c0, fs, hi, lo, start, stop):
                for j, f in enumerate(fs):
                    for k, (a_, b_) in enumerate(((w[0], hi), (w[0], lo), (w[1], hi))):
                        ins = mm(bank[:, 0:HF], a_[:, f, c0:c0 + P], b_[:, f, half * HF:(half + 1) * HF],
                                 start=start and j == 0 and k == 0, stop=stop and j == len(fs) - 1 and k == 2)
                return ins

            def tok_rows():
                pe.wait_ge(S("rows_ready"), 1)
                for m in range(5):
                    n = P if m < MT else TS
                    for r in range(3):
                        ins = tr(bk[6][0:n, (3 * m + r) * SH:(3 * m + r + 1) * SH], rows[0:SH, r, m * P:m * P + n],
                                 ident[0:SH, 0:SH])
                ins.then_inc(S("ssd_ps"), 1)
                for h in range(SH):
                    ins = mm(bk[7][:, h * 12:(h + 1) * 12], ident[0:SH, h:h + 1].to_broadcast([SH, P]),
                             small[0:SH, 24:36], start=True, stop=True)
                ins.then_inc(S("ssd_ps"), 1)

            def conv_ends():
                pe.wait_ge(S("ends_ready"), 8)
                for c in range(8):
                    ins = tr(bk[c // 4][0:27, (c % 4) * P:(c % 4 + 1) * P], gc[:, c, :], ident)
                ins.then_inc(S("conv_ps"), 1)

            def ada_early(x):
                arrived(pe, I_ADA2 + x)
                ada_parts(bk[4 + x // 2], x, slot(I_ADA2 + x))

            for n, (kind, t) in enumerate(tiles):
                bp, bs = bk[2 * (n % 4)], bk[2 * (n % 4) + 1]
                if n >= 4:
                    pe.wait_ge(S("ip_act"), n - 3)
                    pe.wait_ge(S("ip_dve"), by_dve[n - 3])
                sign = tile_sign[n][0]
                if kind == "v":
                    half, m = t // 5, t % 5
                    k = I_IN + first["v"] + half
                    r = P if m < MT else TS
                    w = parts(pe, k)
                    for f in range(KT):
                        for j, (x, w_) in enumerate(((hh_in, w[0]), (hh_in, w[1]), (hl, w[0]))):
                            ins = mm(bp[0:r, 0:IT], x[:, f, m * P:m * P + r], w_[:, f, :],
                                     start=(f == 0 and j == 0), stop=(f == KT - 1 and j == 2))
                elif kind == "d":
                    pe.wait_ge(S("wdt_low"), 1)
                    ins = dense(bp, bs, (wdth, wdtl), 0, SH, range(KT), hh_in, hl)
                else:
                    k = I_IN + first[kind] + t // 2
                    w = parts(pe, k)
                    if n == 0:
                        for f in range(KT):
                            pe.wait_ge(S("h_low"), f + 1)
                            ins = dense(bp, bs, [x[:, f:f + 1, :] for x in w], 0, P, (f,), hh_in, hl,
                                        f == 0, f == KT - 1)
                    else:
                        ins = dense(bp, bs, w, (t % 2) * P, P, range(KT), hh_in, hl)
                ins.then_inc(S(sign), 1)

            pe.wait_ge(S("ip_act"), len(tiles))
            pe.wait_ge(S("ip_dve"), by_dve[-1])
            tok_rows()
            ada_early(0)
            ada_early(1)
            conv_ends()
            ada_early(2)
            ada_early(3)
            pe.wait_ge(S("conv_rows"), 1)
            for m in range(5):
                n = P if m < MT else TS
                if m >= 2:
                    pe.wait_ge(S("kout_ready"), m - 1)
                for h in range(H):
                    ins = tr(bk[m % 2][0:n, h * P:(h + 1) * P], kT[:, h, m * P:m * P + n], ident)
                ins.then_inc(S("kout_ps"), 1)

            units = [(h, qb) for h in range(H) for qb in range(MT)]

            def ada_item(x):
                if x > N_EARLY and x % 2 == 0:
                    pe.wait_ge(S("ada_sb"), 2 + N_ADA1 // 2 + x // 2)
                arrived(pe, I_ADA2 + x)
                ada_parts(bk[1], x, slot(I_ADA2 + x))

            def mod_tiles(k):
                if k == 0:
                    pe.wait_ge(S("ada_sb"), 2 + (N_ADA1 + N_ADA2) // 2)
                for t in range(4):
                    ins = mm(bk[1][:, (4 * k + t) * 9:(4 * k + t + 1) * 9], adas2[:, k, t * P:(t + 1) * P],
                             cst[:, K_SUM:K_SUM + 9], start=True, stop=True)
                if k == N_ADA2 // 2 - 1:
                    ins.then_inc(S("mod_ps"), 1)

            def att_scores(x):
                h, qb = units[x]
                nk = (qb + 1) * P
                near = min(2 * P, nk)
                if x >= 2:
                    pe.wait_ge(S("att_exp"), 2 * (x - 1))
                for j in range(2):
                    mm(bk[2 + 2 * (x % 2) + j][:, 0:nk], qT[64 * j:64 * j + 64, h, qb * P:(qb + 1) * P],
                       kT[64 * j:64 * j + 64, h, 0:nk], start=True, stop=False)
                for j in range(2):
                    ins = mm(bk[2 + 2 * (x % 2) + j][:, nk - near:nk], ident, wb[:, h, 2 * P - near:2 * P],
                             start=False, stop=True)
                ins.then_inc(S("att_s"), 1)

            def att_transpose(x):
                h, qb = units[x]
                pe.wait_ge(S("att_p"), x + 1)
                if x >= 2:
                    pe.wait_ge(S("att_pt"), x - 1)
                for kb in range(qb + 1):
                    ins = tr(bk[6 + x % 2][:, kb * P:(kb + 1) * P], pj[:, x % 2, 0, kb * P:(kb + 1) * P], ident)
                ins.then_inc(S("att_t"), 1)

            def att_values(x):
                h, qb = units[x]
                pe.wait_ge(S("att_pt"), x + 1)
                if qb == 0 and h >= 1:
                    pe.wait_ge(S("att_o"), h)
                for kb in range(qb + 1):
                    ins = mm(bk[0][:, qb * P:(qb + 1) * P], vtk[:, kb, h * VD:(h + 1) * VD],
                             pts[:, x % 2, kb * P:(kb + 1) * P], start=(kb == 0), stop=(kb == qb))
                ins.then_inc(S("att_v"), 1)

            pe.wait_ge(S("kout_ready"), 6)
            pe.wait_ge(S("dec_sb"), 1)
            pe.wait_ge(S("ada_sb"), 2 + (N_ADA1 + N_EARLY) // 2)
            NU = len(units)
            att_scores(0)
            for x in range(NU + 2):
                if x + 1 < NU:
                    att_scores(x + 1)
                if x + N_EARLY < N_ADA2:
                    ada_item(x + N_EARLY)
                elif NU - 3 <= x < NU + 1:
                    mod_tiles(2 * (x - NU + 3))
                    mod_tiles(2 * (x - NU + 3) + 1)
                if 1 <= x <= NU:
                    att_transpose(x - 1)
                if x >= 2:
                    att_values(x - 2)
            def head_norm(bank, k, n):
                pe.wait_ge(S("att_sq"), k + 1)
                mm(bank[:, 0:n], ones, hT[:, k % H, 0:n], start=True, stop=True).then_inc(S("att_ss"), 1)

            for h in range(H):
                head_norm(bk[2 + h], h, TP)

            pe.wait_ge(S("att_o"), H)
            pe.wait_ge(S("mod2"), 1)
            for m in range(5):
                n = P if m < MT else TS
                if m >= 2:
                    pe.wait_ge(S("xtk_v"), m - 1)
                for t in range(4):
                    ins = tr(bk[m % 2][0:n, t * P:(t + 1) * P], xp[:, t, m * P:m * P + n], ident)
                ins.then_inc(S("xtk_ps"), 1)
                if m >= 2:
                    pe.wait_ge(S("btk_a"), m - 1)
                for g in range(GR):
                    ins = tr(bk[6 + m % 2][0:n, g * P:(g + 1) * P], xp[:, 4 + g, m * P:m * P + n], ident)
                ins.then_inc(S("btk_ps"), 1)
            pe.wait_ge(S("att_r"), H)
            pe.wait_ge(S("btk_a"), 5)
            for g in range(GR):
                for c in range(MT):
                    ins = mm(bk[4 + g][:, c * P:(c + 1) * P], xp[:, 4 + g, c * P:(c + 1) * P],
                             xp[:, 6 + g, c * P:(c + 1) * P], start=True, stop=True)
                ins.then_inc(S("cb_ps"), 1)
            for g in range(GR):
                ins = mm(bk[6][0:TS, g * TS:(g + 1) * TS], xp[:, 4 + g, TP:T], xp[:, 6 + g, TP:T],
                         start=True, stop=True)
            ins.then_inc(S("cb_ps"), 1)
            pe.wait_ge(S("xtk_v"), 5)
            for c in range(MT):
                for g in range(GR):
                    ins = mm(bk[c][:, g * 256:(g + 1) * 256], btk[:, c, g * NS:(g + 1) * NS],
                             xw[:, c, g * 256:(g + 1) * 256], start=True, stop=True)
                ins.then_inc(S("st_ps"), 1)

            def bcast(h):
                if h >= 2:
                    pe.wait_ge(S("cexp"), h - 1)
                sel = ident[0:SH, h:h + 1].to_broadcast([SH, P])
                mm(bk[h % 2][:, :], sel, rows[0:SH, 1, 0:TP], start=True, stop=True)
                mm(bk[2 + h % 2][:, 0:TS], sel, rows[0:SH, 1, TP:T], start=True, stop=True).then_inc(S("cs_bc"), 1)

            def ssd_y(h):
                t, r = h // 2, h % 2
                pe.wait_ge(S("g_ready"), h + 1)
                if r == 0 and t >= 2:
                    pe.wait_ge(S("y_sb"), t - 1)
                y, ys = bk[4 + t % 2][64 * r:64 * r + 64, :], bk[6 + t % 2][64 * r:64 * r + 64, :]
                hs = slice(h * SP_, (h + 1) * SP_)
                for c in range(MT):
                    mm(y[:, c * P:(c + 1) * P], xdt[:, c, hs], lg[:, h % 3, c * P:(c + 1) * P],
                       start=True, stop=(c == 0))
                    if c:
                        mm(y[:, c * P:(c + 1) * P], prev[:, c - 1, hs], ceb[:, h % 3, c * P:(c + 1) * P],
                           start=False, stop=True)
                mm(ys[:, 0:TS], xdt[0:TS, MT, hs], lg[0:TS, h % 3, TP:T], start=True, stop=False)
                for b in range(NB):
                    ins = mm(ys[:, b * DT:(b + 1) * DT], h0T[:, b, t, 64 * r:64 * r + 64],
                             ceb[:, h % 3, TP + b * DT:TP + (b + 1) * DT], start=False, stop=(b == NB - 1))
                ins.then_inc(S("y_ps"), 1)

            pe.wait_ge(S("prev_done"), 1)
            for t in range(4):
                ins = tr(bk[3][:, t * P:(t + 1) * P], prev[:, MT - 1, t * P:(t + 1) * P], ident)
            ins.then_inc(S("ssd_ps"), 1)
            pe.wait_ge(S("h0_loaded"), 16 * NB)
            for b in range(NB):
                if b >= 2:
                    pe.wait_ge(S("h0t_sb"), b - 1)
                for t in range(4):
                    ins = tr(bk[b % 2][:, t * P:(t + 1) * P], h0[:, b, t, :], ident)
                ins.then_inc(S("h0t_ps"), 1)
            pe.wait_ge(S("h0t_sb"), NB)
            pe.wait_ge(S("cb_sb"), 3)
            pe.wait_ge(S("final_ready"), 1)
            bcast(0)
            bcast(1)
            for h in range(SH):
                if h + 2 < SH:
                    bcast(h + 2)
                ssd_y(h)
            for g in range(GR):
                for t in (2 * g, 2 * g + 1):
                    pe.wait_ge(S("ssd_sq"), t + 1)
                    mm(bk[2 * g][:, 0:HF], ones, hT[:, t, 0:HF], start=(t % 2 == 0), stop=(t % 2 == 1))
                    ins = mm(bk[2 * g + 1][:, 0:HF], ones, hT[:, t, HF:T], start=(t % 2 == 0), stop=(t % 2 == 1))
                ins.then_inc(S("ssd_ss"), 1)
            pe.wait_ge(S("bblk_ready"), 1)
            pe.wait_ge(S("y_sb"), 4)
            for t in range(4):
                for q in range(2):
                    x = 2 * t + q
                    if x >= 4:
                        pe.wait_ge(S("ssm_sb"), x - 3)
                    mm(bk[4 + x % 4][:, :], xws[:, t * P:(t + 1) * P],
                       bblk[0:TS, t // 2, 4 * q:4 * q + 4, :].rearrange("p b n -> p (b n)"),
                       start=True, stop=True).then_inc(S("ssm_ps"), 1)

            pe.wait_ge(S("dec_start"), 1)
            pe.wait_ge(S("dec_start_a"), 1)

            def turn_k(n, g, i=None, step=0):
                arrived(pe, n, i, step) if step else arrived(pe, n)
                src = slot(n).rearrange("p (q c) -> p q c", q=IP)
                items = g if i is None else i * 8 + (8 + g)
                for p in range(IP):
                    if i is not None or g or p >= 2:
                        pe.wait_ge(S("kt_sb"), items * IP + (p - 1))
                    for h in range(H):
                        ins = tr(bk[p % 2][:, h * P:(h + 1) * P], src[:, p, h * P:(h + 1) * P], ident)
                    ins.then_inc(S("kt_ps" if p < IP - 1 else "ring_used"), 1)

            def score(g, i=None):
                items = g if i is None else i * 8 + (8 + g)
                if g == 0:
                    pe.wait_ge(S("q_ready"), 1 if i is None else i + 2)
                if i is not None or g >= 2:
                    pe.wait_ge(S("s_sb"), items - 1)
                pe.wait_ge(S("kt_sb"), items * IP + IP)
                for h in range(H):
                    ins = mm(bk[2 + g % 2][32 * h:32 * h + 32, :], qcur[:, h, :], kts[:, g % 2, h, :],
                             start=True, stop=True)
                ins.then_inc(S("s_ps"), 1)

            def new_scores():
                for h in range(H):
                    ins = mm(bk[7][32 * h:32 * h + 32, 0:TS], qcur[:, h, :], kT[:, h, TP:T], start=True, stop=True)
                ins.then_inc(S("new_ps"), 1)

            def v_item(n, g, it, i=None, step=0):
                groups = (9 * it if i is None else i * 9) + g
                arrived(pe, n, i, step) if step else arrived(pe, n)
                src = slot(n).rearrange("p (q c) -> p q c", q=IP)
                pe.wait_ge(S("pt_sb"), groups + (2 if g == 7 else 1))
                for p in range(IP):
                    for h in range(H):
                        ins = mm(bk[5][32 * h:32 * h + 16, 0:P], pT[:, g % 2, p * P + 32 * h:p * P + 32 * h + 16],
                                 src[:, p, h * P:(h + 1) * P], start=(g == 0 and p == 0), stop=False)
                ins.then_inc(S("ring_used"), 1)
                if g == 7:
                    for h in range(H):
                        ins = mm(bk[5][32 * h:32 * h + 16, 0:P], pT[0:TS, 0, 32 * h:32 * h + 16],
                                 vtk[0:TS, MT, h * VD:(h + 1) * VD], start=False, stop=True)
                    ins.then_inc(S("o_ps"), 1)

            def turn_p(g, exps):
                if g % 2 == 0 and g < 8:
                    pe.wait_ge(S("exp_done"), exps + (g // 2 + 1))
                bank = bk[4 + 2 * (g % 2)]
                if g < 8:
                    for p in range(IP):
                        ins = tr(bank[:, p * P:(p + 1) * P], pr[:, (IP * g + p) * P:(IP * g + p + 1) * P], ident)
                else:
                    ins = tr(bank[0:TS, 0:P], pr[:, NK:NK + TS], ident)
                ins.then_inc(S("pt_ps"), 1)

            def combine(i, new):
                pe.wait_ge(S("on_ready"), i + 1)
                pe.wait_ge(S("new_sb"), new)
                mm(bk[7][:, P:P + NB * H], on, sel, start=True, stop=True).then_inc(S("od_ps"), 1)

            for g in range(8):
                turn_k(I_DEC + g, g)
                if g >= 1:
                    score(g - 1)
                if g == 4:
                    new_scores()
                if g >= 3:
                    if g == 3:
                        pe.wait_ge(S("x_reloaded"), 16 * 5)
                    turn_x(1, g - 3, xtok2[g - 3], (bk[4], bk[6]))
            score(7)
            pe.wait_ge(S("xt_a"), 10)
            pe.wait_ge(S("xt_v"), 10)
            with pe.Fori(0, NB - 1) as i:
                for what in STEPS:
                    kind, g = what[0], int(what[1:])
                    if kind == "T":
                        turn_k(I_LOOP + BODY.index(f"K{g}"), g, i=i, step=16)
                    if kind == "S":
                        score(g, i)
                    if kind == "P":
                        turn_p(g, i * 4)
                    if kind == "V":
                        v_item(I_LOOP + BODY.index(f"V{g}"), g, None, i=i, step=16)
                    if what == "S3":
                        pe.wait_ge(S("od_sb"), i + 1)
                        new_scores()
                combine(i, i + 2)
            for what in STEPS:
                if what[0] == "P":
                    turn_p(int(what[1:]), 4 * (NB - 1))
                if what[0] == "V":
                    v_item(I_LAST + int(what[1:]), int(what[1:]), NB - 1)
            combine(NB - 1, NB)
            pe.wait_ge(S("od_sq"), 1)
            mm(bk[4][:, 0:H * TS], ones, odt[:, 0, :], start=True, stop=True).then_inc(S("od_ss"), 1)

            w = parts(pe, I_OUT)
            for t in range(2):
                dense_half(bk[2 * t], 0, w, t * P, range(KT), mh, ml, True, True)
                dense_half(bk[2 * t + 1], 1, w, t * P, range(H, KT), mh, ml, True, False)
            pe.wait_ge(S("mix_ready"), 2)
            for t in range(2):
                dense_half(bk[2 * t + 1], 1, w, t * P, range(H), mh, ml, False, True)\
                    .then_inc(S("op_ps" if t == 0 else "ring_used"), 1)

            for k in range(1, 4):
                w = parts(pe, I_OUT + k)
                for t in range(2):
                    x = 2 * k + t
                    if x >= 2:
                        pe.wait_ge(S("op_sb"), x - 1)
                    bp, bs = bk[2 * (x % 2)], bk[2 * (x % 2) + 1]
                    dense(bp, bs, w, t * P, P, range(KT), mh, ml)\
                        .then_inc(S("op_ps" if t == 0 else "ring_used"), 1)
            norm_sum(1)
            for ph in range(2):
                up, down = I_UP + 16 * ph, I_UP + 16 * ph + 8
                if ph == 1:
                    pe.wait_ge(S("down_sb"), KT + 2)
                with pe.Fori(0, 2) as i:
                    for k in range(4):
                        w = parts(pe, up + k, i, 4)
                        for t in range(2):
                            x = 2 * k + t
                            pe.wait_ge(S("up_sb"), i * 8 + (UH * ph + x + 1))
                            bp, bs = ffn_banks(ph, None, x % 2)
                            if ph == 0 and x == 0:
                                for f in range(KT):
                                    pe.wait_ge(S("h_low"), KT + f + 1)
                                    ins = dense(bp, bs, [y[:, f:f + 1, :] for y in w], 0, P, (f,), hh_ffn, hl,
                                                f == 0, f == KT - 1)
                            else:
                                ins = dense(bp, bs, w, t * P, P, range(KT), hh_ffn, hl)
                            ins.then_inc(S("up_ps" if t == 0 else "ring_used"), 1)
                with pe.Fori(0, 2) as i:
                    for k in range(4):
                        w = parts(pe, down + k, i, 4)
                        c, kk = k // 2, k % 2
                        pe.wait_ge(S("u_ready"), UH * ph + 8 * (kk + 1))
                        for t in range(2):
                            if kk == 0:
                                pe.wait_ge(S("down_sb"), i * 4 + (KT * ph + 2 * c + t + 1))
                            bp, bs = ffn_banks(ph, c, t)
                            ins = dense(bp, bs, w, t * P, P, range(8 * kk, 8 * kk + 8), uh, ul, kk == 0, kk == 1)
                            if t == 1:
                                ins.then_inc(S("ring_used"), 1)
                            elif kk == 1:
                                ins.then_inc(S("down_ps"), 1)
            pe.wait_ge(S("down_sb"), 4 + 2 * KT - 2)
            norm_sum(2)
            for m in range(5):
                n = P if m < MT else TS
                for half in range(2):
                    w = 2 * m + half
                    if m == 0:
                        pe.wait_ge(S("xn"), 2 * KT + 4 * (half + 1))
                    if w >= 4:
                        pe.wait_ge(S("yt_a" if half == 0 else "yt_v"), (w - 4) // 2 + 1)
                    for k in range(4):
                        ins = tr(bk[w % 4][0:n, k * P:(k + 1) * P], hT[:, 4 * half + k, m * P:m * P + n], ident)
                    ins.then_inc(S("yt_ps"), 1)

        @block.scalar
        def _(act):
            step = Tally(S("act_step"))
            act.preload_act_table_set("natural_log_exp_and_others")

            def A(out, in_, f, **kw):
                return act.activation(out, in_, f, **kw)

            act.wait_ge(S("cond_loaded"), 16 * 3)
            A(ctmp[0:9, :], crow[0:9, :], ACT.Exp, scale=-1.0).then_inc(S("setup_act"), 1)
            act.wait_ge(S("params_loaded"), 16 * N_PAR)
            A(small[0:SH, 16:17], small[0:SH, 5:6], ACT.Exp).then_inc(S("setup_act"), 1)

            def take_x(k, m, bank):
                n = P if m < MT else TS
                act.wait_ge(S("xt_ps"), 10 * k + 2 * m + 1)
                A(xT[:, 0:4, m * P:m * P + n], bank[:, :].rearrange("p (k c) -> p k c", k=4)[:, :, 0:n],
                  ACT.Copy).then_inc(S("xt_a"), 1)

            act.wait_ge(S("setup_ps"), SETUP_PS["lam_ps"])
            A(small[:, 18:20], bk[6][:, 0:2], ACT.Exp).then_inc(S("setup_act"), 1)
            for m in range(5):
                take_x(0, m, bk[2 * (m % 2)])
            act.wait_ge(S("xt_v"), 5)
            act.wait_ge(S("xt_a"), 5)

            def squares(k, f):
                A(hT[:, f, :] if k == 0 else sq[:, f, :], xT[:, f, :], ACT.Square).then_inc(S("squares"), 1)

            def rstd(k):
                act.wait_ge(S("ssum"), k + 1)
                b0, b1 = norm_banks(k)
                link(act, A(rs[:, 0:HF], b0[:, 0:HF], ACT.Ln, scale=1.0 / D, bias=cst_eps), step)
                link(act, A(rs[:, HF:T], b1[:, 0:HF], ACT.Ln, scale=1.0 / D, bias=cst_eps), step)
                A(rs[:, :], rs[:, :], ACT.Exp, scale=-0.5).then_inc(S("rstd"), 1)

            def modulate(k, g, sh, hh):
                for f in range(KT + 1):
                    if f < KT:
                        act.wait_ge(S("xn"), KT * k + f + 1)
                        A(hT[:, f, 0:TP], hT[:, f, 0:TP], ACT.Identity, scale=g[:, f, 0:1], bias=mod[:, sh + f, 0:1])\
                            .then_inc(S("h_prompt"), 1)
                    if f >= 1:
                        act.wait_ge(S("h_sample"), KT * k + f)
                        act.wait_ge(S("h_prompt"), KT * k + f)
                        A(hh[:, f - 1, :], hT[:, f - 1, :], ACT.Copy).then_inc(S("h_high"), 1)

            cst_eps = small[:, 63:64]
            act.wait_ge(S("eps_ready"), 1)
            for f in range(KT):
                squares(0, f)
            rstd(0)
            act.wait_ge(S("x_free"), 1)
            act.wait_ge(S("tables_stored"), 16)
            split_high(act, I_IN)

            act.wait_ge(S("mod1"), 1)
            modulate(0, g1, 0, hh_in)
            split_high(act, I_IN + 1)
            act.wait_ge(S("wdt_loaded"), 16)
            A(wdth, wdt, ACT.Copy).then_inc(S("wdt_high"), 1)

            def sigmoid(out, x, done):
                link(act, A(out, x, ACT.Exp, scale=-1.0), step)
                link(act, A(out, out, ACT.Ln, bias=1.0), step)
                A(out, out, ACT.Exp, scale=-1.0).then_inc(S(done), 1)

            for n, (kind, t) in enumerate(tiles):
                bp = bk[2 * (n % 4)]
                sign, count = tile_sign[n]
                act.wait_ge(S(sign), count)
                if kind == "q":
                    ins = A(qT[:, t, 0:HF], bp[:, 0:HF], ACT.Copy, scale=HD ** -0.5)
                elif kind == "k":
                    ins = A(kT[:, t, 0:HF], bp[:, 0:HF], ACT.Copy)
                elif kind == "v":
                    half, m = t // 5, t % 5
                    r = P if m < MT else TS
                    ins = A(vtk[0:r, m, half * IT:(half + 1) * IT], bp[0:r, 0:IT], ACT.Copy)
                elif kind == "d":
                    ins = A(rs[0:SH, 0:HF], bp[0:SH, 0:HF], ACT.Identity, bias=small[0:SH, 4:5])
                elif kind == "z":
                    ins = A(zT[:, t, 0:HF], bp[:, 0:HF], ACT.Copy)
                else:
                    ins = A(xp[:, t, 3:3 + HF], bp[:, 0:HF], ACT.Copy)
                ins.then_inc(S("ip_act"), 1)
                if sign == "ring_used" and count + 1 < I_IN + n_in:
                    split_high(act, count + 1)
                if 1 <= n <= 8:
                    c = n - 1
                    act.wait_ge(S("ip_act"), c + 1)
                    act.wait_ge(S("ip_dve"), c + 1)
                    if c >= 2:
                        act.wait_ge(S("xa_ready"), c - 1)
                    pp, ss = seg(xp[:, c, :], 0)
                    w0, b0 = cols[:, C_CW + c:C_CW + c + 1], cols[:, C_CB + c:C_CB + c + 1]
                    A(cv[:, c % 2, 0:TP], pp, ACT.Identity, scale=w0, bias=b0).then_inc(S("tap0"), 1)
                    A(cv[:, c % 2, TP:T].rearrange("p (b t) -> p b t", b=NB), ss, ACT.Identity, scale=w0, bias=b0)\
                        .then_inc(S("tap0"), 1)
                if 2 <= n <= 9:
                    act.wait_ge(S("taps"), n - 1)
                    sigmoid(ce[:, n % 2, :], cv[:, n % 2, :], "conv_gate")
                if n == 10:
                    act.wait_ge(S("dt_abs"), 1)
                    link(act, A(rows[0:SH, 0, :], rows[0:SH, 0, :], ACT.Exp, scale=-1.0), step)
                    A(rows[0:SH, 0, :], rows[0:SH, 0, :], ACT.Ln, bias=1.0).then_inc(S("dt_ln"), 1)
                if n == 11:
                    act.wait_ge(S("dt_gap"), 1)
                    A(rows[0:SH, 2, :], rows[0:SH, 2, :], ACT.Exp).then_inc(S("dt_w"), 1)
                    A(small[0:SH, 24:36], small[0:SH, 24:36], ACT.Exp).then_inc(S("dt_w"), 1)
                if 12 <= n <= 15:
                    act.wait_ge(S("ip_act"), 9 + n - 11)
                    act.wait_ge(S("ip_dve"), 9 + n - 11)
                    sigmoid(mix[:, n - 8, :], zT[:, n - 12, :], "z_gate")
            NU = 16
            for x in range(NU + 1):
                if x >= 7 and x % 4 == 3:
                    h = x // 4 - 1
                    act.wait_ge(S("att_o"), h + 1)
                    A(hT[:, h, 0:TP], mix[:, h, 0:TP], ACT.Square).then_inc(S("att_sq"), 1)
                if x < NU:
                    h, qb = x // MT, x % MT
                    nk = (qb + 1) * P
                    for j in range(2):
                        act.wait_ge(S("att_m"), 2 * x + j + 1)
                        if x >= 2 and j == 0:
                            act.wait_ge(S("att_t"), x - 1)
                        A(pj[:, x % 2, j, 0:nk], bk[2 + 2 * (x % 2) + j][:, 0:nk], ACT.Exp,
                          bias=small[:, 36 + 2 * (x % 2) + j:37 + 2 * (x % 2) + j],
                          accum_out=small[:, 40 + 2 * (x % 2) + j:41 + 2 * (x % 2) + j]).then_inc(S("att_exp"), 1)
                if x >= 1:
                    y = x - 1
                    act.wait_ge(S("att_t"), y + 1)
                    if y >= 2:
                        act.wait_ge(S("att_v"), y - 1)
                    nk = (y % MT + 1) * P
                    A(pts[:, y % 2, 0:nk], bk[6 + y % 2][:, 0:nk], ACT.Copy).then_inc(S("att_pt"), 1)
            act.wait_ge(S("att_o"), H)
            A(hT[:, H - 1, 0:TP], mix[:, H - 1, 0:TP], ACT.Square).then_inc(S("att_sq"), 1)
            def att_rstd(h):
                act.wait_ge(S("att_ss"), h + 1)
                link(act, A(hT[:, 4 + h, 0:TP], bk[2 + h][:, :], ACT.Ln, scale=1.0 / VD, bias=cst_eps), step)
                A(hT[:, 4 + h, 0:TP], hT[:, 4 + h, 0:TP], ACT.Exp, scale=-0.5).then_inc(S("att_r"), 1)

            att_rstd(0)
            att_rstd(1)
            for m in range(5):
                n = P if m < MT else TS
                act.wait_ge(S("btk_ps"), m + 1)
                if m == 0:
                    act.wait_ge(S("out_stored"), 16 * 7)
                A(btk[0:n, m, :], bk[6 + m % 2][0:n, 0:256], ACT.Copy).then_inc(S("btk_a"), 1)
            att_rstd(2)
            att_rstd(3)
            for g in range(GR):
                act.wait_ge(S("cb_ps"), g + 1)
                A(cbT[:, g, 0:TP], bk[4 + g][:, :], ACT.Copy).then_inc(S("cb_sb"), 1)
            act.wait_ge(S("cb_ps"), 3)
            A(cbT[0:TS, :, TP:T], bk[6][0:TS, 0:2 * TS].rearrange("p (g t) -> p g t", g=2), ACT.Copy)\
                .then_inc(S("cb_sb"), 1)
            act.wait_ge(S("att_n"), H)
            for b in range(NB):
                act.wait_ge(S("h0t_ps"), b + 1)
                A(h0T[:, b, :, :].rearrange("p t q -> p (t q)"), bk[b % 2][:, :], ACT.Copy).then_inc(S("h0t_sb"), 1)
            for h in range(SH):
                act.wait_ge(S("seg"), 5 * (h + 1))
                if h >= 3:
                    act.wait_ge(S("y_ps"), h - 2)
                step.up(A(ceb[:, h % 3, 0:TP], bk[h % 2][:, :], ACT.Exp))
                A(ceb[:, h % 3, TP:T], bk[2 + h % 2][:, 0:TS], ACT.Exp).then_inc(S("cexp"), 1)
                step.up(A(lg[:, h % 3, 0:TP], lg[:, h % 3, 0:TP], ACT.Exp))
                A(lg[0:TS, h % 3, TP:T], lg[0:TS, h % 3, TP:T], ACT.Exp).then_inc(S("lexp"), 1)
            for t in range(4):
                act.wait_ge(S("y_gated"), t + 1)
                act.wait_ge(S("y_ps"), SH)
                A(hT[:, t, :], mix[:, 4 + t, :], ACT.Square).then_inc(S("ssd_sq"), 1)
            for g in range(GR):
                act.wait_ge(S("ssd_ss"), g + 1)
                r = hT[:, 4 + g, :]
                link(act, A(r[:, 0:HF], bk[2 * g][:, 0:HF], ACT.Ln, scale=1.0 / 256, bias=cst_eps), step)
                link(act, A(r[:, HF:T], bk[2 * g + 1][:, 0:HF], ACT.Ln, scale=1.0 / 256, bias=cst_eps), step)
                A(r, r, ACT.Exp, scale=-0.5).then_inc(S("ssd_r"), 1)
            act.wait_ge(S("dec_start"), 1)
            act.wait_ge(S("ssd_r"), 2)
            A(small[:, 56:57], cst_eps, ACT.Copy).then_inc(S("dec_start_a"), 1)

            def copy_page(page, i=None):
                if page % IP < IP - 1:
                    n = page // IP * (IP - 1) + page % IP + 1
                    act.wait_ge(S("kt_ps"), n if i is None else i * (8 * (IP - 1)) + (8 * (IP - 1) + n))
                elif i is None:
                    act.wait_ge(S("ring_used"), I_DEC + page // IP + 1)
                else:
                    act.wait_ge(S("ring_used"), i * 16 + (I_LOOP + BODY.index(f"K{page // IP}") + 1))
                g, p = page // IP, page % IP
                if i is not None or g >= 2:
                    act.wait_ge(S("s_ps"), g - 1 if i is None else i * 8 + (g + 7))
                A(kts[:, g % 2, :, p * P:(p + 1) * P], bk[p % 2][:, :].rearrange("p (h c) -> p h c", h=H), ACT.Copy)\
                    .then_inc(S("kt_sb"), 1)

            def softmax_exp(i, c):
                act.wait_ge(S("max_ready"), i + 1)
                lo, hi = c * (NK // 4), (c + 1) * (NK // 4) if c < 3 else NK + TS
                A(pr[:, lo:hi], sc[:, lo:hi], ACT.Exp, bias=small[:, 46:47], accum_out=small[:, 50 + c:51 + c])\
                    .then_inc(S("exp_done"), 1)

            for page in range(PAGES):
                copy_page(page)
                if page % IP == IP - 1:
                    f = page // IP
                    A(mh[:, f, 0:TP if f < H else T], mix[:, f, 0:TP if f < H else T], ACT.Copy)\
                        .then_inc(S("m_high"), 1)
                    if f >= 3:
                        if f == 3:
                            act.wait_ge(S("ssm_stored"), 16 * NB)
                        take_x(1, f - 3, bk[4])
            with act.Fori(0, NB - 1) as i:
                for page in range(PAGES):
                    copy_page(page, i)
                    if 2 <= page < 6:
                        softmax_exp(i, page - 2)
            for c in range(4):
                softmax_exp(NB - 1, c)
            act.wait_ge(S("od_ready"), 1)
            A(odt[:, 0, :].rearrange("p (h t) -> p h t", h=H), mix[:, 0:H, TP:T], ACT.Square).then_inc(S("od_sq"), 1)
            split_high(act, I_OUT)
            split_high(act, I_OUT + 1)
            act.wait_ge(S("od_ss"), 1)
            link(act, A(odt[:, 1, :], bk[4][:, 0:H * TS], ACT.Ln, scale=1.0 / VD, bias=cst_eps), step)
            A(odt[:, 1, :], odt[:, 1, :], ACT.Exp, scale=-0.5).then_inc(S("od_r"), 1)
            act.wait_ge(S("mix_ready"), 1)
            A(mh[:, 0:H, TP:T], mix[:, 0:H, TP:T], ACT.Copy).then_inc(S("m_high"), 1)

            for f in range(KT):
                act.wait_ge(S("op_sb"), f + 1)
                squares(1, f)
                if f % 2 == 1:
                    split_high(act, I_OUT + 2 + f // 2)
            for k in range(2):
                A(small[:, 56:57], cst_eps, ACT.Copy).then_inc(S("up_sb"), 1)
                act.wait_ge(S("up_sb"), k + 1)
            rstd(1)
            modulate(1, g2, 24, hh_ffn)

            def up_tile(ph, x, i):
                n = I_UP + 16 * ph + x // 2
                if x % 2 == 0:
                    act.wait_ge(S("up_ps"), i * 4 + (8 * ph + x // 2 + 1))
                else:
                    act.wait_ge(S("ring_used"), i * 4 + (n + 1))
                tile = u[:, bass.ds(i * 8 + x, 1), :].rearrange("p a t -> p (a t)")
                htile = uh[:, bass.ds(i * 8 + x, 1), :].rearrange("p a t -> p (a t)")
                for half in range(2):
                    ins = A(tile[:, half * HF:(half + 1) * HF], ffn_banks(ph, None, x % 2)[half][:, 0:HF], ACT.Relu)
                    if half == 0:
                        ins.then_inc(S("relu_half"), 1)
                ins.then_inc(S("up_sb"), 1)
                act.wait_ge(S("relu_half"), i * 8 + (UH * ph + x + 1))
                act.wait_ge(S("up_sb"), i * 8 + (UH * ph + x + 3))
                A(htile, tile, ACT.Square).then_inc(S("u_high"), 1)

            for ph in range(2):
                up, down = I_UP + 16 * ph, I_UP + 16 * ph + 8
                with act.Fori(0, 2) as i:
                    for k in range(4):
                        up_tile(ph, 2 * k, i)
                        up_tile(ph, 2 * k + 1, i)
                        split_high(act, up + k + 2, i, 4)
                if ph == 0:
                    with act.Fori(0, 2) as i:
                        for k in range(4):
                            split_high(act, down + k + 2, i, 4)
                else:
                    for k in range(6):
                        split_high(act, down + k + 2)
            for f in range(KT):
                act.wait_ge(S("down_sb"), KT + 4 + f + 1)
                squares(2, f)
            rstd(2)
            for m in range(5):
                n = P if m < MT else TS
                act.wait_ge(S("yt_ps"), 2 * m + 1)
                if m >= 2:
                    act.wait_ge(S(f"y_stored{m % 2}"), 16 * (m // 2))
                A(ytok[0:n, m % 2, 0:TP], bk[(2 * m) % 4][0:n, :], ACT.Copy).then_inc(S("yt_a"), 1)

        @block.vector
        def _(v):
            step = Tally(S("dve_step"))

            def L(ins):
                link(v, ins, step)

            def bc(ap, shape):
                return ap.to_broadcast(shape)

            L(v.memset(small[:, 63:64], EPS))
            v.memset(bk[4][:, :], 0.0).then_inc(S("ada_sb"), 1)
            v.memset(bk[5][:, :], 0.0).then_inc(S("ada_sb"), 1)
            v.memset(small[:, 62:63], 0.0).then_inc(S("eps_ready"), 1)
            v.wait_ge(S("setup_act"), SETUP_ACT["silu_exp"])
            L(v.tensor_scalar(ctmp[0:9, :], ctmp[0:9, :], 1.0, None, ALU.add))
            L(v.reciprocal(ctmp[0:9, :], ctmp[0:9, :]))
            v.tensor_tensor(ctmp[0:9, :], ctmp[0:9, :], crow[0:9, :], ALU.mult).then_inc(S("setup_dve"), 1)
            def take_x(k, m, bank):
                n = P if m < MT else TS
                v.wait_ge(S("xt_ps"), 10 * k + 2 * m + 2)
                v.tensor_copy(xT[:, 4:8, m * P:m * P + n], bank[:, :].rearrange("p (k c) -> p k c", k=4)[:, :, 0:n])\
                    .then_inc(S("xt_v"), 1)

            v.wait_ge(S("setup_ps"), SETUP_PS["ct_ps"])
            v.tensor_copy(cT[:, :, :], bk[5][:, 0:72].rearrange("p (k c) -> p k c", k=KT)).then_inc(S("setup_dve"), 1)
            def copy_ada(i):
                for q in range(2):
                    v.wait_ge(S("ring_used"), i * SLOTS + 2 * q + 2)
                    v.tensor_copy(adas[:, q, :], bk[4 + q][:, :]).then_inc(S("ada_sb"), 1)

            copy_ada(0)
            v.wait_ge(S("params_loaded"), 16 * N_PAR)
            v.wait_ge(S("setup_ps"), SETUP_PS["cols_ps"])
            L(v.tensor_copy(cols[:, :], bk[6][:, 0:NROW]))
            L(v.tensor_scalar(cols[:, C_SUB:C_SUB + 1], cols[:, C_SUB:C_SUB + 1], 0.8, None, ALU.mult))
            v.wait_ge(S("setup_act"), SETUP_ACT["alog_exp"])
            L(v.tensor_scalar(small[0:SH, 16:17], small[0:SH, 16:17], -1.0, None, ALU.mult))
            v.tensor_tensor(small[0:HD, 12:14], small[0:HD, 0:2], small[0:HD, 2:4], ALU.mult)\
                .then_inc(S("setup_dve"), 1)

            v.wait_ge(S("setup_act"), SETUP_ACT["lam_exp"])
            L(v.tensor_copy(small[:, 20:24], bk[6][:, 4:8]))
            L(v.tensor_tensor(small[:, 17:18], small[:, 19:20], small[:, 18:19], ALU.subtract))
            v.tensor_scalar(small[:, 17:18], small[:, 17:18], -0.2, None, ALU.add).then_inc(S("setup_dve"), 1)
            v.wait_ge(S("setup_dve"), SETUP_DVE["lam_ready"])
            v.wait_ge(S("setup_ps"), SETUP_PS["tables_ps"])
            L(v.tensor_copy(brow[0:H, 0, :], bk[6][0:H, 0:TAB]))
            v.tensor_copy(brow[0:H, 1, :], bk[7][0:H, 0:TAB]).then_inc(S("setup_dve"), 1)
            v.wait_ge(S("setup_ps"), SETUP_PS["cs_ps"])
            v.wait_ge(S("xp_zero"), 1)
            pre = xp[:, :, 3 + TP:XPW].rearrange("p c (b w) -> p c b w", w=DT + 3)[:, :, :, 0:3]
            for c in range(8):
                ins = v.tensor_copy(pre[:, c], bk[6][:, c * 24:(c + 1) * 24].rearrange("p (b w) -> p b w", b=NB))
                if c < 7:
                    L(ins)
            ins.then_inc(S("setup_dve"), 1)
            v.wait_ge(S("setup_dve"), SETUP_DVE["prefix_ready"])

            for m in range(5):
                take_x(0, m, (bk[1], bk[7])[m % 2])
            v.wait_ge(S("xt_a"), 5)
            v.memset(small[:, 61:62], 0.0).then_inc(S("x_free"), 1)
            copy_ada(1)

            mod_step = Tally(S("mod_step"))

            def modulate(k, g, sh, hh):
                v.wait_ge(S("rstd"), k + 1)
                for j in range(KT + 2):
                    if j < KT:
                        v.tensor_tensor(hT[:, j, :], xT[:, j, :], rs[:, :], ALU.mult).then_inc(S("xn"), 1)
                        hs = hT[:, j, TP:T].rearrange("p (b t) -> p b t", b=NB)
                        v.wait_ge(S("xn"), KT * k + j + 1)
                        mod_step.up(v.tensor_tensor(hs, hs, bc(g[:, j, 1:9].unsqueeze(2), [P, NB, DT]), ALU.mult))
                        v.wait_ge(mod_step.sem, KT * k + j + 1)
                        v.tensor_tensor(hs, hs, bc(mod[:, sh + j, 1:9].unsqueeze(2), [P, NB, DT]), ALU.add)\
                            .then_inc(S("h_sample"), 1)
                    if k == 0 and j == 2:
                        split_low(v, I_IN)
                    if j >= 2:
                        f = j - 2
                        v.wait_ge(S("h_high"), KT * k + f + 1)
                        v.tensor_tensor(hl[:, f, :], hT[:, f, :], hh[:, f, :], ALU.subtract).then_inc(S("h_low"), 1)

            def take_mod(bank, t0, nt):
                L(v.tensor_tensor(mod[:, t0:t0 + nt, :], bank[:, 0:nt * 9].rearrange("p (t c) -> p t c", c=9),
                                  bc(cols[:, C_BADA + t0:C_BADA + t0 + nt].unsqueeze(2), [P, nt, 9]), ALU.add))

            def gain(g, t0, c0):
                L(v.tensor_scalar(g[:, :, :], mod[:, t0:t0 + KT, :], 1.0, None, ALU.add))
                return v.tensor_tensor(g[:, :, :], g[:, :, :], bc(cols[:, c0:c0 + KT].unsqueeze(2), [P, KT, 9]),
                                       ALU.mult)

            v.wait_ge(S("mod_ps"), N_ADA1 // SLOTS)
            take_mod(bk[3], 0, 16)
            gain(g1, 8, C_GMIX).then_inc(S("mod1"), 1)
            v.wait_ge(S("mod1"), 1)
            modulate(0, g1, 0, hh_in)
            split_low(v, I_IN + 1)
            v.wait_ge(S("wdt_high"), 1)
            v.tensor_tensor(wdtl, wdt, wdth, ALU.subtract).then_inc(S("wdt_low"), 1)
            L(v.scalar_tensor_tensor(sel, picks[:, 1, :], small[:, 17:18], picks[:, 0, :], ALU.mult, ALU.add))

            def conv_taps(c):
                step.up(v.tensor_copy(gc[:, c, 0:3], xp[:, c, TP:3 + TP]))
                v.tensor_copy(gc[:, c, 3:27].rearrange("p (b w) -> p b w", b=NB),
                              xp[:, c, 3 + TP:XPW].rearrange("p (b w) -> p b w", w=DT + 3)[:, :, DT:DT + 3])\
                    .then_inc(S("ends_ready"), 1)
                v.wait_ge(S("tap0"), 2 * c + 2)
                cp, cs = cv[:, c % 2, 0:TP], cv[:, c % 2, TP:T].rearrange("p (b t) -> p b t", b=NB)
                for s in range(1, 4):
                    pp, ss = seg(xp[:, c, :], s)
                    w = cols[:, C_CW + 8 * s + c:C_CW + 8 * s + c + 1]
                    step.up(v.scalar_tensor_tensor(cp, pp, w, cp, ALU.mult, ALU.add))
                    ins = v.scalar_tensor_tensor(cs, ss, w, cs, ALU.mult, ALU.add)
                    if s < 3:
                        L(ins)
                ins.then_inc(S("taps"), 1)

            def conv_out(c):
                v.wait_ge(S("taps"), c + 1)
                v.wait_ge(S("ends_ready"), c + 1)
                v.wait_ge(S("conv_gate"), c + 1)
                v.tensor_tensor(xp[:, c, 0:T], cv[:, c % 2, :], ce[:, c % 2, :], ALU.mult).then_inc(S("xa_ready"), 1)

            dt, cs, dw = (rows[0:SH, r, :] for r in range(3))
            raw = dA = rs[0:SH, :]

            v.wait_ge(S("qbd_zero"), 1)
            for n, (kind, t) in enumerate(tiles):
                if 2 <= n <= 9:
                    conv_out(n - 2)
                if 1 <= n <= 8:
                    v.wait_ge(S("ip_dve"), n)
                    v.wait_ge(S("ip_act"), n)
                    conv_taps(n - 1)
                if n == 10:
                    v.wait_ge(S("ip_dve"), 9)
                    v.wait_ge(S("ip_act"), 9)
                    L(v.tensor_scalar(dt, raw, -1.0, None, ALU.mult))
                    v.tensor_tensor(dt, dt, raw, ALU.max).then_inc(S("dt_abs"), 1)
                if n == 11:
                    v.wait_ge(S("dt_ln"), 1)
                    L(v.scalar_tensor_tensor(dt, raw, 0.0, dt, ALU.max, ALU.add))
                    L(v.tensor_scalar(dA, dt, small[0:SH, 16:17], None, ALU.mult))
                    L(v.tensor_tensor_scan(cs, dw, dA, 0.0, ALU.mult, ALU.add))
                    csp, css = cs[:, 0:TP].rearrange("p (c t) -> p c t", c=MT), cs[:, TP:T].rearrange("p (c t) -> p c t", c=NB)
                    dwp, dws = dw[:, 0:TP].rearrange("p (c t) -> p c t", c=MT), dw[:, TP:T].rearrange("p (c t) -> p c t", c=NB)
                    L(v.tensor_tensor(dwp, bc(csp[:, :, P - 1:P], [SH, MT, P]), csp, ALU.subtract))
                    L(v.tensor_tensor(dws, bc(css[:, :, DT - 1:DT], [SH, NB, DT]), css, ALU.subtract))
                    L(v.tensor_copy(small[0:SH, 24:28].unsqueeze(2), csp[:, :, P - 1:P]))
                    v.tensor_copy(small[0:SH, 28:36].unsqueeze(2), css[:, :, DT - 1:DT]).then_inc(S("dt_gap"), 1)
                if n == 12:
                    v.wait_ge(S("dt_w"), 2)
                    v.tensor_tensor(dw, dw, dt, ALU.mult).then_inc(S("rows_ready"), 1)
                if 13 <= n <= 16:
                    v.wait_ge(S("z_gate"), n - 12)
                    v.tensor_tensor(zT[:, n - 13, :], zT[:, n - 13, :], mix[:, n - 9, :], ALU.mult)\
                        .then_inc(S("z_ready"), 1)
                if kind == "v":
                    if tile_sign[n][0] == "ring_used" and tile_sign[n][1] + 1 < I_IN + n_in:
                        split_low(v, tile_sign[n][1] + 1)
                    continue
                bs = bk[2 * (n % 4) + 1]
                sign, count = tile_sign[n]
                v.wait_ge(S(sign), count)
                sv = bs[:, TP - HF:HF].rearrange("p (b t) -> p b t", b=NB)
                if kind == "q":
                    step.up(v.tensor_scalar(qT[:, t, HF:TP], bs[:, 0:TP - HF], HD ** -0.5, None, ALU.mult))
                    L(v.tensor_scalar(qbd[0:64, :, t, 0, :], sv[0:64], HD ** -0.5, None, ALU.mult))
                    ins = v.tensor_scalar(qbd[64:128, :, t, 1, :], sv[64:128], HD ** -0.5, None, ALU.mult)
                elif kind == "k":
                    ins = v.tensor_copy(kT[:, t, HF:T], bs[:, 0:HF])
                elif kind == "d":
                    ins = v.tensor_scalar(rs[0:SH, HF:T], bs[0:SH, 0:HF], small[0:SH, 4:5], None, ALU.add)
                elif kind == "z":
                    ins = v.tensor_copy(zT[:, t, HF:T], bs[:, 0:HF])
                else:
                    step.up(v.tensor_copy(xp[:, t, 3 + HF:3 + TP], bs[:, 0:TP - HF]))
                    ins = v.tensor_copy(seg(xp[:, t, :], 3)[1], sv)
                ins.then_inc(S("ip_dve"), 1)
                if sign == "ring_used" and count + 1 < I_IN + n_in:
                    split_low(v, count + 1)
            v.wait_ge(S("ip_dve"), by_dve[-1])
            v.wait_ge(S("ip_act"), len(tiles))

            v.wait_ge(S("ssd_ps"), SSD_PS["tok_ps"])
            L(v.tensor_copy(tok[:, 0:MT, :, :], bk[6][:, 0:MT * 24].rearrange("p (m r h) -> p m r h", m=MT, r=3)))
            L(v.tensor_copy(tok[0:TS, MT, :, :], bk[6][0:TS, MT * 24:5 * 24].rearrange("p (r h) -> p r h", r=3)))
            v.wait_ge(S("ssd_ps"), SSD_PS["dec_ps"])
            v.tensor_copy(dec[:, :, :], bk[7][:, 0:96].rearrange("p (h c) -> p h c", h=SH)).then_inc(S("dec_sb"), 1)
            v.wait_ge(S("dec_sb"), 1)
            v.wait_ge(S("z_ready"), 4)
            v.wait_ge(S("conv_ps"), 1)
            v.wait_ge(S("tables_stored"), 16)
            L(v.tensor_copy(sout[0:27, 0:512], bk[0][0:27, :]))
            v.tensor_copy(sout[0:27, 512:1024], bk[1][0:27, :]).then_inc(S("conv_rows"), 1)

            for m in range(5):
                n = P if m < MT else TS
                v.wait_ge(S("kout_ps"), m + 1)
                v.tensor_copy(kouts[m][0:n, :], bk[m % 2][0:n, :]).then_inc(S("kout_ready"), 1)

            v.wait_ge(S("ring_used"), I_ADA2 + N_EARLY)
            for k in range(N_EARLY // 2):
                v.tensor_copy(adas2[:, k, :], bk[4 + k][:, :]).then_inc(S("ada_sb"), 1)

            v.wait_ge(S("bias_loaded"), 16 * (1 + 2 * H))
            v.tensor_copy(wb, wrev[:, :, ::-1]).then_inc(S("kout_ready"), 1)
            L(v.tensor_copy(nearb[:, 0:DT], nearr[:, 0:DT][:, ::-1]))
            L(v.tensor_copy(nearb[:, DT:NBIAS], nearr[:, DT:NBIAS][:, ::-1]))
            L(v.tensor_tensor(newb.rearrange("p b (c k) -> p (b c) k", c=NB), newb.rearrange("p b (c k) -> p (b c) k", c=NB),
                              bc(nearb[:, 0:DT].unsqueeze(1), [P, NB * NB, DT]), ALU.add))

            NU = 16

            def att_max(x):
                h, qb = x // MT, x % MT
                nk = (qb + 1) * P
                v.wait_ge(S("att_s"), x + 1)
                for j in range(2):
                    s = bk[2 + 2 * (x % 2) + j]
                    m_ = small[:, 36 + 2 * (x % 2) + j:37 + 2 * (x % 2) + j]
                    v.tensor_reduce(m_, s[:, 0:nk], AX, ALU.max, negate=True).then_inc(S("att_m"), 1)

            def att_combine(x):
                nk = (x % MT + 1) * P
                v.wait_ge(S("att_exp"), 2 * x + 2)
                r = small[:, 44 + 2 * (x % 2):46 + 2 * (x % 2)]
                L(v.reciprocal(r, small[:, 40 + 2 * (x % 2):42 + 2 * (x % 2)]))
                L(v.tensor_tensor(r[:, 1:2], r[:, 1:2], small[:, 17:18], ALU.mult))
                p0, p1 = pj[:, x % 2, 0, 0:nk], pj[:, x % 2, 1, 0:nk]
                L(v.tensor_scalar(p0, p0, r[:, 0:1], None, ALU.mult))
                v.scalar_tensor_tensor(p0, p1, r[:, 1:2], p0, ALU.mult, ALU.add).then_inc(S("att_p"), 1)

            def att_out(h):
                v.wait_ge(S("att_v"), MT * (h + 1))
                v.tensor_copy(mix[:, h, 0:TP], bk[0][:, :]).then_inc(S("att_o"), 1)

            for x in range(NU + 3):
                if x >= 6 and (x - 6) % 4 == 0:
                    att_out((x - 6) // 4)
                if x < NU:
                    att_max(x)
                if 1 <= x <= NU:
                    att_combine(x - 1)
                if x >= 2 and x % 2 == 0 and x + N_EARLY <= N_ADA2:
                    v.wait_ge(S("ring_used"), I_ADA2 + N_EARLY + x)
                    if (N_EARLY + x) // 2 - 1 == 5:
                        v.wait_ge(S("kout_stored0"), 16 * 3)
                        v.wait_ge(S("kout_stored1"), 16 * 2)
                    v.tensor_copy(adas2[:, (N_EARLY + x) // 2 - 1, :], bk[1][:, :]).then_inc(S("ada_sb"), 1)
            v.wait_ge(S("mod_ps"), N_ADA1 // SLOTS + 1)
            take_mod(bk[1], 16, 32)
            gain(g2, 32, C_GFFN).then_inc(S("mod2"), 1)
            v.wait_ge(S("mod2"), 1)

            v.wait_ge(S("xa_ready"), 8)
            for m in range(5):
                n = P if m < MT else TS
                v.wait_ge(S("xtk_ps"), m + 1)
                src = bk[m % 2][0:n, :].rearrange("p (h q) -> p h q", h=SH)
                L(v.tensor_tensor(xdt[0:n, m, :].rearrange("p (h q) -> p h q", h=SH), src,
                                  bc(tok[0:n, m, 0, :].unsqueeze(2), [n, SH, SP_]), ALU.mult))
                dst = xw[0:n, m, :] if m < MT else xws[:, :]
                v.tensor_tensor(dst.rearrange("p (h q) -> p h q", h=SH), src,
                                bc(tok[0:n, m, 2, :].unsqueeze(2), [n, SH, SP_]), ALU.mult).then_inc(S("xtk_v"), 1)
            v.wait_ge(S("att_o"), 4)
            for h in range(H):
                v.wait_ge(S("att_r"), h + 1)
                v.scalar_tensor_tensor(mix[:, h, 0:TP], mix[:, h, 0:TP], cols[:, C_SUB:C_SUB + 1], hT[:, 4 + h, 0:TP],
                                       ALU.mult, ALU.mult)\
                    .then_inc(S("att_n"), 1)
            v.wait_ge(S("att_n"), H)
            v.wait_ge(S("xtk_v"), 5)
            v.wait_ge(S("st_ps"), 1)
            L(v.tensor_copy(prev[:, 0, :], bk[0][:, :]))
            for c in range(1, MT):
                v.wait_ge(S("st_ps"), c + 1)
                L(v.tensor_tensor(prev[:, c, :].rearrange("p (h q) -> p h q", h=SH),
                                  prev[:, c - 1, :].rearrange("p (h q) -> p h q", h=SH),
                                  bc(dec[:, :, c:c + 1], [P, SH, SP_]), ALU.mult))
                ins = v.tensor_tensor(prev[:, c, :], prev[:, c, :], bk[c][:, :], ALU.add)
                if c < MT - 1:
                    L(ins)
            ins.then_inc(S("prev_done"), 1)

            v.wait_ge(S("prev_done"), 1)
            v.wait_ge(S("ssd_ps"), SSD_PS["final_ps"])
            v.tensor_copy(rs[:, 0:512], bk[3][:, :]).then_inc(S("final_ready"), 1)
            for h in range(SH + 2):
                if h < SH:
                    v.wait_ge(S("cs_bc"), h + 1)
                    if h >= 3:
                        v.wait_ge(S("y_ps"), h - 2)
                    for c in range(MT):
                        v.scalar_tensor_tensor(lg[:, h % 3, c * P:(c + 1) * P], bk[h % 2][:, c * P:(c + 1) * P],
                                               tok[:, c, 1, h:h + 1], cst[:, K_NM:K_NM + P], ALU.subtract, ALU.add)\
                            .then_inc(S("seg"), 1)
                    v.scalar_tensor_tensor(lg[0:TS, h % 3, TP:T], bk[2 + h % 2][0:TS, 0:TS], tok[0:TS, MT, 1, h:h + 1],
                                           cst[0:TS, K_NMS:K_NMS + TS], ALU.subtract, ALU.add).then_inc(S("seg"), 1)
                if 1 <= h <= SH:
                    k, g = h - 1, (h - 1) // 4
                    v.wait_ge(S("cb_sb"), 3)
                    v.wait_ge(S("lexp"), k + 1)
                    step.up(v.tensor_tensor(lg[:, k % 3, 0:TP], lg[:, k % 3, 0:TP], cbT[:, g, 0:TP], ALU.mult))
                    step.up(v.tensor_tensor(lg[0:TS, k % 3, TP:T], lg[0:TS, k % 3, TP:T], cbT[0:TS, g, TP:T], ALU.mult))
                    v.tensor_tensor(ceb[:, k % 3, :], ceb[:, k % 3, :], xp[:, 6 + g, 0:T], ALU.mult)\
                        .then_inc(S("g_ready"), 1)
                if h >= 2 and h % 2 == 1:
                    t = (h - 2) // 2
                    v.wait_ge(S("y_ps"), 2 * t + 2)
                    skip = small[:, 20 + t:21 + t]
                    L(v.scalar_tensor_tensor(mix[:, 4 + t, 0:TP], xp[:, t, 0:TP], skip, bk[4 + t % 2][:, :],
                                             ALU.mult, ALU.add))
                    v.scalar_tensor_tensor(mix[:, 4 + t, TP:T], xp[:, t, TP:T], skip, bk[6 + t % 2][:, 0:TS],
                                           ALU.mult, ALU.add).then_inc(S("y_sb"), 1)
                    v.wait_ge(S("y_sb"), t + 1)
                    v.tensor_tensor(mix[:, 4 + t, :], mix[:, 4 + t, :], zT[:, t, :], ALU.mult)\
                        .then_inc(S("y_gated"), 1)
            v.wait_ge(S("y_gated"), 4)
            v.wait_ge(step.sem, step.n)
            for g in range(GR):
                ins = v.tensor_tensor(bblk[0:TS, g, :, :], bc(btk[0:TS, MT, g * NS:(g + 1) * NS].unsqueeze(1), [TS, NB, NS]),
                                      bc(cst[0:TS, K_BLK:K_BLK + NB].unsqueeze(2), [TS, NB, NS]), ALU.mult)
                if g == 0:
                    L(ins)
            ins.then_inc(S("bblk_ready"), 1)
            for r in range(2):
                half = slice(64 * r, 64 * r + 64)
                L(v.tensor_copy(hdec[half, :, :], dec[half, r:SH:2, MT:MT + NB]))
            for t in range(4):
                for q in range(2):
                    v.wait_ge(S("ssm_ps"), 2 * t + q + 1)
                    for j in range(4):
                        b = 4 * q + j
                        ins = v.scalar_tensor_tensor(h0[:, b, t, :], h0[:, b, t, :], hdec[:, t, b:b + 1],
                                                     bk[4 + (2 * t + q) % 4][:, j * NS:(j + 1) * NS], ALU.mult, ALU.add)
                        if j < 3:
                            step.up(ins)
                    ins.then_inc(S("ssm_sb"), 1)
            v.wait_ge(step.sem, step.n)
            v.wait_ge(S("ssm_sb"), 8)
            v.memset(small[:, 61:62], 0.0).then_inc(S("ssm_ready"), 1)
            for g in range(GR):
                v.wait_ge(S("ssd_r"), g + 1)
                for t in (2 * g, 2 * g + 1):
                    L(v.scalar_tensor_tensor(mix[:, 4 + t, :], mix[:, 4 + t, :], cols[:, C_SSD + t:C_SSD + t + 1],
                                             hT[:, 4 + g, :], ALU.mult, ALU.mult))

            L(v.memset(qcur, 0.0))
            L(v.memset(bk[5][:, :], 0.0))
            v.memset(small[:, 61:62], 0.0).then_inc(S("dec_start"), 1)
            chain = Tally(S("dec_step"))

            def take_scores(g, n):
                v.wait_ge(S("s_ps"), n + (g + 1))
                bank, dst = bk[2 + g % 2], sc[:, g * 512:(g + 1) * 512]
                if g < 7:
                    chain.up(v.tensor_reduce(small[:, 36 + g:37 + g], bank[:, :], AX, ALU.max))
                    v.tensor_copy(dst, bank[:, :]).then_inc(S("s_sb"), 1)
                else:
                    chain.up(v.tensor_tensor(dst[:, 384:512], bank[:, 384:512], nearb[:, DT:NBIAS], ALU.add))
                    v.tensor_copy(dst[:, 0:384], bank[:, 0:384]).then_inc(S("s_sb"), 1)
                    v.wait_ge(S("s_sb"), n + 8)
                    v.wait_ge(chain.sem, chain.n)
                    link(v, v.tensor_reduce(small[:, 43:44], dst, AX, ALU.max), chain)

            def take_new(b, n):
                v.wait_ge(S("new_ps"), n + 1)
                link(v, v.tensor_tensor(sc[:, NK:NK + TS], bk[7][:, 0:TS],
                                        newb[:, bass.ds(b, 1), :].rearrange("p a c -> p (a c)"), ALU.add), chain)
                v.tensor_reduce(small[:, 44:45], sc[:, NK:NK + TS], AX, ALU.max).then_inc(S("new_sb"), 1)

            def largest(b):
                v.wait_ge(S("new_sb"), b + 1)
                v.tensor_reduce(small[:, 46:47], small[:, 36:45], AX, ALU.max, negate=True).then_inc(S("max_ready"), 1)

            def copy_p(groups, g):
                v.wait_ge(S("pt_ps"), groups + (g + 1))
                bank = bk[4 + 2 * (g % 2)]
                if g < 8:
                    ins = v.tensor_copy(pT[:, g % 2, :], bank[:, :])
                else:
                    ins = v.tensor_copy(pT[0:TS, 0, 0:P], bank[0:TS, 0:P])
                ins.then_inc(S("pt_sb"), 1)

            def inverse(i):
                v.wait_ge(S("exp_done"), i * 4 + 4)
                link(v, v.tensor_reduce(small[:, 54:55], small[:, 50:54], AX, ALU.add), chain)
                link(v, v.reciprocal(small[:, 55:56], small[:, 54:55]), chain)

            def finish(i):
                v.wait_ge(S("o_ps"), i + 1)
                v.tensor_scalar(on, bk[5][:, 0:P], small[:, 55:56], None, ALU.mult).then_inc(S("on_ready"), 1)

            def take_out(i):
                v.wait_ge(S("od_ps"), i + 1)
                v.tensor_copy(mix[:, 0:H, bass.ds(TP + i * DT, DT)],
                              bk[7][:, P:P + NB * H].rearrange("p (h t) -> p h t", h=H)).then_inc(S("od_sb"), 1)

            for g in range(8):
                v.wait_ge(S("m_high"), g + 1)
                end = TP if g < H else T
                step.up(v.tensor_tensor(ml[:, g, 0:end], mix[:, g, 0:end], mh[:, g, 0:end], ALU.subtract))
                if g >= 1:
                    take_scores(g - 1, 0)
                if g == 4:
                    take_new(0, 0)
                if g >= 3:
                    if g == 3:
                        v.wait_ge(S("ssm_stored"), 16 * NB)
                    take_x(1, g - 3, bk[6])
            take_scores(7, 0)
            largest(0)
            v.memset(small[:, 61:62], 0.0).then_inc(S("od_sb"), 1)
            v.wait_ge(S("od_sb"), 1)
            base = chain.n
            per = 9 + 1 + 2
            with v.Fori(0, NB - 1) as i:
                chain.n = i * per + base
                for what in STEPS:
                    kind, g = what[0], int(what[1:])
                    if what == "S0":
                        inverse(i)
                    if kind == "S":
                        take_scores(g, i * 8 + 8)
                    if kind == "P":
                        copy_p(i * 9, g)
                    if what == "S3":
                        take_new(i + 1, i + 1)
                    if what == "V7":
                        finish(i)
                largest(i + 1)
                take_out(i)
            chain.n = base + per * (NB - 1)
            inverse(NB - 1)
            for g in range(9):
                copy_p(9 * (NB - 1), g)
            finish(NB - 1)
            v.wait_ge(S("od_ps"), NB)
            v.tensor_copy(mix[:, 0:H, T - DT:T], bk[7][:, P:P + NB * H].rearrange("p (h t) -> p h t", h=H))\
                .then_inc(S("od_sb"), 1)
            v.wait_ge(S("od_sb"), NB + 1)
            v.memset(small[:, 61:62], 0.0).then_inc(S("od_ready"), 1)
            split_low(v, I_OUT)
            v.wait_ge(S("ssm_stored"), 16 * NB)
            v.wait_ge(S("od_r"), 1)
            r4 = odt[:, 1, :].rearrange("p (h t) -> p h t", h=H)
            v.scalar_tensor_tensor(mix[:, 0:H, TP:T], mix[:, 0:H, TP:T], cols[:, C_SUB:C_SUB + 1], r4,
                                   ALU.mult, ALU.mult)\
                .then_inc(S("mix_ready"), 1)
            split_low(v, I_OUT + 1)
            v.wait_ge(S("m_high"), KT + 1)
            v.tensor_tensor(ml[:, 0:H, TP:T], mix[:, 0:H, TP:T], mh[:, 0:H, TP:T], ALU.subtract)\
                .then_inc(S("mix_ready"), 1)
            v.wait_ge(S("xt_a"), 10)
            v.wait_ge(S("xt_v"), 10)

            for x in range(KT):
                if x % 2 == 0:
                    v.wait_ge(S("op_ps"), x // 2 + 1)
                else:
                    v.wait_ge(S("ring_used"), I_OUT + x // 2 + 1)
                bp, bs = bk[2 * (x % 2)], bk[2 * (x % 2) + 1]
                ga = mod[:, 16 + x, :]
                xs = xT[:, x, TP:T].rearrange("p (b t) -> p b t", b=NB)
                step.up(v.scalar_tensor_tensor(xT[:, x, 0:HF], bp[:, 0:HF], ga[:, 0:1], xT[:, x, 0:HF], ALU.mult, ALU.add))
                step.up(v.scalar_tensor_tensor(xT[:, x, HF:TP], bs[:, 0:TP - HF], ga[:, 0:1], xT[:, x, HF:TP],
                                               ALU.mult, ALU.add))
                g8 = rs[:, 0:TS].rearrange("p (b t) -> p b t", b=NB)
                L(v.tensor_tensor(g8, bs[:, TP - HF:HF].rearrange("p (b t) -> p b t", b=NB),
                                  bc(ga[:, 1:9].unsqueeze(2), [P, NB, DT]), ALU.mult))
                v.tensor_tensor(xs, xs, g8, ALU.add).then_inc(S("op_sb"), 1)
                v.wait_ge(S("op_sb"), x + 1)
                if x % 2 == 1:
                    split_low(v, I_OUT + 2 + x // 2)
            modulate(1, g2, 24, hh_ffn)
            for k in range(4):
                v.memset(small[:, 61:62], 0.0).then_inc(S("down_sb"), 1)
                v.wait_ge(S("down_sb"), k + 1)
            square = Tally(S("square"))
            down_step = Tally(S("down_step"))

            def up_low(ph, x, i):
                v.wait_ge(S("u_high"), i * 8 + (UH * ph + x + 1))
                tile = u[:, bass.ds(i * 8 + x, 1), :].rearrange("p a t -> p (a t)")
                htile = uh[:, bass.ds(i * 8 + x, 1), :].rearrange("p a t -> p (a t)")
                ltile = ul[:, bass.ds(i * 8 + x, 1), :].rearrange("p a t -> p (a t)")
                square.n = i * 8 + (UH * ph + x)
                link(v, v.tensor_tensor(tile, tile, tile, ALU.mult), square)
                v.tensor_tensor(ltile, tile, htile, ALU.subtract).then_inc(S("u_ready"), 1)

            def down_tiles(ph, c, i):
                down = I_UP + 16 * ph + 8
                for t in range(2):
                    if t == 0:
                        v.wait_ge(S("down_ps"), i * 2 + (4 * ph + c + 1))
                    else:
                        v.wait_ge(S("ring_used"), i * 4 + (down + 2 * c + 2))
                    down_step.n = i * 12 + (24 * ph + 6 * c + 3 * t)
                    bp, bs = ffn_banks(ph, c, t)
                    tile = xT[:, bass.ds(i * 4 + (2 * c + t), 1), :].rearrange("p a t -> p (a t)")
                    ga = mod[:, bass.ds(i * 4 + (40 + 2 * c + t), 1), :].rearrange("p a c -> p (a c)")
                    down_step.up(v.scalar_tensor_tensor(tile[:, 0:HF], bp[:, 0:HF], ga[:, 0:1], tile[:, 0:HF],
                                                        ALU.mult, ALU.add))
                    down_step.up(v.scalar_tensor_tensor(tile[:, HF:TP], bs[:, 0:TP - HF], ga[:, 0:1], tile[:, HF:TP],
                                                        ALU.mult, ALU.add))
                    g8 = rs[:, t * TS:(t + 1) * TS].rearrange("p (b t) -> p b t", b=NB)
                    link(v, v.tensor_tensor(g8, bs[:, TP - HF:HF].rearrange("p (b t) -> p b t", b=NB),
                                            bc(ga[:, 1:9].unsqueeze(2), [P, NB, DT]), ALU.mult), down_step)
                    xs = tile[:, TP:T].rearrange("p (b t) -> p b t", b=NB)
                    v.tensor_tensor(xs, xs, g8, ALU.add).then_inc(S("down_sb"), 1)

            for ph in range(2):
                up, down = I_UP + 16 * ph, I_UP + 16 * ph + 8
                with v.Fori(0, 2) as i:
                    for k in range(4):
                        up_low(ph, 2 * k, i)
                        up_low(ph, 2 * k + 1, i)
                        split_low(v, up + k + 2, i, 4)
                if ph == 0:
                    with v.Fori(0, 2) as i:
                        for k in range(4):
                            split_low(v, down + k + 2, i, 4)
                            if k % 2 == 1:
                                down_tiles(ph, k // 2, i)
                    v.wait_ge(S("down_sb"), KT + 4)
                else:
                    for i in range(2):
                        for k in range(4):
                            if 4 * i + k < 6:
                                split_low(v, down + 4 * i + k + 2)
                            if k % 2 == 1:
                                down_tiles(ph, k // 2, i)
            v.wait_ge(S("down_sb"), 2 * KT + 4)
            v.wait_ge(S("rstd"), 3)
            for f in range(KT):
                v.scalar_tensor_tensor(hT[:, f, :], xT[:, f, :], cols[:, C_GFIN + f:C_GFIN + f + 1], rs[:, :],
                                       ALU.mult, ALU.mult).then_inc(S("xn"), 1)
            for m in range(5):
                n = P if m < MT else TS
                v.wait_ge(S("yt_ps"), 2 * m + 2)
                if m >= 2:
                    v.wait_ge(S(f"y_stored{m % 2}"), 16 * (m // 2))
                v.tensor_copy(ytok[0:n, m % 2, TP:D], bk[(2 * m + 1) % 4][0:n, :]).then_inc(S("yt_v"), 1)


N_PAR = 22
N_POOL = 320


def shape_constants():
    import numpy as np

    c = np.zeros((P, K_N), np.float32)
    c[:, K_ID:K_ID + P] = np.eye(P)
    c[:, K_ONE:K_ONE + P] = 1
    s, l = np.meshgrid(np.arange(P), np.arange(P), indexing="ij")
    c[:, K_NM:K_NM + P] = np.where(s <= l, 0, BIG)
    s, l = s[:TS, :TS], l[:TS, :TS]
    c[:TS, K_NMS:K_NMS + TS] = np.where((s <= l) & (s // DT == l // DT), 0, BIG)
    c[:TS, K_BLK:K_BLK + NB] = np.arange(TS)[:, None] // DT == np.arange(NB)
    q = np.arange(NB * H)
    row = 32 * (q // DT) + q % DT
    for r in range(4):
        c[32 * r + np.arange(9), K_SUM + np.arange(9)] = 1
    picks = np.zeros((P, 2, NB * H), np.float32)
    picks[row, 0, q] = 1
    picks[row + DT, 1, q] = 1
    r, b, k = np.meshgrid(np.arange(P), np.arange(NB), np.arange(TS), indexing="ij")
    seen = (k // DT == b) & (k % DT <= r % DT) | (r % 32 >= 2 * DT)
    new = np.where(seen, 0, BIG).astype(np.float32).reshape(P, NB * TS)
    d = np.arange(TAB) - OFF
    n = np.maximum(d, 0)
    lt = np.log(np.maximum(n, 1).astype(np.float32) / np.float32(16)) / np.float32(np.log(8.0)) * np.float32(16)
    bucket = np.where(n < 16, n, np.minimum(16 + lt.astype(np.int32), 31))
    hot = np.zeros((33, 2, TAB), np.float32)
    hot[:32, 0] = (np.arange(32)[:, None] == bucket).astype(np.float32)
    hot[31, 0] -= 1
    hot[:, 0, d < 0] = 0
    hot[32, 0, d < 0] = BIG
    far = 2 * P - 1 + OFF
    hot[:, 1, 0:far + 1] = hot[:, 0, far::-1]
    starts = np.ones((SH, T), np.float32)
    starts[:, 0:TP:P] = 0
    starts[:, TP:T:DT] = 0
    return c, hot, starts, new, picks


_OUTS = [("y_p", (TP, D)), ("y_s", (TS, D)), ("k_p", (TP, 512)), ("v_p", (TP, 512)), ("conv_p", (3, CONV)),
         ("ssm_p", (512, NS)), ("k_s", (TS, 512)), ("v_s", (TS, 512)), ("conv_s", (NB * 3, CONV)),
         ("ssm_s", (NB * 512, NS))]
_SHAPES = [(1, TP, D), (NB, DT, D), (1, 1, TP, H, 2, HD), (1, 1, TP, H, VD), (1, 1, 3, CONV), (1, 1, SH, SP_, NS),
           (1, NB, DT, H, 2, HD), (1, NB, DT, H, VD), (1, NB, 3, CONV), (1, NB, SH, SP_, NS)]


def kernel(**inputs):
    import concourse.bacc as _bacc
    import numpy as _np
    from concourse.bass_utils import run_bass_kernel_spmd as _run

    nc = _bacc.Bacc("TRN2", target_bir_lowering=False, num_devices=1)
    arrays = {k: _np.ascontiguousarray(v) for k, v in inputs.items()}
    arrays["cache_k"] = arrays["cache_k"].reshape(N_POOL, PAGE, 512)
    arrays["cache_v"] = arrays["cache_v"].reshape(N_POOL, PAGE, 512)
    arrays["shape_consts"], arrays["shape_hot"], arrays["shape_starts"], arrays["shape_new"], arrays["shape_picks"] = shape_constants()
    arrays = {f"in_{k}": v for k, v in arrays.items()}
    a = {k[3:]: nc.dram_tensor(k, v.shape, mybir.dt.from_np(v.dtype), kind="ExternalInput").ap()
         for k, v in arrays.items()}
    o = {k: nc.dram_tensor(f"out_{k}", s, F32, kind="ExternalOutput").ap() for k, s in _OUTS}
    scratch = nc.dram_tensor("bias_tables", (2, H, TAB), F32, kind="Internal").ap()
    program(nc, a, o, scratch)
    r = _run(nc, [arrays], core_ids=[0])
    return tuple(r.results[0][f"out_{k}"].reshape(s) for (k, _), s in zip(_OUTS, _SHAPES))
```
